# Optimizing a Trainium2 kernel written in Bass

```python
import jax, jax.numpy as jnp
from jax import lax
import numpy as np

D_MODEL = 1024
BATCH = 1
SEQ = 512
DEPTH = 2
DEC_BATCH = 8
DEC_SEQ = 4
PAST_LEN = 2048
PAGE_SIZE = 128

N_EVEN = (DEPTH + 1) // 2
N_ODD = DEPTH // 2
EPS = 1e-6
D_FF = ((8 * D_MODEL // 3 + 255) // 256) * 256

POOL_WIDTH = D_MODEL // 4
POOL_WINDOWS = (2, 4, 8, 16)
POOL_GROUPS = len(POOL_WINDOWS)
POOL_GDIM = POOL_WIDTH // POOL_GROUPS
POOL_BUF = max(POOL_WINDOWS) - 1
ML_HEADS = 4
ML_WIDTH = D_MODEL - POOL_WIDTH
ML_DH = ML_WIDTH // ML_HEADS
ML_CHUNK = 64
FORGET_BIAS = 3.0
EVEN_IN = POOL_WIDTH + 4 * ML_WIDTH + 2 * ML_HEADS

NSA_HEADS = 12
HEAD_DIM = 64
NSA_WIDTH = NSA_HEADS * HEAD_DIM
KV_HEADS = 2
GQ = NSA_HEADS // KV_HEADS
KV_W = KV_HEADS * HEAD_DIM
CMP_STRIDE = 16
CMP_BLOCK = 2 * CMP_STRIDE
CMP_LEAD = CMP_BLOCK // CMP_STRIDE - 1
SEL_BLOCK = 64
RATIO = SEL_BLOCK // CMP_STRIDE
SEL_TOPN = 16
WINDOW = 512
Q_BLOCK = 64
CONV_CH = D_MODEL - NSA_WIDTH
CONV_K = 3
ODD_IN = NSA_WIDTH + 6 * KV_W + 3 * NSA_HEADS + 3 * CONV_CH

kernel_name = 'hybrid_pool_mlstm_nsa_conv_step'

def _rmsnorm(x, g):
    xf = x.astype(jnp.float32)
    y = xf * lax.rsqrt(jnp.mean(xf * xf, axis=-1, keepdims=True) + EPS)
    return (y * g.astype(jnp.float32)).astype(x.dtype)

def _swiglu(x, w_in, w_out):
    a, b = jnp.split(x @ w_in, 2, axis=-1)
    return (jax.nn.silu(a) * b) @ w_out

def _masked_softmax(s, mask):
    s = jnp.where(mask, s, -jnp.inf)
    m = jnp.max(s, axis=-1, keepdims=True)
    m = jnp.where(jnp.isfinite(m), m, 0.0)
    e = jnp.exp(s - m)
    return e / jnp.maximum(jnp.sum(e, axis=-1, keepdims=True), 1e-30)

def _alibi_slopes():
    sl = 2.0 ** (-8.0 * np.arange(1, NSA_HEADS + 1) / NSA_HEADS)
    return jnp.asarray(sl, jnp.float32).reshape(KV_HEADS, GQ)

def _pool_mix(u, prefix, pos0, w_pool, scale):
    B, T, _ = u.shape
    full = jnp.concatenate([prefix, u], axis=1)
    cs = jnp.cumsum(full.astype(jnp.float32), axis=1)
    cs = jnp.concatenate([jnp.zeros((B, 1, POOL_WIDTH), jnp.float32), cs], axis=1)
    pos = pos0 + jnp.arange(T)
    end = cs[:, POOL_BUF + 1:]
    means = []
    for g, w in enumerate(POOL_WINDOWS):
        lo, hi = g * POOL_GDIM, (g + 1) * POOL_GDIM
        win_sum = end[..., lo:hi] - cs[:, POOL_BUF + 1 - w:POOL_BUF + 1 - w + T, lo:hi]
        cnt = jnp.minimum(pos + 1, w).astype(jnp.float32)
        means.append(win_sum / cnt[None, :, None])
    mixed = (jnp.concatenate(means, axis=-1) - u.astype(jnp.float32)).astype(u.dtype)
    y = jnp.einsum('btgc,gcd->btgd', mixed.reshape(B, T, POOL_GROUPS, POOL_GDIM), w_pool)
    return y.reshape(B, T, POOL_WIDTH) * scale, full[:, -POOL_BUF:]

def _mlstm(q, k, v, ig, fg, c0, n0, m0):
    f32 = jnp.float32
    B, T, H, D = q.shape
    L = ML_CHUNK if T % ML_CHUNK == 0 else T
    nc = T // L

    def chunks(a):
        a = a.astype(f32).reshape((B, nc, L) + a.shape[2:])
        return jnp.swapaxes(jnp.moveaxis(a, 1, 0), 2, 3)

    xs = (chunks(q), chunks(k.astype(f32) * (D ** -0.5)), chunks(v), chunks(ig),
          chunks(jax.nn.log_sigmoid(fg.astype(f32))))
    causal = jnp.tril(jnp.ones((L, L), dtype=bool))

    def step(carry, inp):
        c, n, m = carry
        qc, kc, vc, ic, fc = inp
        b = jnp.cumsum(fc, axis=-1)
        dmat = jnp.where(causal, b[..., :, None] - b[..., None, :] + ic[..., None, :], -jnp.inf)
        inter = b + m[..., None]
        mt = jnp.maximum(jnp.max(dmat, axis=-1), inter)
        w = jnp.exp(dmat - mt[..., None])
        a = jnp.exp(inter - mt)
        s = jnp.einsum('bhtd,bhsd->bhts', qc, kc) * w
        num = jnp.einsum('bhts,bhse->bhte', s, vc) + a[..., None] * jnp.einsum('bhed,bhtd->bhte', c, qc)
        den = jnp.sum(s, axis=-1) + a * jnp.einsum('bhd,bhtd->bht', n, qc)
        h = num / jnp.maximum(jnp.abs(den), jnp.exp(-mt))[..., None]
        g_end = b[..., -1:] - b + ic
        m_new = jnp.maximum(b[..., -1] + m, jnp.max(g_end, axis=-1))
        wk = jnp.exp(g_end - m_new[..., None])
        decay = jnp.exp(b[..., -1] + m - m_new)
        c_new = decay[..., None, None] * c + jnp.einsum('bhs,bhse,bhsd->bhed', wk, vc, kc)
        n_new = decay[..., None] * n + jnp.einsum('bhs,bhsd->bhd', wk, kc)
        return (c_new, n_new, m_new), h

    (c, n, m), h = lax.scan(step, (c0.astype(f32), n0.astype(f32), m0.astype(f32)), xs)
    h = jnp.moveaxis(jnp.swapaxes(h, 2, 3), 0, 1).reshape(B, T, H, D)
    return h, c, n, m

def _even_mixer(h, pos0, pool_buf, c0, n0, m0, w_in, b_gate, w_pool, pool_scale, w_out):
    B, T, _ = h.shape
    z = h @ w_in
    s1 = POOL_WIDTH
    s2 = s1 + ML_WIDTH
    s3 = s2 + ML_WIDTH
    s4 = s3 + ML_WIDTH
    s5 = s4 + ML_WIDTH
    u, q, k, v, og, gt = jnp.split(z, [s1, s2, s3, s4, s5], axis=-1)
    y_pool, new_pool = _pool_mix(u, pool_buf, pos0, w_pool, pool_scale)
    gt = gt + b_gate
    hd = lambda a: a.reshape(B, T, ML_HEADS, ML_DH)
    hm, c, n, m = _mlstm(hd(q), hd(k), hd(v), gt[..., :ML_HEADS], gt[..., ML_HEADS:], c0, n0, m0)
    y_ml = jax.nn.sigmoid(og) * hm.reshape(B, T, ML_WIDTH).astype(og.dtype)
    y = jnp.concatenate([y_pool, y_ml], axis=-1) @ w_out
    return y, new_pool, c, n, m

def _compress(kv, pos_w, w, b):
    B, L = kv.shape[:2]
    nch = L // CMP_STRIDE
    ch = kv[:, :nch * CMP_STRIDE].reshape(B, nch, CMP_STRIDE, 2, KV_HEADS, HEAD_DIM)
    pre = (jnp.einsum('bnjkgd,kj->bnkgd', ch[:, :-1], pos_w[:, :CMP_STRIDE]) +
           jnp.einsum('bnjkgd,kj->bnkgd', ch[:, 1:], pos_w[:, CMP_STRIDE:]))
    return jnp.einsum('bnkgd,kde->bnkge', pre, w) + b[None, None, :, None, :]

def _sel_blocks(kv):
    B, L = kv.shape[:2]
    ns = -(-L // SEL_BLOCK)
    kv = jnp.pad(kv, ((0, 0), (0, ns * SEL_BLOCK - L), (0, 0), (0, 0), (0, 0)))
    kv = kv.reshape(B, ns, SEL_BLOCK, 2, KV_HEADS, HEAD_DIM)
    return jnp.transpose(kv, (0, 4, 1, 2, 3, 5))

def _nsa_query_block(q, gates, p0, kv_cmp, kv_sel, band, band_p0):
    f32 = jnp.float32
    B, Q = q.shape[:2]
    qg = q.reshape(B, Q, KV_HEADS, GQ, HEAD_DIM) * (HEAD_DIM ** -0.5)
    slopes = _alibi_slopes()[None, None, :, :, None]
    tpos = p0 + jnp.arange(Q)

    nc = kv_cmp.shape[1]
    cpos = CMP_STRIDE * jnp.arange(nc) + (CMP_BLOCK - 1)
    dist = tpos[:, None] - cpos[None, :]
    s = jnp.einsum('bqgid,bngd->bqgin', qg, kv_cmp[:, :, 0], preferred_element_type=f32)
    s = s - slopes * dist[None, :, None, None, :].astype(f32)
    p_cmp = _masked_softmax(s, (dist >= 0)[None, :, None, None, :])
    o_cmp = jnp.einsum('bqgin,bngd->bqgid', p_cmp, kv_cmp[:, :, 1])

    ns = kv_sel.shape[2]
    imp = jnp.sum(p_cmp, axis=3)
    pad_r = RATIO * (ns + 1) - nc - CMP_LEAD
    imp = jnp.pad(imp, ((0, 0), (0, 0), (0, 0), (CMP_LEAD, pad_r))).reshape(B, Q, KV_HEADS, ns + 1, RATIO)
    score = imp[..., :-1, :].sum(-1) + imp[..., 1:, :CMP_LEAD].sum(-1)
    blk = jnp.arange(ns)[None, :]
    cur = (tpos // SEL_BLOCK)[:, None]
    visible = blk <= cur
    forced = (blk == 0) | (blk == cur) | (blk == cur - 1)
    score = jnp.where(forced[None, :, None, :], jnp.inf,
                      jnp.where(visible[None, :, None, :], score, -jnp.inf))
    n_sel = min(SEL_TOPN, ns)
    _, idx = lax.top_k(score, n_sel)
    bi = jnp.arange(B)[:, None, None, None]
    gi = jnp.arange(KV_HEADS)[None, None, :, None]
    sel = kv_sel[bi, gi, idx]
    spos = idx[..., None] * SEL_BLOCK + jnp.arange(SEL_BLOCK)
    sdist = tpos[None, :, None, None, None] - spos
    s = jnp.einsum('bqgid,bqgnrd->bqginr', qg, sel[..., 0, :], preferred_element_type=f32)
    s = s - slopes[..., None] * sdist[:, :, :, None].astype(f32)
    s = s.reshape(B, Q, KV_HEADS, GQ, n_sel * SEL_BLOCK)
    smask = (sdist >= 0).reshape(B, Q, KV_HEADS, 1, n_sel * SEL_BLOCK)
    p = _masked_softmax(s, smask).reshape(B, Q, KV_HEADS, GQ, n_sel, SEL_BLOCK)
    o_sel = jnp.einsum('bqginr,bqgnrd->bqgid', p, sel[..., 1, :])

    wb = band.shape[1]
    bpos = band_p0 + jnp.arange(wb)
    wdist = tpos[:, None] - bpos[None, :]
    wmask = (wdist >= 0) & (wdist < WINDOW) & (bpos[None, :] >= 0)
    s = jnp.einsum('bqgid,bkgd->bqgik', qg, band[:, :, 0], preferred_element_type=f32)
    s = s - slopes * wdist[None, :, None, None, :].astype(f32)
    p = _masked_softmax(s, wmask[None, :, None, None, :])
    o_win = jnp.einsum('bqgik,bkgd->bqgid', p, band[:, :, 1])

    g = gates.reshape(B, Q, KV_HEADS, GQ, 3).astype(f32)
    o = g[..., 0:1] * o_cmp + g[..., 1:2] * o_sel + g[..., 2:3] * o_win
    return o.reshape(B, Q, NSA_WIDTH).astype(q.dtype)

def _odd_mixer(h, pos0, past_kv, win_buf, conv_buf, w_in, cmp_pos_w, cmp_w, cmp_b, conv_w, w_out):
    B, T, _ = h.shape
    z = h @ w_in
    o1 = NSA_WIDTH
    o2 = o1 + 6 * KV_W
    o3 = o2 + 3 * NSA_HEADS
    o4 = o3 + CONV_CH
    o5 = o4 + CONV_CH
    q, kv, gt, bg, cg, xin = jnp.split(z, [o1, o2, o3, o4, o5], axis=-1)
    q = q.reshape(B, T, NSA_HEADS, HEAD_DIM)
    kv = kv.reshape(B, T, 3, 2, KV_HEADS, HEAD_DIM)
    gates = jax.nn.sigmoid(gt.astype(jnp.float32)).reshape(B, T, NSA_HEADS, 3)
    kv_pg, kv_win = kv[:, :, :2], kv[:, :, 2]
    kv_all = kv_pg if past_kv is None else jnp.concatenate([past_kv, kv_pg], axis=1)
    kv_cmp = _compress(kv_all[:, :, 0], cmp_pos_w, cmp_w, cmp_b)
    kv_sel = _sel_blocks(kv_all[:, :, 1])
    if past_kv is None:
        win_src = jnp.concatenate([jnp.zeros((B, WINDOW - 1) + kv_win.shape[2:], kv_win.dtype), kv_win], axis=1)
        nqb = T // Q_BLOCK
        qb = jnp.moveaxis(q.reshape(B, nqb, Q_BLOCK, NSA_HEADS, HEAD_DIM), 1, 0)
        gb = jnp.moveaxis(gates.reshape(B, nqb, Q_BLOCK, NSA_HEADS, 3), 1, 0)

        def one_block(args):
            bi, qq, gg = args
            p0 = pos0 + bi * Q_BLOCK
            band = lax.dynamic_slice_in_dim(win_src, bi * Q_BLOCK, WINDOW - 1 + Q_BLOCK, axis=1)
            return _nsa_query_block(qq, gg, p0, kv_cmp, kv_sel, band, p0 - (WINDOW - 1))

        o = lax.map(one_block, (jnp.arange(nqb), qb, gb))
        o = jnp.moveaxis(o, 0, 1).reshape(B, T, NSA_WIDTH)
        new_win = kv_win[:, -min(WINDOW, T):]
    else:
        wlen = win_buf.shape[1]
        win_src = jnp.concatenate([win_buf, kv_win], axis=1)
        o = _nsa_query_block(q, gates, pos0, kv_cmp, kv_sel, win_src, pos0 - wlen)
        new_win = win_src[:, -wlen:]
    u = cg * xin
    full = jnp.concatenate([conv_buf, u], axis=1)
    conv = full[:, 0:T] * conv_w[0]
    for j in range(1, CONV_K):
        conv = conv + full[:, j:j + T] * conv_w[j]
    y = jnp.concatenate([o, bg * conv], axis=-1) @ w_out
    new_rows = kv_pg.reshape(B, T, 4, KV_HEADS, HEAD_DIM)
    return y, new_rows, new_win, full[:, -(CONV_K - 1):]

def _gather_past(pool, page_table):
    bd, npg = page_table.shape
    pages = pool[page_table]
    return pages.reshape(bd, npg * PAGE_SIZE, 2, 2, KV_HEADS, HEAD_DIM)

def _trunk(x, pos0, pool_buf, ml_c, ml_n, ml_m, kv_cache, page_table, win_buf, conv_buf,
           norm_g, final_g, w_ffn_in, w_ffn_out, w_in_even, b_gate_even, w_pool, pool_scale,
           w_out_even, w_in_odd, cmp_pos_w, cmp_w, cmp_b, conv_w, w_out_odd):
    pools, cs, ns, ms, rows, wins, convs = [], [], [], [], [], [], []
    for l in range(DEPTH):
        x = x + 0.5 * _swiglu(_rmsnorm(x, norm_g[l, 0]), w_ffn_in[l, 0], w_ffn_out[l, 0])
        h = _rmsnorm(x, norm_g[l, 1])
        j = l // 2
        if l % 2 == 0:
            y, pb, c, n, m = _even_mixer(h, pos0, pool_buf[j], ml_c[j], ml_n[j], ml_m[j], w_in_even[j],
                                         b_gate_even[j], w_pool[j], pool_scale[j], w_out_even[j])
            pools.append(pb)
            cs.append(c)
            ns.append(n)
            ms.append(m)
        else:
            past = None if kv_cache is None else _gather_past(kv_cache[j], page_table)
            wb = None if win_buf is None else win_buf[j]
            y, r, wn, cn = _odd_mixer(h, pos0, past, wb, conv_buf[j], w_in_odd[j], cmp_pos_w[j],
                                      cmp_w[j], cmp_b[j], conv_w[j], w_out_odd[j])
            rows.append(r)
            wins.append(wn)
            convs.append(cn)
        x = x + y
        x = x + 0.5 * _swiglu(_rmsnorm(x, norm_g[l, 2]), w_ffn_in[l, 1], w_ffn_out[l, 1])
    states = (jnp.stack(pools), jnp.stack(cs), jnp.stack(ns), jnp.stack(ms),
              jnp.stack(rows), jnp.stack(wins), jnp.stack(convs))
    return _rmsnorm(x, final_g), states

def setup_inputs(seed: int = 0) -> dict:
    key = jax.random.key(seed)
    ks = jax.random.split(key, 26)
    f32 = jnp.float32

    def nrm(k, shape, scale=1.0):
        return scale * jax.random.normal(k, shape, f32)

    n_pages = PAST_LEN // PAGE_SIZE
    n_used = DEC_BATCH * n_pages
    n_pool = n_used + (n_used + 3) // 4
    win_len = min(WINDOW, PAST_LEN)
    page_table = jax.random.permutation(ks[9], n_pool)[:n_used].reshape(DEC_BATCH, n_pages).astype(jnp.int32)
    b_gate_even = jnp.concatenate([nrm(ks[15], (N_EVEN, ML_HEADS), 0.1),
                                   FORGET_BIAS + nrm(ks[16], (N_EVEN, ML_HEADS), 0.1)], axis=-1)
    return {
        'x_prompt': nrm(ks[0], (BATCH, SEQ, D_MODEL)),
        'x_sample': nrm(ks[1], (DEC_BATCH, DEC_SEQ, D_MODEL)),
        'state_pool': nrm(ks[2], (N_EVEN, DEC_BATCH, POOL_BUF, POOL_WIDTH)),
        'state_mlstm_c': nrm(ks[3], (N_EVEN, DEC_BATCH, ML_HEADS, ML_DH, ML_DH), 0.3),
        'state_mlstm_n': nrm(ks[4], (N_EVEN, DEC_BATCH, ML_HEADS, ML_DH), 0.3),
        'state_mlstm_m': nrm(ks[5], (N_EVEN, DEC_BATCH, ML_HEADS)),
        'cache_nsa_kv': nrm(ks[6], (N_ODD, n_pool, PAGE_SIZE, 4, KV_HEADS, HEAD_DIM)),
        'state_win_kv': nrm(ks[7], (N_ODD, DEC_BATCH, win_len, 2, KV_HEADS, HEAD_DIM)),
        'state_conv': nrm(ks[8], (N_ODD, DEC_BATCH, CONV_K - 1, CONV_CH)),
        'page_table': page_table,
        'norm_g': 1.0 + nrm(ks[10], (DEPTH, 3, D_MODEL), 0.02),
        'final_g': 1.0 + nrm(ks[11], (D_MODEL,), 0.02),
        'w_ffn_in': nrm(ks[12], (DEPTH, 2, D_MODEL, 2 * D_FF), D_MODEL ** -0.5),
        'w_ffn_out': nrm(ks[13], (DEPTH, 2, D_FF, D_MODEL), D_FF ** -0.5),
        'w_in_even': nrm(ks[14], (N_EVEN, D_MODEL, EVEN_IN), D_MODEL ** -0.5),
        'b_gate_even': b_gate_even,
        'w_pool': nrm(ks[17], (N_EVEN, POOL_GROUPS, POOL_GDIM, POOL_GDIM), POOL_GDIM ** -0.5),
        'pool_scale': 1.0 + nrm(ks[18], (N_EVEN, POOL_WIDTH), 0.02),
        'w_out_even': nrm(ks[19], (N_EVEN, POOL_WIDTH + ML_WIDTH, D_MODEL), D_MODEL ** -0.5),
        'w_in_odd': nrm(ks[20], (N_ODD, D_MODEL, ODD_IN), D_MODEL ** -0.5),
        'cmp_pos_w': (1.0 + nrm(ks[21], (N_ODD, 2, CMP_BLOCK), 0.1)) * (CMP_BLOCK ** -0.5),
        'cmp_w': nrm(ks[22], (N_ODD, 2, HEAD_DIM, HEAD_DIM), HEAD_DIM ** -0.5),
        'cmp_b': nrm(ks[23], (N_ODD, 2, HEAD_DIM), 0.02),
        'conv_w': nrm(ks[24], (N_ODD, CONV_K, CONV_CH), CONV_K ** -0.5),
        'w_out_odd': nrm(ks[25], (N_ODD, NSA_WIDTH + CONV_CH, D_MODEL), D_MODEL ** -0.5),
    }

def reference(x_prompt, x_sample, state_pool, state_mlstm_c, state_mlstm_n, state_mlstm_m,
              cache_nsa_kv, state_win_kv, state_conv, page_table,
              norm_g, final_g, w_ffn_in, w_ffn_out, w_in_even, b_gate_even, w_pool, pool_scale,
              w_out_even, w_in_odd, cmp_pos_w, cmp_w, cmp_b, conv_w, w_out_odd):
    bp = x_prompt.shape[0]
    dt = x_prompt.dtype
    f32 = jnp.float32
    pool0 = jnp.zeros((N_EVEN, bp, POOL_BUF, POOL_WIDTH), dt)
    c0 = jnp.zeros((N_EVEN, bp, ML_HEADS, ML_DH, ML_DH), f32)
    n0 = jnp.zeros((N_EVEN, bp, ML_HEADS, ML_DH), f32)
    m0 = jnp.zeros((N_EVEN, bp, ML_HEADS), f32)
    conv0 = jnp.zeros((N_ODD, bp, CONV_K - 1, CONV_CH), dt)
    y_prompt, (pool_p, c_p, n_p, m_p, kv_p, win_p, conv_p) = _trunk(
        x_prompt, 0, pool0, c0, n0, m0, None, None, None, conv0,
        norm_g, final_g, w_ffn_in, w_ffn_out, w_in_even, b_gate_even, w_pool, pool_scale,
        w_out_even, w_in_odd, cmp_pos_w, cmp_w, cmp_b, conv_w, w_out_odd)
    y_sample, (pool_s, c_s, n_s, m_s, kv_s, win_s, conv_s) = _trunk(
        x_sample, PAST_LEN, state_pool, state_mlstm_c, state_mlstm_n, state_mlstm_m,
        cache_nsa_kv, page_table, state_win_kv, state_conv,
        norm_g, final_g, w_ffn_in, w_ffn_out, w_in_even, b_gate_even, w_pool, pool_scale,
        w_out_even, w_in_odd, cmp_pos_w, cmp_w, cmp_b, conv_w, w_out_odd)
    return (y_prompt, y_sample, pool_p, pool_s, c_p, c_s, n_p, n_s, m_p, m_s,
            kv_p, kv_s, win_p, win_s, conv_p, conv_s)


_drawn_inputs = setup_inputs


def setup_inputs(seed=0):
    import zlib

    import numpy as np

    out = dict(_drawn_inputs(seed))
    spreads = {}
    factors = {'final_g': 2.815, 'pool_scale': 5.99, 'cmp_pos_w': 3.083, 'cmp_b': 8.0}
    for name, (base, spread) in spreads.items():
        noise = np.random.default_rng([zlib.crc32(name.encode()), seed]).standard_normal(out[name].shape)
        drawn = base * np.exp(spread * noise) if base else spread * noise
        out[name] = __import__('jax').numpy.asarray(drawn.astype(out[name].dtype))
    for name, factor in factors.items():
        out[name] = (out[name] * factor).astype(out[name].dtype)
    return out
```

```python
from contextlib import ExitStack

import numpy as np
import concourse.bass as bass
from concourse import mybir

F32 = mybir.dt.float32
I32 = mybir.dt.int32
ALU = mybir.AluOpType
ACT = mybir.ActivationFunctionType
AX = mybir.AxisListType
ds = bass.ds

D = 1024
NK = D // 128
SEQ = 512
NB = 8
NT = 4
TS = NB * NT
T = SEQ + TS
HALF = T // 2
SPLIT = SEQ - HALF
PAST = 2048
PAGE = 128
NPG = PAST // PAGE
DFF = 2816
NF = DFF // 128
EPS = 1e-6
H4 = 4
DH = 192
EC = 96
KTILES = 5
NH = 12
HD = 64
GQ = 6
NCP = SEQ // 16 - 1
NCS = PAST // 16 - 1
NBLK = PAST // 64 + 1
BIG = 3e37
SLOT = 4096

STEPS_FFN = NF // 2 + 8
STEP_EVEN = STEPS_FFN
STEP_HEADS = STEP_EVEN + 1
STEP_EOUT = STEP_HEADS + 2 * H4
STEP_FFN1 = STEP_EOUT + 4
STEP_FFN2 = STEP_FFN1 + STEPS_FFN
STEP_ODD = STEP_FFN2 + STEPS_FFN
STEP_Q = STEP_ODD + 4
STEP_OOUT = STEP_Q + 6
STEP_FFN3 = STEP_OOUT + 4


def slopes():
    return 2.0 ** (-8.0 * np.arange(1, NH + 1) / NH)


def tok_tile(t):
    return 128 if t < 4 else TS


def make_consts():
    parts, at = [], {}

    def put(name, a):
        a = np.asarray(a, np.float32)
        full = np.zeros((128, int(np.prod(a.shape[1:]))), np.float32)
        full[:a.shape[0]] = a.reshape(a.shape[0], -1)
        at[name] = (sum(x.shape[1] for x in parts), full.shape[1])
        parts.append(full)

    p = np.arange(128)
    put("ident", np.eye(128))
    put("ones", np.ones((128, 128)))
    put("zeros", np.zeros((128, 128)))
    put("eps", np.full((128, 1), EPS))
    put("mean", np.full((128, 128), 1.0 / D))
    put("late", np.where(p[:, None] <= p[None, :], 0.0, 1e30))
    s = np.arange(TS)
    same = (s[:, None] // NT) == (s[None, :] // NT)
    put("late_s", np.where(same & (s[:, None] <= s[None, :]), 0.0, 1e30))
    put("of_batch", (s[:, None] // NT) == np.arange(NB)[None, :])
    put("onehot4", np.eye(4))
    w = np.array([[2, 8], [4, 16]])
    wp = w[p // 64]
    put("inv_w", 1.0 / wp)
    put("inv_first", 1.0 / np.minimum(np.arange(16)[None, None, :] + 1.0, wp[:, :, None]))
    c = np.arange(512)
    dist = p[:, None] - (c[None, :] - 384)
    put("dist", np.where(dist >= 0, dist, BIG))
    n = np.arange(32)
    dc = (128 * np.arange(4)[None, :, None] + p[:, None, None]) - (16 * n[None, None, :] + 31)
    put("dist_cmp", np.where((dc >= 0) & (n < NCP)[None, None, :], dc, BIG))
    r = p % 32
    t, hq, g, b2 = r % NT, r // NT, (p // 32) % 2, p // 64
    real = r < GQ * NT
    n = np.arange(128)
    put("dist_cmp_s", PAST + t[:, None] - (16 * n[None, :] + 31))
    put("dist_blk", t[:, None] - np.arange(64)[None, :])
    k = np.arange(512)
    put("dist_win", np.where(k[None, :] > t[:, None], 512 + t[:, None] - k[None, :], BIG))
    pair = np.arange(4)
    ok = ((s[None, None, :] // NT) == (2 * pair[None, :, None] + b2[:, None, None])) & \
        ((s % NT)[None, None, :] <= t[:, None, None])
    put("dist_new", np.where(ok, t[:, None, None] - (s % NT)[None, None, :], BIG))
    sl = slopes()
    put("neg_slope", np.broadcast_to(-sl[None, :], (128, NH)))
    rs = np.where(real, sl[np.minimum(g * GQ + hq, NH - 1)], 1.0)
    put("neg_slope_row", -rs[:, None])
    put("blk_base", -rs[:, None] * (PAST - 64.0 * np.arange(NBLK))[None, :])
    put("same_query", real[:, None] & real[None, :] & (b2[:, None] == b2[None, :]) &
        (g[:, None] == g[None, :]) & (t[:, None] == t[None, :]))
    put("row_token", (s[:, None, None] == ((2 * pair[None, :, None] + b2[None, None, :]) * NT + t[None, None, :])))
    put("row_head", real[:, None] & ((g * GQ + hq)[:, None] == np.arange(NH)[None, :]))
    return np.concatenate(parts, axis=1), at


CONSTS, CAT = make_consts()
NCONST = CONSTS.shape[1]


class Arena:

    def __init__(self, tensor, size):
        self.tensor, self.size, self.at = tensor, size, 0

    def take(self, *shape):
        n = int(np.prod(shape))
        assert self.at + n <= self.size, (self.at, n, self.size)
        v = self.tensor[:, self.at:self.at + n]
        self.at += n
        if len(shape) == 2:
            v = v.rearrange("p (a b) -> p a b", a=shape[0])
        if len(shape) == 3:
            v = v.rearrange("p (a b c) -> p a b c", a=shape[0], b=shape[1])
        return v


class Chain:

    def __init__(self, eng, sem):
        self.eng, self.sem, self.n, self.moving = eng, sem, 0, 0

    def after(self, ins):
        ins.then_inc(self.sem, 1)
        self.n += 1
        self.eng.wait_ge(self.sem, self.n + self.moving)

    def loop(self, i, per, body):
        start = self.n
        self.moving = i * per
        body()
        assert self.n - start == per, ("links of a body", self.n - start)
        self.moving = 0

    def skip(self, count):
        self.n += count


def trunk(nc, x_prompt, x_sample, state_pool, state_mlstm_c, state_mlstm_n, state_mlstm_m,
          cache_nsa_kv, state_win_kv, state_conv, page_table,
          norm_g, final_g, w_ffn_in, w_ffn_out, w_in_even, b_gate_even, w_pool, pool_scale,
          w_out_even, w_in_odd, cmp_pos_w, cmp_w, cmp_b, conv_w, w_out_odd, consts,
          y_prompt, y_sample, pool_p, pool_s, c_p, c_s, n_p, n_s, m_p, m_s,
          kv_rows_p, kv_rows_s, win_p, win_s, conv_p, conv_s):
    ctx = ExitStack()
    with ctx:
        ctx.enter_context(nc.allow_non_contiguous_dma("small transposed vectors"))
        def sb(name, shape, dt=F32):
            return ctx.enter_context(nc.sbuf_tensor(name, shape, dt))

        def sem(name):
            return ctx.enter_context(nc.semaphore(name))

        x = sb("x", [128, NK, T])
        h = sb("h", [128, NK, T])
        ring = sb("ring", [128, 2, SLOT])
        cst = sb("cst", [128, NCONST])
        vecs = sb("vecs", [128, 64])
        ns = sb("ns", [128, 5 * T])
        pt = sb("pt", [1, NB * NPG], I32)
        A_SIZE, G_SIZE = 14080, 2 * NPG * 512
        arena_t = sb("arena_t", [128, A_SIZE])
        pages_t = sb("pages_t", [128, G_SIZE])
        ps = ctx.enter_context(nc.psum_tensor("ps", [128, 8, 512], F32))

        def const(name, rows=128):
            a, n = CAT[name]
            return cst[0:rows, a:a + n]

        ident, ones = const("ident"), const("ones")
        gain = lambda r, c: vecs[:, 8 * r + c:8 * r + c + 1]
        V_POOL, V_CONV = 56, 58
        sq = [ns[:, i * T:(i + 1) * T] for i in (0, 1)]
        sil = [ns[:, i * T:(i + 1) * T] for i in (2, 3)]
        rinv = ns[:, 4 * T:5 * T]
        gated = arena_t[:, 0:NF * T].rearrange("p (f t) -> p f t", f=NF)

        def halves(ap):
            return ap.rearrange("p (s t) -> p s t", s=2)

        def banks(b, rows=128):
            return ps[0:rows, b:b + 2, 0:HALF]

        consts_in, inputs_in = sem("consts_in"), sem("inputs_in")
        x_in = [sem(f"x_in_{t}") for t in range(KTILES)]
        weights_in = [sem("weights_in_0"), sem("weights_in_1")]
        step_done = sem("step_done")
        vecs_flip, vecs_ready = sem("vecs_flip"), sem("vecs_ready")
        x_flipped, x_copied, x_taken = sem("x_flipped"), sem("x_copied"), sem("x_taken")
        sq_ready, sq_used = sem("sq_ready"), sem("sq_used")
        rms_ready, rinv_ready, h_ready = sem("rms_ready"), sem("rinv_ready"), sem("h_ready")
        up_first, sil_ready, up_free = sem("up_first"), sem("sil_ready"), sem("up_free")
        down_done, down_free = sem("down_done"), sem("down_free")
        y_flipped, y_copied, y_stored = sem("y_flipped"), sem("y_copied"), sem("y_stored")
        stored = sem("stored")
        vchain = sem("vchain")
        n_stored = [0]

        def use_step(pe, n, moved=0):
            pe.wait_ge(weights_in[n % 2], 32 * (n // 2 + 1) + moved)

        def slot(n, *shape):
            v = ring[:, n % 2, 0:int(np.prod(shape))]
            if len(shape) == 2:
                return v.rearrange("p (k n) -> p k n", k=shape[0])
            return v.rearrange("p (a k n) -> p a k n", a=shape[0], k=shape[1])

        def load(sp, n, out_in, moved=0, first=False):
            if n >= 2 or not first:
                sp.wait_ge(step_done, n - 1 + moved)
            for o, i in out_in:
                sp.dma_start(o, i).then_inc(weights_in[n % 2], 16)

        def load_ffn(sp, f, base):
            w_in = w_ffn_in[f // 2, f % 2].rearrange("(k p) n -> p k n", p=128)
            w_out = w_ffn_out[f // 2, f % 2].rearrange("(k p) n -> p k n", p=128)

            def up(j, at, moved, first):
                n = base + j
                v = slot(n, 2, NK, 256)
                load(sp, n, [(v[:, 0], w_in[:, :, ds(at, 256)]),
                             (v[:, 1], w_in[:, :, ds(at + DFF, 256)])], moved, first)

            def down(j, at, moved):
                n = base + NF // 2 + j
                v = slot(n, NF // 2, 256)
                k = (j % 2) * (NF // 2)
                load(sp, n, [(v[:, 0:6], w_out[:, k:k + 6, ds(at, 256)]),
                             (v[:, 6:11], w_out[:, k + 6:k + 11, ds(at, 256)])], moved)

            if base == 0:
                up(0, 0, 0, True)
                up(1, 256, 0, True)
                with sp.Fori(1, 5) as i:
                    for u in range(2):
                        up(u, i * 512 + 256 * u, i * 2, False)
            else:
                with sp.Fori(0, 5) as i:
                    for u in range(2):
                        up(u, i * 512 + 256 * u, i * 2, False)
            up(10, 2560, 0, False)
            with sp.Fori(0, 2) as i:
                for j in range(4):
                    down(j, i * 512 + 256 * (j // 2), i * 4)

        def pe_ffn(pe, f, base):
            pe.wait_ge(h_ready, NK * ([0, 2, 3, 5][f] + 1))

            def up(j, i):
                n = base + j
                use_step(pe, n, i * 32)
                w = slot(n, 2, NK, 256)
                for u in range(2):
                    pe.wait_ge(up_free, 24 * f + 2 * j + u + 1 + i * 4)
                    for ab in range(2):
                        for k in range(NK):
                            for s in range(2):
                                mm = pe.matmul(ps[:, 4 * u + 2 * ab + s, 0:HALF], w[:, ab, k, 128 * u:128 * u + 128],
                                               h[:, k, HALF * s:HALF * s + HALF], start=(k == 0), stop=(k == NK - 1))
                    mm.then_inc(up_first if u == 0 else step_done, 1)

            with pe.Fori(0, 5) as i:
                up(0, i)
                up(1, i)
            up(10, 0)
            pe.wait_ge(up_free, 24 * f + 24)

            def down(j, i):
                n = base + NF // 2 + j
                q = [0, 2, 3, 5][f]
                use_step(pe, n, i * 64)
                w = slot(n, NF // 2, 256)
                if j % 2 == 0:
                    pe.wait_ge(down_free, 6 * q + j // 2 + 1 + i * 2)
                for c in range(2):
                    for k in range(NF // 2):
                        for s in range(2):
                            mm = pe.matmul(ps[:, 4 * (j // 2) + 2 * c + s, 0:HALF], w[:, k, 128 * c:128 * c + 128],
                                           gated[:, (j % 2) * (NF // 2) + k, HALF * s:HALF * s + HALF],
                                           start=(j % 2 == 0 and k == 0), stop=(j % 2 == 1 and k == NF // 2 - 1))
                mm.then_inc(step_done, 1)

            with pe.Fori(0, 2) as i:
                for j in range(4):
                    down(j, i)

        def act_ffn(act, f, base):
            def up(j, i):
                for u in range(2):
                    if u == 0:
                        act.wait_ge(up_first, 11 * f + j + 1 + i * 2)
                    else:
                        act.wait_ge(step_done, base + j + 1 + i * 2)
                    act.activation(halves(sil[u]), banks(4 * u), ACT.Silu).then_inc(sil_ready, 1)

            with act.Fori(0, 5) as i:
                up(0, i)
                up(1, i)
            up(10, 0)

        def dve_ffn(dve, f, base):
            q = [0, 2, 3, 5][f]
            dve.sem_inc(up_free, 2)

            def up(c, at, i):
                dve.wait_ge(sil_ready, NF * f + c + 1 + i * 4)
                dve.tensor_tensor(gated[:, ds(at, 1)].rearrange("p a (s t) -> p (a s) t", s=2), halves(sil[c % 2]),
                                  banks(4 * (c % 2) + 2), ALU.mult).then_inc(up_free, 1)

            with dve.Fori(0, 5) as i:
                for c in range(4):
                    up(c, i * 4 + c, i)
            for c in (20, 21):
                up(c, c, 0)
            dve.sem_inc(down_free, 2)
            dve_add(dve, q, base + NF // 2, 2, 0.5)

        def dve_add(dve, q, base, per, scale):
            with dve.Fori(0, 2) as i:
                for u in range(2):
                    dve.wait_ge(step_done, base + per * (u + 1) + i * (2 * per))
                    for c in range(2):
                        xs = x[:, ds(i * 4 + 2 * u + c, 1)].rearrange("p a (s t) -> p (a s) t", s=2)
                        add = dve.scalar_tensor_tensor(out=xs, in0=banks(4 * u + 2 * c), scalar=scale,
                                                       in1=xs, op0=ALU.mult, op1=ALU.add)
                    add.then_inc(down_free, 1)

        def act_norm(act, r):
            if r == 0:
                act.wait_ge(x_copied, KTILES)
                act.wait_ge(x_taken, KTILES)
            else:
                act.wait_ge(down_free, 6 * r)
            for c in range(NK):
                if c >= 2:
                    act.wait_ge(sq_used, NK * r + c - 1)
                act.activation(sq[c % 2], x[:, c, :], ACT.Square).then_inc(sq_ready, 1)
            act.wait_ge(sq_used, NK * (r + 1))
            act.activation(halves(rinv), banks(0), ACT.Sqrt, bias=const("eps")).then_inc(rms_ready, 1)

        def pe_norm(pe, r):
            if r > 0:
                pe.wait_ge(down_free, 6 * r)
            else:
                pe.wait_ge(x_copied, KTILES)
                pe.wait_ge(x_taken, KTILES)
            for c in range(NK):
                pe.wait_ge(sq_ready, NK * r + c + 1)
                for s in range(2):
                    mm = pe.matmul(ps[:, s, 0:HALF], const("mean"), sq[c % 2][:, HALF * s:HALF * s + HALF],
                                   start=(c == 0), stop=(c == NK - 1))
                mm.then_inc(sq_used, 1)

        def dve_norm(dve, r):
            dve.wait_ge(rms_ready, r + 1)
            if r == 0:
                dve.wait_ge(vecs_ready, 1)
            dve.reciprocal(rinv, rinv).then_inc(rinv_ready, 1)
            dve.wait_ge(rinv_ready, r + 1)
            for c in range(NK):
                dve.scalar_tensor_tensor(out=h[:, c, :], in0=x[:, c, :], scalar=gain(r, c), in1=rinv,
                                         op0=ALU.mult, op1=ALU.mult).then_inc(h_ready, 1)

        xt = arena_t[:, 0:KTILES * D].rearrange("p (t n) -> p t n", t=KTILES)
        gain_rows = pages_t[0:64, G_SIZE - 128:G_SIZE]

        def flip(pe, out, in_):
            k, m = in_.shape[0], int(np.prod(in_.shape[1:]))
            if k == 128 and m == 128:
                return pe.transpose(out, in_, ident)
            return pe.matmul(out, in_, ident[0:k, 0:k], start=True, stop=True)

        def pe_load(pe):
            pe.wait_ge(consts_in, 16)
            pe.wait_ge(inputs_in, 64)
            flip(pe, ps[:, 7, 0:64], gain_rows[0:64, :]).then_inc(vecs_flip, 1)
            for t in range(KTILES):
                pe.wait_ge(x_in[t], 16)
                if t >= 2:
                    pe.wait_ge(x_copied, t - 1)
                    pe.wait_ge(x_taken, t - 1)
                for c in range(NK):
                    mm = flip(pe, ps[:, 2 * (t % 2) + c // 4, 128 * (c % 4):128 * (c % 4) + tok_tile(t)],
                              xt[0:tok_tile(t), t, 128 * c:128 * c + 128])
                mm.then_inc(x_flipped, 1)

        def sp_load(sp):
            sp.dma_start(cst[:, :], consts).then_inc(consts_in, 16)
            sp.dma_start(gain_rows[0:48, :], norm_g.rearrange("l s (c p) -> (l s c) p", p=128)).then_inc(inputs_in, 16)
            sp.dma_start(gain_rows[48:56, :], final_g.rearrange("(c p) -> c p", p=128)).then_inc(inputs_in, 16)
            sp.dma_start(gain_rows[56:58, :], pool_scale[0].rearrange("(c p) -> c p", p=128)).then_inc(inputs_in, 16)
            sp.dma_start(gain_rows[58:64, :], conv_w[0].rearrange("j (c p) -> (j c) p", p=128)).then_inc(inputs_in, 16)
            for t in range(4):
                sp.dma_start(xt[:, t, :], x_prompt[0, 128 * t:128 * t + 128, :]).then_inc(x_in[t], 16)
            sp.dma_start(xt[0:TS, 4, :], x_sample.rearrange("b t n -> (b t) n")).then_inc(x_in[4], 16)

        def copy_x(eng, copy, lo, done):
            for t in range(KTILES):
                w = tok_tile(t)
                eng.wait_ge(x_flipped, t + 1)
                copy(x[:, lo:lo + 4, 128 * t:128 * t + w],
                     ps[:, 2 * (t % 2) + lo // 4, :].rearrange("p (c t) -> p c t", c=4)[:, :, 0:w]).then_inc(done, 1)

        def act_load(act):
            copy_x(act, act.copy, 0, x_copied)

        def dve_load(dve):
            dve.wait_ge(vecs_flip, 1)
            dve.tensor_copy(vecs[:, :], ps[:, 7, 0:64]).then_inc(vecs_ready, 1)
            copy_x(dve, dve.tensor_copy, 4, x_taken)

        yt = xt

        def pe_final(pe):
            pe.wait_ge(h_ready, NK * 7)
            for t in range(KTILES):
                w = tok_tile(t)
                if t >= 2:
                    pe.wait_ge(y_copied, t - 1)
                for c in range(NK):
                    mm = flip(pe, ps[0:w, 4 + 2 * (t % 2) + c // 4, 128 * (c % 4):128 * (c % 4) + 128],
                              h[:, c, 128 * t:128 * t + w])
                mm.then_inc(y_flipped, 1)

        def act_final(act):
            for t in range(KTILES):
                w = tok_tile(t)
                act.wait_ge(y_flipped, t + 1)
                b = 4 + 2 * (t % 2)
                act.copy(yt[0:w, t, :].rearrange("p (b n) -> p b n", b=2), ps[0:w, b:b + 2, :]).then_inc(y_copied, 1)
                act.wait_ge(y_copied, t + 1)
                out = y_prompt[0, 128 * t:128 * t + w, :] if t < 4 else y_sample.rearrange("b t n -> (b t) n")
                act.dma_start(out, yt[0:w, t, :]).then_inc(y_stored, 16)
            act.wait_ge(y_stored, 16 * KTILES)

        A, G = Arena(arena_t, A_SIZE), Arena(pages_t, G_SIZE - 128)
        yml = A.take(2 * H4, T)
        ypool = A.take(2, T)
        uep, ues = A.take(2, 15 + SEQ), A.take(2, NB, 15 + NT)
        w2p, w2s = A.take(2, 15 + SEQ), A.take(2, NB, 15 + NT)
        w4p, w4s = A.take(2, 15 + SEQ), A.take(2, NB, 15 + NT)
        mixed = A.take(2, T)
        ROW = 2 * T + TS + NB
        rows, rows_h = A.take(ROW), A.take(ROW)
        acol, wkcol = A.take(KTILES, H4), A.take(KTILES, H4)
        dec_b = A.take(H4)
        kw = A.take(KTILES, DH)
        qT, kT, ogT = G.take(2, T), G.take(2, T), G.take(2, T)
        vtok = G.take(KTILES, DH)
        kwb = G.take(NB, DH)
        wt = G.take(4, SEQ)
        cS = G.take(NB, 2, DH)
        cT = G.take(2, 2, DH)
        c_new_p, n_new_p = G.take(2, DH), G.take(DH)
        nS, nN = G.take(H4, DH), G.take(H4, DH)
        nT = G.take(2, H4, NB)
        pool_rows = G.take(256)
        wp_bd = G.take(2, 128)
        u_rows = G.take(2, 256)
        em_s, den_s, wts = G.take(TS), G.take(TS), G.take(TS)
        qn, acc_s = G.take(2, TS), G.take(2, TS)
        small = G.take(160)
        a_s, dec_s = small[:, 32:64], small[:, 96:104]
        m0, b_i, b_f, m_out = G.take(NB), G.take(1), G.take(1), G.take(NB)
        em, rden = ns[0:EC, 0:SEQ], ns[0:EC, T:T + SEQ]
        gate = Arena(arena_t, 8 * T)
        g_i, g_f, g_l, g_e, g_a, g_x = (gate.take(T) for _ in range(6))
        g_wk = gate.take(T)
        ones4, head4 = ones[0:4, :], const("onehot4", 4)

        ein, wp_in, c_in = sem("ein"), sem("wp_in"), sem("c_in")
        zeroed, gchain = sem("zeroed"), sem("gchain")
        e0_done, u_ready, mixed_ready = sem("e0_done"), sem("u_ready"), sem("mixed_ready")
        prefix_flip, prefix_ready = sem("prefix_flip"), sem("prefix_ready")
        gf_ready, gl_ready = sem("gf_ready"), sem("gl_ready")
        wk_arg, wk_ready, mout_ready = sem("wk_arg"), sem("wk_ready"), sem("mout_ready")
        cols_flip, cols_ready = sem("cols_flip"), sem("cols_ready")
        q_done, qT_ready, kT_ready, v_done, v_ready, og_ready = (sem(n) for n in (
            "q_done", "qT_ready", "kT_ready", "v_done", "v_ready", "og_ready"))
        rowh_ready, mb_done, kflip_done, kw_ready = sem("rowh_ready"), sem("mb_done"), sem("kflip_done"), sem("kw_ready")
        warg_ready, w_ready, s_done, sT_ready = sem("warg_ready"), sem("w_ready"), sem("s_done"), sem("sT_ready")
        small_done, small_ready, wsarg_ready, ws_ready = (sem(n) for n in (
            "small_done", "small_ready", "wsarg_ready", "ws_ready"))
        mrow_done, em_ready, num_done, den_done = sem("mrow_done"), sem("em_ready"), sem("num_done"), sem("den_done")
        cp_done, cp_ready, yp_ready = sem("cp_done"), sem("cp_ready"), sem("yp_ready")
        ct_done, cT_ready, cn_done, cn_ready = sem("ct_done"), sem("cT_ready"), sem("cn_done"), sem("cn_ready")
        qn_ready, sfin_done, head_free = sem("qn_ready"), sem("sfin_done"), sem("head_free")
        ypool_done, ypool_ready, rows_done, rows_ready = (sem(n) for n in (
            "ypool_done", "ypool_ready", "rows_done", "rows_ready"))
        c_stored, waited = sem("c_stored"), sem("waited")
        SEGS = [(0, 0, HALF, 0), (1, 0, SPLIT, HALF)]

        def load_even(sp):
            w = w_in_even[0].rearrange("(k p) n -> p k n", p=128)
            n = STEP_EVEN
            v = slot(n, NK, 264)
            load(sp, n, [(v[:, :, 0:256], w[:, :, 0:256]), (v[:, :, 256:264], w[:, :, 3328:3336])])
            with sp.Fori(0, H4) as i:
                for u in range(2):
                    n = STEP_HEADS + u
                    v = slot(n, NK, 2 * DH)
                    a, b = ((256, 1024), (1792, 2560))[u]
                    load(sp, n, [(v[:, :, 0:DH], w[:, :, ds(i * DH + a, DH)]),
                                 (v[:, :, DH:2 * DH], w[:, :, ds(i * DH + b, DH)])], i * 2)
            wo = w_out_even[0]
            with sp.Fori(0, 2) as i:
                for u in range(2):
                    n = STEP_EOUT + u
                    v = slot(n, 10, 256)
                    at = i * 512 + 256 * u
                    load(sp, n, [(v[:, 0:2], wo[0:256].rearrange("(k p) n -> p k n", p=128)[:, :, ds(at, 256)]),
                                 (v[0:EC, 2:10], wo[256:D].rearrange("(k p) n -> p k n", p=EC)[:, :, ds(at, 256)])],
                         i * 2)

        def pool_even(po, C):
            po.memset(wp_bd[:, :, :], 0.0).then_inc(zeroed, 1)
            po.dma_start(pool_rows[0:120, :], state_pool[0].rearrange("b r n -> (b r) n")).then_inc(ein, 16)
            po.dma_start(nS[0:NB, :, :], state_mlstm_n[0]).then_inc(ein, 16)
            po.dma_start(m0[0:H4, :], state_mlstm_m[0].rearrange("b h -> h b")).then_inc(ein, 16)
            po.dma_start(b_i[0:H4, :], b_gate_even[0, 0:H4].rearrange("(h o) -> h o", o=1)).then_inc(ein, 16)
            po.dma_start(b_f[0:H4, :], b_gate_even[0, H4:2 * H4].rearrange("(h o) -> h o", o=1)).then_inc(ein, 16)
            po.wait_ge(zeroed, 1)
            for g in range(4):
                r = 64 * (g % 2)
                po.dma_start(wp_bd[r:r + 64, g // 2, r:r + 64], w_pool[0, g]).then_inc(wp_in, 16)
            po.dma_start(pool_s[0, :, 0:11, :], state_pool[0, :, 4:15, :]).then_inc(stored, 16)
            n_stored[0] += 1
            po.wait_ge(h_ready, NK * 2)
            po.memset(uep[:, :, 0:15], 0.0).then_inc(zeroed, 1)
            po.wait_ge(zeroed, 2)
            po.wait_ge(u_ready, 6)
            po.wait_ge(prefix_ready, 1)
            for e, a, b in ((uep, w2p, w4p), (ues, w2s, w4s)):
                v = lambda t, lo, hi: t[..., lo:hi]
                n = 15 + (SEQ if e is uep else NT)
                c1 = lambda t: t[:, 1]
                C.after(po.tensor_tensor(v(a, 1, n), v(e, 1, n), v(e, 0, n - 1), ALU.add))
                C.after(po.tensor_tensor(v(b, 3, n), v(a, 3, n), v(a, 1, n - 2), ALU.add))
                C.after(po.tensor_tensor(v(c1(a), 7, n), v(c1(b), 7, n), v(c1(b), 3, n - 4), ALU.add))
                C.after(po.tensor_tensor(v(c1(b), 15, n), v(c1(a), 15, n), v(c1(a), 7, n - 8), ALU.add))
            inv_w, inv_f = const("inv_w"), const("inv_first").rearrange("p (c t) -> p c t", c=2)
            mp, ms = mixed[:, :, 0:SEQ], mixed[:, :, SEQ:T].rearrange("p c (b t) -> p c b t", b=NB)
            for r, sp_, ss_ in ((0, w2p, w2s), (64, w4p, w4s)):
                q = slice(r, r + 64)
                for c in range(2):
                    C.after(po.tensor_scalar(mp[q, c], sp_[q, c, 15:15 + SEQ], inv_w[q, c:c + 1], None, ALU.mult))
                    C.after(po.tensor_scalar(ms[q, c], ss_[q, c, :, 15:15 + NT], inv_w[q, c:c + 1], None, ALU.mult))
                C.after(po.tensor_tensor(mp[q, :, 0:16], sp_[q, :, 15:31], inv_f[q], ALU.mult))
            C.after(po.tensor_tensor(mp, mp, uep[:, :, 15:15 + SEQ], ALU.subtract))
            for c in range(2):
                po.tensor_tensor(ms[:, c], ms[:, c], ues[:, c, :, 15:15 + NT], ALU.subtract).then_inc(mixed_ready, 1)

            po.wait_ge(mout_ready, 1)
            po.dma_start(m_s[0].rearrange("b h -> h b"), m_out[0:H4, :]).then_inc(stored, 16)
            po.dma_start(m_p[0, 0].rearrange("(h o) -> h o", o=1), rows[0:H4, T + SEQ - 1:T + SEQ]).then_inc(stored, 16)
            n_stored[0] += 2
            with po.Fori(0, H4) as i:
                po.wait_ge(head_free, i + 1)
                po.sem_inc(waited, 1)
                for b in range(NB):
                    po.dma_start(cS[0:EC, b], state_mlstm_c[0, b, ds(i, 1)].rearrange("h (e p) d -> p (h e) d", p=EC)
                                 ).then_inc(c_in, 16)
                po.wait_ge(cp_ready, i * 2 + 2)
                po.sem_inc(waited, 1)
                po.dma_start(c_p[0, 0, ds(i, 1)].rearrange("h (e p) d -> p (h e) d", p=EC), c_new_p[0:EC]
                             ).then_inc(c_stored, 16)
                po.dma_start(n_p[0, 0, ds(i, 1)], n_new_p[0:1, :]).then_inc(c_stored, 16)
                for b in range(NB):
                    po.wait_ge(cn_ready, i * NB + b + 1)
                    po.sem_inc(waited, 1)
                    po.dma_start(c_s[0, b, ds(i, 1)].rearrange("h (e p) d -> p (h e) d", p=EC), cS[0:EC, b]
                                 ).then_inc(c_stored, 16)
                po.wait_ge(c_stored, i * (16 * (NB + 2)) + 16 * (NB + 2))
            po.wait_ge(head_free, H4 + 1)
            po.dma_start(n_s[0], nN[0:NB]).then_inc(stored, 16)
            po.wait_ge(rows_ready, 2)
            po.dma_start(pool_p[0, 0], u_rows[0:15, 0]).then_inc(stored, 16)
            for b in range(NB):
                po.dma_start(pool_s[0, b, 11:15, :], u_rows[NT * b:NT * b + NT, 1]).then_inc(stored, 16)
            n_stored[0] += NB + 2

        def project(pe, w, cols, m, b):
            for k in range(NK):
                for s in range(2):
                    mm = pe.matmul(ps[0:m, b + s, 0:HALF], w[:, k, cols:cols + m], h[:, k, HALF * s:HALF * s + HALF],
                                   start=(k == 0), stop=(k == NK - 1))
            return mm

        def project_tok(pe, out, w, lo, hi, t):
            for k in range(NK):
                mm = pe.matmul(out, h[:, k, 128 * t:128 * t + tok_tile(t)], w[:, k, lo:hi],
                               start=(k == 0), stop=(k == NK - 1))
            return mm

        def pe_even(pe):
            n = STEP_EVEN
            use_step(pe, n)
            pe.wait_ge(h_ready, NK * 2)
            w = slot(n, NK, 264)
            project(pe, w, 256, 4, 4)
            project(pe, w, 260, 4, 6).then_inc(e0_done, 1)
            project(pe, w, 0, 128, 0)
            project(pe, w, 128, 128, 2).then_inc(step_done, 1)
            pe.wait_ge(ein, 80)
            pe.wait_ge(gf_ready, 2)
            for c in range(2):
                mm = flip(pe, ps[:, 4, 128 * c:128 * c + 120], pool_rows[0:120, 128 * c:128 * c + 128])
            mm.then_inc(prefix_flip, 1)
            for hd in range(H4):
                for c in range(2):
                    mm = flip(pe, ps[0:EC, 5, (c * H4 + hd) * NB:(c * H4 + hd + 1) * NB], nS[0:NB, hd, EC * c:EC * c + EC])
            mm.then_inc(prefix_flip, 1)
            pe.wait_ge(wk_ready, 1)
            for t in range(KTILES):
                r = slice(128 * t, 128 * t + tok_tile(t))
                flip(pe, ps[0:tok_tile(t), 6, 4 * t:4 * t + 4], g_a[0:4, r])
                flip(pe, ps[0:tok_tile(t), 6, 32 + 4 * t:36 + 4 * t], g_wk[0:4, r])
            flip(pe, ps[0:NB, 6, 64:68], rows[0:4, 2 * T + TS:ROW]).then_inc(cols_flip, 1)
            pe.wait_ge(u_ready, 6)
            pe.wait_ge(prefix_ready, 2)
            pe.wait_ge(cols_ready, 2)
            with pe.Fori(0, H4) as i:
                pe_head(pe, i)
            pe.wait_ge(head_free, H4 + 1)
            pe.wait_ge(mixed_ready, 2)
            for c in range(2):
                for s in range(2):
                    mm = pe.matmul(ps[:, 2 * c + s, 0:HALF], wp_bd[:, c, :], mixed[:, c, HALF * s:HALF * s + HALF],
                                   start=True, stop=True)
            mm.then_inc(ypool_done, 1)
            for c in range(2):
                flip(pe, ps[0:15, 4, 128 * c:128 * c + 128], uep[:, c, SEQ:SEQ + 15])
                mm = flip(pe, ps[0:TS, 5, 128 * c:128 * c + 128], mixed_u(c))
            mm.then_inc(rows_done, 1)
            pe.wait_ge(ypool_ready, 2)
            pe.wait_ge(rows_ready, 2)
            rhs = [(128, ypool[:, c]) for c in range(2)] + [(EC, yml[0:EC, c]) for c in range(2 * H4)]
            with pe.Fori(0, 2) as i:
                for u in range(2):
                    pe_out(pe, 1, STEP_EOUT, u, i, rhs)

        def mixed_u(c):
            return u_last[:, c, :]

        u_last = G.take(2, TS)

        def pe_out(pe, q, base, u, i, rhs):
            n = base + u
            use_step(pe, n, i * 32)
            pe.wait_ge(down_free, 6 * q + u + 1 + i * 2)
            w = slot(n, len(rhs), 256)
            for c in range(2):
                for k, (rows_k, r) in enumerate(rhs):
                    for s in range(2):
                        mm = pe.matmul(ps[:, 4 * u + 2 * c + s, 0:HALF], w[0:rows_k, k, 128 * c:128 * c + 128],
                                       r[:, HALF * s:HALF * s + HALF], start=(k == 0), stop=(k == len(rhs) - 1))
            mm.then_inc(step_done, 1)

        def pe_head(pe, i):
            pe.wait_ge(head_free, i + 1)
            use_step(pe, STEP_HEADS, i * 32)
            w = slot(STEP_HEADS, NK, 2 * DH)
            for c in range(2):
                mm = project(pe, w, EC * c, EC, 2 * c)
            mm.then_inc(q_done, 1)
            for c in range(2):
                mm = project(pe, w, DH + EC * c, EC, 4 + 2 * c)
            mm.then_inc(step_done, 1)
            use_step(pe, STEP_HEADS + 1, i * 32)
            w = slot(STEP_HEADS + 1, NK, 2 * DH)
            pe.wait_ge(qT_ready, i * 2 + 2)
            for t in range(KTILES):
                mm = project_tok(pe, ps[0:tok_tile(t), t // 2, DH * (t % 2):DH * (t % 2) + DH], w, 0, DH, t)
            mm.then_inc(v_done, 1)
            pe.wait_ge(rowh_ready, i + 1)
            pe.matmul(ps[:, 3, :], ones4, rows_h[0:4, 0:SEQ], start=True, stop=True).then_inc(mb_done, 1)
            pe.wait_ge(kT_ready, i * 2 + 2)
            for c in range(2):
                mm = project(pe, w, DH + EC * c, EC, 4 + 2 * c)
            mm.then_inc(step_done, 1)
            pe.wait_ge(v_ready, i * 2 + 2)
            for t in range(KTILES):
                for c in range(2):
                    mm = flip(pe, ps[0:tok_tile(t), t // 2, DH * (t % 2) + EC * c:DH * (t % 2) + EC * c + EC],
                              kT[0:EC, c, 128 * t:128 * t + tok_tile(t)])
            mm.then_inc(kflip_done, 1)
            pe.wait_ge(og_ready, i * 2 + 2)
            for j in range(4):
                for c in range(2):
                    mm = pe.matmul(ps[:, 4 + j, 128 * j:SEQ], kT[0:EC, c, 128 * j:128 * j + 128],
                                   qT[0:EC, c, 128 * j:SEQ], start=(c == 0), stop=(c == 1))
                mm.then_inc(s_done, 1)
            pe.wait_ge(kw_ready, i * 6 + 5)
            pe.matmul(ps[0:EC, 0, 32:64], ones4[:, 0:EC], rows_h[0:4, 2 * T:2 * T + TS], start=True, stop=True)
            pe.matmul(ps[0:EC, 0, 0:32], ones4[:, 0:EC], rows_h[0:4, SEQ:T], start=True, stop=True)
            pe.matmul(ps[0:EC, 0, 64:96], ones4[:, 0:EC], rows_h[0:4, T + SEQ:2 * T], start=True, stop=True)
            pe.matmul(ps[0:EC, 0, 96:104], ones4[:, 0:EC], rows_h[0:4, 2 * T + TS:ROW], start=True, stop=True)
            for c in range(2):
                mm = pe.matmul(ps[0:TS, 0, 128:160], kT[0:EC, c, SEQ:T], qT[0:EC, c, SEQ:T], start=(c == 0), stop=(c == 1))
            mm.then_inc(small_done, 1)
            pe.wait_ge(warg_ready, i * 4 + 4)
            pe.matmul(ps[0:EC, 3, :], ones4[:, 0:EC], rows_h[0:4, T:T + SEQ], start=True, stop=True).then_inc(mrow_done, 1)
            for c in range(2):
                for j in range(4):
                    if c == 0:
                        pe.wait_ge(sT_ready, i * 4 + j + 1)
                    mm = pe.matmul(ps[0:EC, 1 + c, 128 * j:SEQ], vtok[:, j, EC * c:EC * c + EC], wt[:, j, 128 * j:SEQ],
                                   start=(j == 0), stop=(j == 3))
            mm.then_inc(num_done, 1)
            for j in range(4):
                mm = pe.matmul(ps[0:EC, 4, 128 * j:SEQ], ones[:, 0:EC], wt[:, j, 128 * j:SEQ], start=(j == 0), stop=(j == 3))
            mm.then_inc(den_done, 1)
            for c in range(2):
                for j in range(4):
                    pe.matmul(ps[0:EC, 5, DH * c:DH * c + DH], vtok[:, j, EC * c:EC * c + EC], kw[:, j, :],
                              start=(j == 0), stop=(j == 3))
            for j in range(4):
                mm = pe.matmul(ps[0:1, 6, 0:DH], ones[:, 0:1], kw[:, j, :], start=(j == 0), stop=(j == 3))
            mm.then_inc(cp_done, 1)
            pe.wait_ge(c_in, i * (16 * NB) + 16 * NB)
            pe.wait_ge(yp_ready, i * 2 + 2)
            pe.wait_ge(cp_ready, i * 2 + 2)

            def c_flip(b):
                if b >= 2:
                    pe.wait_ge(cT_ready, i * NB + b - 1)
                for e in range(2):
                    for d in range(2):
                        mm = pe.matmul(ps[0:EC, 4 + b % 2, DH * d + EC * e:DH * d + EC * e + EC],
                                       cS[0:EC, b, e, EC * d:EC * d + EC], ident[0:EC, 0:EC], start=True, stop=True)
                mm.then_inc(ct_done, 1)

            pe.wait_ge(small_ready, i + 1)
            c_flip(0)
            for b in range(NB):
                if b + 1 < NB:
                    c_flip(b + 1)
                pe.wait_ge(cT_ready, i * NB + b + 1)
                for e in range(2):
                    for d in range(2):
                        pe.matmul(ps[0:EC, 0, 288 + 32 * e + NT * b:288 + 32 * e + NT * b + NT],
                                  cT[0:EC, b % 2, d, EC * e:EC * e + EC], qT[0:EC, d, SEQ + NT * b:SEQ + NT * b + NT],
                                  start=(d == 0), stop=(d == 1))
                if b == 0:
                    pe.wait_ge(kw_ready, i * 6 + 6)
                if b >= 2:
                    pe.wait_ge(cn_ready, i * NB + b - 1)
                for e in range(2):
                    mm = pe.matmul(ps[0:EC, 6 + b % 2, DH * e:DH * e + DH], vtok[0:TS, 4, EC * e:EC * e + EC],
                                   kwb[0:TS, b, :], start=True, stop=True)
                mm.then_inc(cn_done, 1)
            pe.matmul(ps[0:NB, 1, 0:DH], const("of_batch", TS), kw[0:TS, 4, :], start=True, stop=True)
            pe.wait_ge(ws_ready, i * 2 + 2)
            pe.wait_ge(qn_ready, i + 1)
            for c in range(2):
                pe.matmul(ps[0:EC, 0, 160 + 32 * c:192 + 32 * c], vtok[0:TS, 4, EC * c:EC * c + EC], wts[0:TS, :],
                          start=True, stop=True)
            pe.matmul(ps[0:EC, 0, 224:256], ones[0:TS, 0:EC], wts[0:TS, :], start=True, stop=True)
            for c in range(2):
                mm = pe.matmul(ps[0:EC, 0, 256:288], ones[0:EC, 0:EC], qn[0:EC, c, :], start=(c == 0), stop=(c == 1))
            mm.then_inc(sfin_done, 1)

        def act_even(act):
            act.wait_ge(gf_ready, 3)
            act.activation(g_e[0:4], g_x[0:4], ACT.Exp).then_inc(gl_ready, 1)
            act.wait_ge(gl_ready, 1)
            act.activation(g_l[0:4], g_e[0:4], ACT.Ln, bias=1.0).then_inc(gl_ready, 1)
            act.wait_ge(step_done, STEP_EVEN + 1)
            for c in range(2):
                for s, lo, hi, at in SEGS:
                    act.copy(uep[:, c, 15 + at:15 + at + hi - lo], ps[:, 2 * c + s, lo:hi]).then_inc(u_ready, 1)
                act.copy(ues[:, c, :, 15:15 + NT],
                         ps[:, 2 * c + 1, SPLIT:HALF].rearrange("p (b t) -> p b t", b=NB)).then_inc(u_ready, 1)
                act.copy(u_last[:, c, :], ps[:, 2 * c + 1, SPLIT:HALF])
            act.wait_ge(prefix_flip, 2)
            act.copy(ues[:, :, :, 0:15], ps[:, 4, 0:256].rearrange("p (c n) -> p c n", c=2)[:, :, 0:120]
                     .rearrange("p c (b r) -> p c b r", b=NB)).then_inc(prefix_ready, 1)
            act.copy(nT[0:EC].rearrange("p c h b -> p (c h b)"), ps[0:EC, 5, 0:2 * H4 * NB]).then_inc(prefix_ready, 1)
            act.wait_ge(wk_arg, 2)
            act.activation(rows[0:4, 2 * T:ROW], rows[0:4, 2 * T:ROW], ACT.Exp)
            act.activation(g_wk[0:4], g_wk[0:4], ACT.Exp).then_inc(wk_ready, 1)
            with act.Fori(0, H4) as i:
                act_head(act, i)
            act.wait_ge(ypool_done, 1)
            for c in range(2):
                act.activation(halves(ypool[:, c]), banks(2 * c), ACT.Copy,
                               scale=vecs[:, V_POOL + c:V_POOL + c + 1]).then_inc(ypool_ready, 1)
            act.wait_ge(rows_done, 1)
            act.copy(u_rows[0:15, 0], ps[0:15, 4, 0:256]).then_inc(rows_ready, 1)
            act.copy(u_rows[0:TS, 1], ps[0:TS, 5, 0:256]).then_inc(rows_ready, 1)

        def act_head(act, i):
            act.wait_ge(q_done, i + 1)
            for c in range(2):
                act.copy(halves(qT[0:EC, c]), banks(2 * c, EC)).then_inc(qT_ready, 1)
            act.wait_ge(step_done, STEP_HEADS + 1 + i * 2)
            for c in range(2):
                act.mul(halves(kT[0:EC, c]), banks(4 + 2 * c, EC), DH ** -0.5).then_inc(kT_ready, 1)
            act.wait_ge(v_done, i + 1)
            act.copy(vtok[:, 0:4].rearrange("p (b t) d -> p b (t d)", b=2), ps[:, 0:2, 0:2 * DH]).then_inc(v_ready, 1)
            act.copy(vtok[0:TS, 4], ps[0:TS, 2, 0:DH]).then_inc(v_ready, 1)
            act.wait_ge(step_done, STEP_HEADS + 2 + i * 2)
            for c in range(2):
                act.activation(halves(ogT[0:EC, c]), banks(4 + 2 * c, EC), ACT.Sigmoid).then_inc(og_ready, 1)
            for j in range(4):
                act.wait_ge(warg_ready, i * 4 + j + 1)
                act.activation(wt[:, j, 128 * j:SEQ], wt[:, j, 128 * j:SEQ], ACT.Exp, scale=-1.0).then_inc(w_ready, 1)
            act.wait_ge(mrow_done, i + 1)
            act.activation(em, ps[0:EC, 3, :], ACT.Exp, scale=-1.0).then_inc(em_ready, 1)
            act.wait_ge(small_ready, i + 1)
            act.activation(em_s[0:EC], small[0:EC, 64:96], ACT.Exp, scale=-1.0).then_inc(em_ready, 1)
            act.wait_ge(wsarg_ready, i + 1)
            act.activation(wts[0:TS], wts[0:TS], ACT.Exp, scale=-1.0).then_inc(ws_ready, 1)
            act.wait_ge(cp_done, i + 1)
            act.wait_ge(c_in, i * (16 * NB) + 16 * NB)
            act.copy(c_new_p[0:EC], ps[0:EC, 5, 0:2 * DH].rearrange("p (e d) -> p e d", e=2)).then_inc(cp_ready, 1)
            act.copy(n_new_p[0:1], ps[0:1, 6, 0:DH]).then_inc(cp_ready, 1)
            for b in range(NB):
                act.wait_ge(ct_done, i * NB + b + 1)
                if b >= 2:
                    act.wait_ge(cn_done, i * NB + b - 1)
                act.copy(cT[0:EC, b % 2], ps[0:EC, 4 + b % 2, 0:2 * DH].rearrange("p (e d) -> p e d", e=2)
                         ).then_inc(cT_ready, 1)

        def dve_even(dve, C):
            dve.wait_ge(e0_done, 1)
            dve.wait_ge(ein, 80)
            dve.tensor_scalar(halves(g_i[0:4]), banks(4, 4), b_i[0:4], None, ALU.add).then_inc(gf_ready, 1)
            dve.tensor_scalar(halves(g_f[0:4]), banks(6, 4), b_f[0:4], None, ALU.add).then_inc(gf_ready, 1)
            dve.wait_ge(gf_ready, 2)
            dve.scalar_tensor_tensor(out=g_x[0:4], in0=g_f[0:4], scalar=-1.0, in1=g_f[0:4],
                                     op0=ALU.mult, op1=ALU.min).then_inc(gf_ready, 1)
            dve.wait_ge(gl_ready, 2)
            C.after(dve.scalar_tensor_tensor(out=g_f[0:4], in0=g_f[0:4], scalar=0.0, in1=g_l[0:4],
                                             op0=ALU.min, op1=ALU.subtract))
            fs, bs = (v[0:4, SEQ:T].rearrange("p (b t) -> p b t", b=NB) for v in (g_f, g_e))
            C.after(dve.memset(ones_row, 1.0))
            C.after(dve.tensor_tensor_scan(g_e[0:4, 0:SEQ], ones_row, g_f[0:4, 0:SEQ], 0.0, ALU.mult, ALU.add))
            C.after(dve.tensor_copy(bs[:, :, 0], fs[:, :, 0]))
            for t in range(1, NT):
                C.after(dve.tensor_tensor(bs[:, :, t], bs[:, :, t - 1], fs[:, :, t], ALU.add))
            C.after(dve.tensor_tensor(g_a[0:4], g_i[0:4], g_e[0:4], ALU.subtract))
            M, m, ga = rows[0:4, 0:T], rows[0:4, T:2 * T], rows[0:4, 2 * T:2 * T + TS]
            Ms, as_ = (v.rearrange("p (b t) -> p b t", b=NB) for v in (M[:, SEQ:T], g_a[0:4, SEQ:T]))
            C.after(dve.tensor_tensor_scan(M[:, 0:SEQ], g_a[0:4, 0:SEQ], g_a[0:4, 0:SEQ], 0.0, ALU.max, ALU.max))
            C.after(dve.tensor_tensor(Ms[:, :, 0], m0[0:4], as_[:, :, 0], ALU.max))
            for t in range(1, NT):
                C.after(dve.tensor_tensor(Ms[:, :, t], Ms[:, :, t - 1], as_[:, :, t], ALU.max))
            C.after(dve.tensor_tensor(m, g_e[0:4], M, ALU.add))
            dve.tensor_copy(m_out[0:4], rows[0:4, T + SEQ + 3:2 * T:4]).then_inc(mout_ready, 1)
            for t in range(NT):
                dve.tensor_tensor(ga.rearrange("p (b t) -> p b t", b=NB)[:, :, t], m0[0:4], Ms[:, :, t], ALU.subtract)
            dve.tensor_tensor(rows[0:4, 2 * T + TS:ROW], m0[0:4], Ms[:, :, 3], ALU.subtract)
            dve.tensor_scalar(g_wk[0:4, 0:SEQ], g_a[0:4, 0:SEQ], M[:, SEQ - 1:SEQ], None, ALU.subtract).then_inc(wk_arg, 1)
            dve.tensor_tensor(g_wk[0:4, SEQ:T].rearrange("p (b t) -> p b t", b=NB), as_,
                              Ms[:, :, 3].unsqueeze(2).broadcast_to([4, NB, NT]), ALU.subtract).then_inc(wk_arg, 1)
            dve.wait_ge(cols_flip, 1)
            dve.tensor_copy(acol.rearrange("p t h -> p (t h)")[:, 0:16], ps[:, 6, 0:16])
            dve.tensor_copy(acol[0:TS, 4], ps[0:TS, 6, 16:20])
            dve.tensor_copy(wkcol.rearrange("p t h -> p (t h)")[:, 0:16], ps[:, 6, 32:48]).then_inc(cols_ready, 1)
            dve.tensor_copy(wkcol[0:TS, 4], ps[0:TS, 6, 48:52])
            dve.tensor_copy(dec_b[0:NB], ps[0:NB, 6, 64:68]).then_inc(cols_ready, 1)
            dve.wait_ge(cols_ready, 2)
            dve.sem_inc(head_free, 1)
            per = 21
            with dve.Fori(0, H4) as i:
                C.loop(i, per, lambda: dve_head(dve, C, i))
            C.skip(per * (H4 - 1))
            dve.wait_ge(ypool_ready, 2)
            dve.wait_ge(rows_ready, 2)
            dve.sem_inc(down_free, 2)
            dve_add(dve, 1, STEP_EOUT, 1, 1.0)

        def dve_head(dve, C, i):
            late, late_s = const("late"), const("late_s", TS)
            dve.tensor_scalar(rows_h[0:4], rows[0:4], head4[:, ds(i, 1)], None, ALU.mult).then_inc(rowh_ready, 1)
            dve.wait_ge(mb_done, i + 1)
            for j in range(4):
                a = acol[:, j, ds(i, 1)]
                dve_w = dve.scalar_tensor_tensor(out=wt[:, j, 128 * j:128 * j + 128], in0=ps[:, 3, 128 * j:128 * j + 128],
                                                 scalar=a, in1=late, op0=ALU.subtract, op1=ALU.max)
                if j < 3:
                    dve_w = dve.tensor_scalar(wt[:, j, 128 * j + 128:SEQ], ps[:, 3, 128 * j + 128:SEQ], a, 0.0,
                                              ALU.subtract, ALU.max)
                dve_w.then_inc(warg_ready, 1)
            dve.wait_ge(kflip_done, i + 1)
            for t in range(KTILES):
                r = tok_tile(t)
                dve.tensor_scalar(kw[0:r, t], ps[0:r, t // 2, DH * (t % 2):DH * (t % 2) + DH],
                                  wkcol[0:r, t, ds(i, 1)], None, ALU.mult).then_inc(kw_ready, 1)
            for j in range(4):
                dve.wait_ge(w_ready, i * 4 + j + 1)
                dve.wait_ge(s_done, i * 4 + j + 1)
                dve.tensor_tensor(wt[:, j, 128 * j:SEQ], wt[:, j, 128 * j:SEQ], ps[:, 4 + j, 128 * j:SEQ],
                                  ALU.mult).then_inc(sT_ready, 1)
            dve.wait_ge(small_done, i + 1)
            C.after(dve.tensor_copy(small[0:EC, 0:104], ps[0:EC, 0, 0:104]))
            dve.tensor_copy(small[0:TS, 128:160], ps[0:TS, 0, 128:160]).then_inc(small_ready, 1)
            dve.wait_ge(small_ready, i + 1)
            dve.scalar_tensor_tensor(out=wts[0:TS], in0=small[0:TS, 0:32], scalar=acol[0:TS, 4, ds(i, 1)], in1=late_s,
                                     op0=ALU.subtract, op1=ALU.max).then_inc(wsarg_ready, 1)
            dve.wait_ge(kw_ready, i * 6 + 5)
            dve.tensor_tensor(kwb[0:TS], kw[0:TS, 4].unsqueeze(1).broadcast_to([TS, NB, DH]),
                              const("of_batch", TS).unsqueeze(2).broadcast_to([TS, NB, DH]), ALU.mult
                              ).then_inc(kw_ready, 1)
            for c in range(2):
                q = dve.tensor_tensor(qn[0:EC, c].rearrange("p (b t) -> p b t", b=NB),
                                      qT[0:EC, c, SEQ:T].rearrange("p (b t) -> p b t", b=NB),
                                      nT[0:EC, c, ds(i, 1)].rearrange("p h b -> p (h b)").unsqueeze(2)
                                      .broadcast_to([EC, NB, NT]), ALU.mult)
                if c == 1:
                    q.then_inc(qn_ready, 1)
                else:
                    C.after(q)
            dve.wait_ge(ws_ready, i * 2 + 1)
            dve.tensor_tensor(wts[0:TS], wts[0:TS], small[0:TS, 128:160], ALU.mult).then_inc(ws_ready, 1)
            dve.wait_ge(em_ready, i * 2 + 1)
            dve.wait_ge(den_done, i + 1)
            C.after(dve.tensor_tensor(rden, ps[0:EC, 4, :], em, ALU.max))
            C.after(dve.scalar_tensor_tensor(out=rden, in0=ps[0:EC, 4, :], scalar=-1.0, in1=rden, op0=ALU.mult, op1=ALU.max))
            C.after(dve.reciprocal(rden, rden))
            for c in range(2):
                y = yml[0:EC, ds(i * 2 + c, 1), 0:SEQ].rearrange("p a t -> p (a t)")
                C.after(dve.tensor_tensor(ogT[0:EC, c, 0:SEQ], ogT[0:EC, c, 0:SEQ], rden, ALU.mult))
                dve.tensor_tensor(y, ogT[0:EC, c, 0:SEQ], ps[0:EC, 1 + c, :], ALU.mult).then_inc(yp_ready, 1)
            for b in range(NB):
                dve.wait_ge(cn_done, i * NB + b + 1)
                dve.scalar_tensor_tensor(out=cS[0:EC, b], in0=cS[0:EC, b], scalar=dec_s[0:EC, b:b + 1],
                                         in1=ps[0:EC, 6 + b % 2, 0:2 * DH].rearrange("p (e d) -> p e d", e=2),
                                         op0=ALU.mult, op1=ALU.add).then_inc(cn_ready, 1)
            dve.wait_ge(sfin_done, i + 1)
            nh = nS[0:NB, ds(i, 1)].rearrange("p a d -> p (a d)")
            C.after(dve.scalar_tensor_tensor(out=nN[0:NB, ds(i, 1)].rearrange("p a d -> p (a d)"), in0=nh,
                                             scalar=dec_b[0:NB, ds(i, 1)], in1=ps[0:NB, 1, 0:DH],
                                             op0=ALU.mult, op1=ALU.add))
            C.after(dve.tensor_tensor(den_s[0:EC], a_s[0:EC], ps[0:EC, 0, 256:288], ALU.mult))
            C.after(dve.tensor_tensor(den_s[0:EC], den_s[0:EC], ps[0:EC, 0, 224:256], ALU.add))
            dve.wait_ge(em_ready, i * 2 + 2)
            C.after(dve.tensor_tensor(em_s[0:EC], em_s[0:EC], den_s[0:EC], ALU.max))
            C.after(dve.scalar_tensor_tensor(out=den_s[0:EC], in0=den_s[0:EC], scalar=-1.0, in1=em_s[0:EC],
                                             op0=ALU.mult, op1=ALU.max))
            C.after(dve.reciprocal(den_s[0:EC], den_s[0:EC]))
            for c in range(2):
                u = acc_s[0:EC, c]
                C.after(dve.tensor_tensor(u, a_s[0:EC], ps[0:EC, 0, 288 + 32 * c:320 + 32 * c], ALU.mult))
                C.after(dve.tensor_tensor(u, u, ps[0:EC, 0, 160 + 32 * c:192 + 32 * c], ALU.add))
                C.after(dve.tensor_tensor(u, u, den_s[0:EC], ALU.mult))
                y = yml[0:EC, ds(i * 2 + c, 1), SEQ:T].rearrange("p a t -> p (a t)")
                C.after(dve.tensor_tensor(y, u, ogT[0:EC, c, SEQ:T], ALU.mult))
            dve.wait_ge(cn_ready, i * NB + NB)
            dve.sem_inc(head_free, 1)

        ones_row = ns[0:4, 2 * T:2 * T + SEQ]

        A, G = Arena(arena_t, A_SIZE), Arena(pages_t, G_SIZE)
        kvtok = A.take(KTILES, 6 * 128)
        ktS, ktW = A.take(T), A.take(T)
        gts = A.take(KTILES, 3 * NH)
        yconv = A.take(2, T)
        oT = A.take(GQ, T)
        qB = A.take(NB, 64)
        cmp_a = A.take(2, 9)
        cmp_bd = A.take(2, 128)
        k_bias, v_bias = A.take(1), A.take(128)
        kcT_p, vc_p = A.take(32), A.take(128)
        imp, score, score2, top8 = A.take(132), A.take(NBLK), A.take(NBLK), A.take(8)
        blk_add = A.take(NBLK)
        mx, rs, gs, mx_p, rs_p, coef = A.take(3), A.take(3), A.take(3), A.take(2, 2), A.take(2, 2), A.take(2, 2)
        A_TAIL = A.at
        qTp = A.take(2, SEQ)
        ptS, ptW = A.take(SEQ), A.take(SEQ)
        mc, o1 = A.take(2, 4), A.take(HD)
        sP = ns[:, 0:4 * SEQ].rearrange("p (u b k) -> p u b k", u=2, b=2)
        sc_p = ns[:, 4 * SEQ:4 * SEQ + 2 * 128].rearrange("p (g j n) -> p g j n", g=2, j=4)
        half_ring = lambda i: ring[:, i, SLOT // 2:SLOT]
        otok = [half_ring(i)[:, 0:2 * 6 * 128].rearrange("p (j n) -> p j n", j=2) for i in range(2)]
        ptC = half_ring(0)[0:32, 1536:2048].rearrange("p (j q) -> p j q", j=4)
        ptC2 = half_ring(1)[0:32, 1536:2048].rearrange("p (j q) -> p j q", j=4)
        A2 = Arena(arena_t, A_SIZE)
        A2.at = A_TAIL
        qP, eP, g36, pcS = A2.take(2, 64), A2.take(128), A2.take(NH, 3), A2.take(128)
        o_s = A2.take(128)
        hflat = h[:, :, :].rearrange("p c t -> p (c t)")
        H = Arena(hflat, NK * T)
        pT = H.take(23, 128)
        preS, kcS, vcS = H.take(2, 256), H.take(2, 128), H.take(2, 128)
        sS, sW = ns[:, 0:PAST + TS], ns[:, PAST + TS:PAST + TS + 512 + TS]
        ktc = [half_ring(0)[:, 1024 * i:1024 * i + 1024].rearrange("p (b k) -> p b k", b=2) for i in range(2)]
        pages = pages_t[:, :].rearrange("p (b g n) -> p b g n", b=2, g=NPG)
        cvp, cvs = G.take(2, 2 + SEQ), G.take(2, NB, 2 + NT)
        bgT, cgT = G.take(2, T), G.take(2, T)
        cv_t = G.take(T)
        cs_rows, c_rows = G.take(256), G.take(2, 256)
        pre_p = G.take(64)

        cm_in, pt_in = sem("cm_in"), sem("pt_in")
        kv_ready, gt_ready, bg_ready, cg_done, cg_ready = (sem(n) for n in (
            "kv_ready", "gt_ready", "bg_ready", "cg_done", "cg_ready"))
        cu_ready, conv_ready = sem("cu_ready"), sem("conv_ready")
        ktf_done, kt_ready = sem("ktf_done"), sem("kt_ready")
        pre_done, pre_ready, kc_done, kc_ready, vc_ready = (sem(n) for n in (
            "pre_done", "pre_ready", "kc_done", "kc_ready", "vc_ready"))
        qp_ready, scmp_done, scmp_neg, scmp_exp, scmp_ready, tcmp_done, ptc_ready = (sem(n) for n in (
            "qp_ready", "scmp_done", "scmp_neg", "scmp_exp", "scmp_ready", "tcmp_done", "ptc_ready"))
        sc_done, sc_free, neg_ready, exp_ready, t_done = (sem(n) for n in (
            "sc_done", "sc_free", "neg_ready", "exp_ready", "t_done"))
        pts_ready, ptw_ready, pv_done, o_used = sem("pts_ready"), sem("ptw_ready"), sem("pv_done"), sem("o_used")
        chunk_free, of_done, of_ready = sem("chunk_free"), sem("of_done"), sem("of_ready")
        pages_in, pages_used, pair_free = sem("pages_in"), sem("pages_used"), sem("pair_free")
        qP_ready = sem("qP_ready")
        scs_done, negc_ready, expc_ready, pc_ready, imp_done = (sem(n) for n in (
            "scs_done", "negc_ready", "expc_ready", "pc_ready", "imp_done"))
        tk_done, ktc_ready, sk_done, sk_ready, new_done = (sem(n) for n in (
            "tk_done", "ktc_ready", "sk_done", "sk_ready", "new_done"))
        negs_ready, exps_ready, tp_done, pTa_ready, pTv_ready = (sem(n) for n in (
            "negs_ready", "exps_ready", "tp_done", "pTa_ready", "pTv_ready"))
        pvs_done, os_ready, ot_done = sem("pvs_done"), sem("os_ready"), sem("ot_done")

        def load_odd(sp):
            w = w_in_odd[0].rearrange("(k p) n -> p k n", p=128)
            for u in range(2):
                n = STEP_ODD + u
                v = slot(n, NK, 384)
                a = 768 + 384 * u
                load(sp, n, [(v[:, :, 0:192], w[:, :, a:a + 192]), (v[:, :, 192:384], w[:, :, a + 192:a + 384])])
            n = STEP_ODD + 2
            v = slot(n, NK, 292)
            load(sp, n, [(v[:, :, 0:36], w[:, :, 1536:1572]), (v[:, :, 36:292], w[:, :, 1572:1828])])
            n = STEP_ODD + 3
            v = slot(n, NK, 512)
            load(sp, n, [(v[:, :, 0:256], w[:, :, 1828:2084]), (v[:, :, 256:512], w[:, :, 2084:2340])])
            with sp.Fori(0, 3) as i:
                for u in range(2):
                    n = STEP_Q + u
                    v = slot(n, NK, 128)
                    load(sp, n, [(v[:, :, 64 * g:64 * g + 64], w[:, :, ds(i * 128 + 64 * u + 384 * g, 64)])
                                 for g in range(2)], i * 2)
            wo = w_out_odd[0]
            wh = wo[0:768].rearrange("(g i p) n -> g p i n", g=2, i=GQ)
            with sp.Fori(0, 2) as i:
                for u in range(2):
                    n = STEP_OOUT + u
                    v = slot(n, 8, 256)
                    at = i * 512 + 256 * u
                    load(sp, n, [(v[64 * g:64 * g + 64, 0:GQ], wh[g][:, :, ds(at, 256)]) for g in range(2)], i * 2)
                    sp.dma_start(v[:, GQ:8], wo[768:D].rearrange("(k p) n -> p k n", p=128)[:, :, ds(at, 256)]
                                 ).then_inc(oconv_in[n % 2], 16)

        oconv_in = [sem("oconv_in_0"), sem("oconv_in_1")]

        def pool_odd(po, C):
            po.wait_ge(h_ready, NK * 5)
            for z in (cmp_a[:, :, :], cmp_bd[:, :, :], qB[:, :, :], imp[:, :], cvp[:, :, 0:2]):
                mz = po.memset(z, 0.0)
                mz.then_inc(zeroed, 1)
            po.wait_ge(zeroed, 7)
            n = 0
            for kv in range(2):
                for c in range(9):
                    lo, hi = max(0, 16 * (c - 1)), min(128, 16 * (c - 1) + 32)
                    j = lo - 16 * (c - 1)
                    po.dma_start(cmp_a[lo:hi, kv, c:c + 1],
                                 cmp_pos_w[0, kv, j:j + hi - lo].rearrange("(j o) -> j o", o=1)).then_inc(cm_in, 16)
                for g in range(2):
                    r = slice(64 * g, 64 * g + 64)
                    po.dma_start(cmp_bd[r, kv, r], cmp_w[0, kv]).then_inc(cm_in, 16)
            for g in range(2):
                r = slice(64 * g, 64 * g + 64)
                po.dma_start(k_bias[r], cmp_b[0, 0].rearrange("(d o) -> d o", o=1)).then_inc(cm_in, 16)
                po.dma_start(v_bias[:, r], cmp_b[0, 1:2, :].broadcast_to([128, HD])).then_inc(cm_in, 16)
            po.dma_start(cs_rows[0:2 * NB], state_conv[0].rearrange("b j n -> (b j) n")).then_inc(cm_in, 16)
            po.dma_start(pt[:, :], page_table.rearrange("(o b) g -> o (b g)", o=1)).then_inc(pt_in, 16)
            po.dma_start(win_s[0, :, 0:508].rearrange("b k r g d -> b k (r g d)"),
                         state_win_kv[0, :, 4:512].rearrange("b k r g d -> b k (r g d)")).then_inc(stored, 16)
            po.wait_ge(kv_ready, 10)
            po.dma_start(kv_rows_p[0, 0].rearrange("(t p) r g d -> p t (r g d)", p=128), kvtok[:, 0:4, 0:512]).then_inc(stored, 16)
            po.dma_start(kv_rows_s[0].rearrange("b t r g d -> (b t) (r g d)"), kvtok[0:TS, 4, 0:512]).then_inc(stored, 16)
            po.dma_start(win_p[0, 0].rearrange("(t p) r g d -> p t (r g d)", p=128), kvtok[:, 0:4, 512:768]).then_inc(stored, 16)
            for b in range(NB):
                po.dma_start(win_s[0, b, 508:512].rearrange("k r g d -> k (r g d)"),
                             kvtok[NT * b:NT * b + NT, 4, 512:768]).then_inc(stored, 16)
            n_stored[0] += 4 + NB
            po.wait_ge(cu_ready, 2)
            po.wait_ge(prefix_ready, 3)
            po.wait_ge(bg_ready, 2)
            for c in range(2):
                tap = lambda j: vecs[:, V_CONV + 2 * j + c:V_CONV + 2 * j + c + 1]
                y, t = yconv[:, c], cv_t
                for o, tmp, e, w in ((y[:, 0:SEQ], t[:, 0:SEQ], cvp[:, c], SEQ),
                                     (y[:, SEQ:T].rearrange("p (b t) -> p b t", b=NB),
                                      t[:, SEQ:T].rearrange("p (b t) -> p b t", b=NB), cvs[:, c], NT)):
                    C.after(po.tensor_scalar(o, e[..., 0:w], tap(0), None, ALU.mult))
                    for j in (1, 2):
                        C.after(po.tensor_scalar(tmp, e[..., j:j + w], tap(j), None, ALU.mult))
                        C.after(po.tensor_tensor(o, o, tmp, ALU.add))
                po.tensor_tensor(y, y, bgT[:, c], ALU.mult).then_inc(conv_ready, 1)
            po.wait_ge(rows_ready, 4)
            po.dma_start(conv_p[0, 0], c_rows[0:2, 0]).then_inc(crow_stored, 16)
            po.dma_start(conv_s[0].rearrange("b j n -> (b j) n"), c_rows[0:2 * NB, 1]).then_inc(crow_stored, 16)
            po.wait_ge(crow_stored, 32)
            po.wait_ge(conv_ready, 2)
            po.wait_ge(pre_ready, 1)
            po.wait_ge(kc_ready, 1)
            po.wait_ge(vc_ready, 1)
            po.wait_ge(pt_in, 16)
            with po.Fori(0, NB // 2) as i:
                po.wait_ge(pages_used, i + 1)
                for b in range(2):
                    for g in range(NPG):
                        page = po.value_load(pt[0:1, ds(i * (2 * NPG) + (b * NPG + g), 1)], min_val=0,
                                             max_val=cache_nsa_kv.shape[1] - 1)
                        po.dma_start(pages[:, b, g], cache_nsa_kv[0, ds(page, 1)].rearrange("a k r g d -> (a k) (r g d)")
                                     ).then_inc(pages_in, 16)
                po.wait_ge(win_free, i + 1)
                po.sem_inc(waited, 1)
                for b in range(2):
                    po.dma_start(wst_[:, b], state_win_kv[0, ds(i * 2 + b, 1)].rearrange(
                        "a (t p) r g d -> p (a t) (r g d)", p=128)).then_inc(pages_in, 16)

        crow_stored, win_free = sem("crow_stored"), sem("win_free")
        wst_ = half_ring(1).rearrange("p (b t n) -> p b t n", b=2, t=4)
        PAGES = 16 * (2 * NPG + 2)

        def compress(pe, b, at, src, rows_pages, kv, cols):
            pe.matmul(ps[:, b, at:at + cols], ident, zeros[:, 0:cols], start=True, stop=False, skip_group_check=True)
            for p in range(rows_pages):
                lo = 1 if p == 0 else 0
                hi = 8 if p == rows_pages - 1 else 9
                mm = pe.matmul(ps[:, b, at + 8 * p - 1 + lo:at + 8 * p - 1 + hi], src(p), cmp_a[:, kv, lo:hi],
                               start=False, stop=(p == rows_pages - 1), skip_group_check=True)
            return mm

        zeros = const("zeros")

        def pe_odd(pe):
            pe.wait_ge(h_ready, NK * 5)
            for u in range(2):
                n = STEP_ODD + u
                use_step(pe, n)
                w = slot(n, NK, 384)
                for t in range(KTILES):
                    if u == 1 and t == 3:
                        pe.wait_ge(kv_ready, 2)
                    mm = project_tok(pe, ps[0:tok_tile(t), (5 * u + t) % 8, 0:384], w, 0, 384, t)
                mm.then_inc(step_done, 1)
            pe.wait_ge(kv_ready, 10)
            n = STEP_ODD + 2
            use_step(pe, n)
            w = slot(n, NK, 292)
            for t in range(KTILES):
                project_tok(pe, ps[0:tok_tile(t), 7, 36 * t:36 * t + 36], w, 0, 36, t)
            for c in range(2):
                mm = project(pe, w, 36 + 128 * c, 128, 2 * c)
            mm.then_inc(step_done, 1)
            n = STEP_ODD + 3
            use_step(pe, n)
            w = slot(n, NK, 512)
            project(pe, w, 0, 128, 4)
            pe.wait_ge(gt_ready, 1)
            project(pe, w, 128, 128, 6).then_inc(cg_done, 1)
            for c in range(2):
                pe.wait_ge(bg_ready, c + 1)
                mm = project(pe, w, 256 + 128 * c, 128, 2 * c)
            mm.then_inc(step_done, 1)
            pe.wait_ge(cg_ready, 2)
            for b, at in ((4, 256), (6, 512)):
                for t in range(4):
                    flip(pe, ps[:, b, 128 * t:128 * t + 128], kvtok[:, t, at:at + 128])
                mm = flip(pe, ps[:, b + 1, 0:TS], kvtok[0:TS, 4, at:at + 128])
            mm.then_inc(ktf_done, 1)
            pe.wait_ge(cu_ready, 2)
            pe.wait_ge(cm_in, 16 * 27)
            for c in range(2):
                mm = flip(pe, ps[:, 0, 16 * c:16 * c + 16], cs_rows[0:2 * NB, 128 * c:128 * c + 128])
            mm.then_inc(prefix_flip, 1)
            for kv in range(2):
                mm = compress(pe, 1, 32 * kv, lambda p: kvtok[:, p, 128 * kv:128 * kv + 128], 4, kv, 32)
            mm.then_inc(pre_done, 1)
            pe.wait_ge(kt_ready, 4)
            for c in range(2):
                flip(pe, ps[0:2, 4, 128 * c:128 * c + 128], cvp[:, c, SEQ:SEQ + 2])
            for c in range(2):
                mm = flip(pe, ps[0:2 * NB, 5, 128 * c:128 * c + 128], cv_last[:, c, :])
            mm.then_inc(rows_done, 1)
            pe.wait_ge(pre_ready, 1)
            pe.matmul(ps[:, 2, 0:32], cmp_bd[:, 0], pre_p[:, 0:32], start=True, stop=True)
            pe.matmul(ps[0:32, 3, 0:128], pre_p[:, 32:64], cmp_bd[:, 1], start=True, stop=True).then_inc(kc_done, 1)
            pe.wait_ge(rows_ready, 4)
            pe.wait_ge(kc_ready, 1)
            pe.wait_ge(vc_ready, 1)
            with pe.Fori(0, 3) as i:
                for u in range(2):
                    pe_queries(pe, i, u)
            pe.wait_ge(o_used, 49)
            for j in range(4):
                if j >= 2:
                    pe.wait_ge(of_ready, j - 1)
                for c in range(GQ):
                    mm = flip(pe, ps[:, 2 * (j % 2) + c // 4, 128 * (c % 4):128 * (c % 4) + 128],
                              otok[j // 2][:, j % 2, 128 * c:128 * c + 128])
                mm.then_inc(of_done, 1)
            pe.wait_ge(of_ready, 4)
            with pe.Fori(0, NB // 2) as i:
                pe_pair(pe, i)
            pe.wait_ge(pair_free, NB // 2 + 1)
            pe.wait_ge(conv_ready, 2)
            rhs = [(128, oT[:, c]) for c in range(GQ)] + [(128, yconv[:, c]) for c in range(2)]
            with pe.Fori(0, 2) as i:
                for u in range(2):
                    pe.wait_ge(oconv_in[(STEP_OOUT + u) % 2], i * 16 + 16)
                    pe_out(pe, 4, STEP_OOUT, u, i, rhs)

        cv_last = G.take(2, 2 * NB)

        def pe_queries(pe, i, u):
            n = STEP_Q + u
            use_step(pe, n, i * 32)
            w = slot(n, NK, 128)
            pe.wait_ge(pts_ready, i * 16 + 8 * u + 1)
            pe.wait_ge(ptw_ready, i * 16 + 8 * u + 1)
            project(pe, w, 0, 128, 4).then_inc(step_done, 1)
            pe.wait_ge(qp_ready, i * 8 + 4 * u + 4)
            pe.wait_ge(o_used, i * 16 + 8 * u + 1)
            q = lambda g, j: qTp[64 * g:64 * g + 64, u, 128 * j:128 * j + 128]
            for g in range(2):
                for j in range(4):
                    mm = pe.matmul(ps[:, 6 + g, 32 * j:32 * j + 32], q(g, j), kcT_p[64 * g:64 * g + 64, :],
                                   start=True, stop=True)
                mm.then_inc(scmp_done, 1)

            def scores(k):
                g, j = k // 4, k % 4
                pe.wait_ge(sc_free, i * 16 + 8 * u + k + 1)
                pe.matmul(ps[:, 2 * (k % 2), 0:128 * j + 128], q(g, j), ktS[64 * g:64 * g + 64, 0:128 * j + 128],
                          start=True, stop=True)
                pe.matmul(ps[:, 2 * (k % 2) + 1, 0:128 * j + 128], q(g, j), ktW[64 * g:64 * g + 64, 0:128 * j + 128],
                          start=True, stop=True).then_inc(sc_done, 1)

            scores(0)
            for g in range(2):
                pe.wait_ge(scmp_ready, i * 4 + 2 * u + g + 1)
                for j in range(4):
                    mm = pe.matmul(ps[0:32, 4 + g, 128 * j:128 * j + 128], sc_p[:, g, j, :], ident, start=True, stop=True)
                mm.then_inc(tcmp_done, 1)
            for k in range(8):
                g, j = k // 4, k % 4
                if k < 7:
                    scores(k + 1)
                pe.wait_ge(exp_ready, i * 16 + 8 * u + k + 1)
                if k == 0:
                    pe.wait_ge(ptc_ready, i * 4 + 2 * u + 2)
                pe.wait_ge(pts_ready, i * 16 + 8 * u + k + 1)
                pe.wait_ge(ptw_ready, i * 16 + 8 * u + k + 1)
                for br in range(2):
                    for t in range(j + 1):
                        mm = pe.transpose(ps[:, 4 + br, 128 * t:128 * t + 128], sP[:, k % 2, br, 128 * t:128 * t + 128], ident)
                mm.then_inc(t_done, 1)
                o = 6 + k % 2
                if k >= 1:
                    pe.wait_ge(o_used, i * 16 + 8 * u + k)
                pe.wait_ge(pts_ready, i * 16 + 8 * u + k + 2)
                pe.wait_ge(ptw_ready, i * 16 + 8 * u + k + 2)
                pe.matmul(ps[:, o, 0:HD], (ptC, ptC2)[g][:, j, :], vc_p[0:32, 64 * g:64 * g + 64], start=True, stop=True)
                for br, p, at in ((0, ptS, 384), (1, ptW, 640)):
                    for t in range(j + 1):
                        mm = pe.matmul(ps[:, o, HD * (br + 1):HD * (br + 2)], p[:, 128 * t:128 * t + 128],
                                       kvtok[:, t, at + 64 * g:at + 64 * g + 64], start=(t == 0), stop=(t == j))
                mm.then_inc(pv_done, 1)

        def pe_pair(pe, i):
            row = lambda b: slice(64 * b, 64 * b + 64)
            pe.wait_ge(pair_free, i + 1)
            pe.wait_ge(pages_in, i * PAGES + PAGES)
            for kv in range(2):
                for b in range(2):
                    mm = compress(pe, kv, 128 * b, lambda p: pages[:, b, p, 128 * kv:128 * kv + 128], NPG, kv, 128)
            mm.then_inc(pre_done, 1)

            def flip_keys(c):
                if c == 0:
                    pe.wait_ge(pre_ready, i + 2)
                if c >= 2:
                    pe.wait_ge(ktc_ready, i * 5 + c - 1)
                for b in range(2):
                    for t in range(4):
                        src = pages[:, b, 4 * c + t, 256:384] if c < 4 else wst_[:, b, t, 0:128]
                        mm = pe.transpose(ps[:, (0, 6)[c % 2] + b, 128 * t:128 * t + 128], src, ident)
                mm.then_inc(tk_done, 1)

            pe.wait_ge(pre_ready, i + 2)
            pe.matmul(ps[:, 2, 0:256], cmp_bd[:, 0], preS[:, 0, :], start=True, stop=True)
            for b in range(2):
                mm = pe.matmul(ps[0:NCS, 3, 128 * b:128 * b + 128], preS[:, 1, 128 * b:128 * b + NCS], cmp_bd[:, 1],
                               start=True, stop=True)
            mm.then_inc(kc_done, 1)
            flip_keys(0)
            pe.wait_ge(qP_ready, i * 2 + 2)
            pe.wait_ge(kc_ready, i + 2)
            for b in range(2):
                mm = pe.matmul(ps[row(b), 4, 0:NCS], qP[:, b], kcS[:, b, 0:NCS], start=True, stop=True)
            mm.then_inc(scs_done, 1)
            pe.wait_ge(vc_ready, i + 2)
            for c in range(5):
                if c < 4:
                    flip_keys(c + 1)
                pe.wait_ge(ktc_ready, i * 5 + c + 1)
                if c >= 2:
                    pe.wait_ge(sk_ready, i * 5 + c - 1)
                for b in range(2):
                    mm = pe.matmul(ps[row(b), 2 + c % 2, :], qP[:, b], ktc[c % 2][:, b], start=True, stop=True)
                mm.then_inc(sk_done, 1)
            for b in range(2):
                pe.matmul(ps[row(b), 5, 0:TS], qP[:, b], ktS[:, SEQ:T], start=True, stop=True)
                pe.matmul(ps[row(b), 5, TS:2 * TS], qP[:, b], ktW[:, SEQ:T], start=True, stop=True)
            pe.matmul(ps[:, 5, 64:64 + 3 * NH], eP[0:TS, :], gts[0:TS, 4, :], start=True, stop=True).then_inc(new_done, 1)
            pe.wait_ge(pc_ready, i + 1)
            pe.matmul(ps[:, 4, 128:128 + NCS], const("same_query"), pcS[:, 0:NCS], start=True, stop=True).then_inc(imp_done, 1)
            pe.wait_ge(exps_ready, i * 2 + 2)
            for t in range(16):
                pe.transpose(ps[:, t // 4, 128 * (t % 4):128 * (t % 4) + 128], sS[:, 128 * t:128 * t + 128], ident)
            for t in range(4):
                pe.transpose(ps[:, 4, 128 * t:128 * t + 128], sW[:, 128 * t:128 * t + 128], ident)
            flip(pe, ps[0:TS, 5, 128:256], sS[:, PAST:PAST + TS])
            flip(pe, ps[0:TS, 5, 256:384], sW[:, 512:512 + TS])
            flip(pe, ps[0:NCS, 5, 0:128], pcS[:, 0:NCS]).then_inc(tp_done, 1)
            pe.wait_ge(pTa_ready, i * 3 + 3)
            pe.wait_ge(pTv_ready, i * 4 + 4)
            for b in range(2):
                pe.matmul(ps[row(b), 6, 0:128], pT[0:NCS, 20, row(b)], vcS[0:NCS, b], start=True, stop=True)
                for t in range(17):
                    lhs, rhs = (pT[:, t, row(b)], pages[:, b, t, 384:512]) if t < 16 else \
                        (pT[0:TS, 21, row(b)], kvtok[0:TS, 4, 384:512])
                    pe.matmul(ps[row(b), 6, 128:256], lhs, rhs, start=(t == 0), stop=(t == 16))
                for t in range(5):
                    lhs, rhs = (pT[:, 16 + t, row(b)], wst_[:, b, t, 128:256]) if t < 4 else \
                        (pT[0:TS, 22, row(b)], kvtok[0:TS, 4, 640:768])
                    mm = pe.matmul(ps[row(b), 6, 256:384], lhs, rhs, start=(t == 0), stop=(t == 4))
            mm.then_inc(pvs_done, 1)
            pe.wait_ge(os_ready, i + 1)
            pe.transpose(ps[:, 7, 0:128], o_s[:, :], ident).then_inc(ot_done, 1)

        def act_odd(act):
            for u in range(2):
                act.wait_ge(step_done, STEP_ODD + u + 1)
                for t in range(KTILES):
                    r = tok_tile(t)
                    act.copy(kvtok[0:r, t, 384 * u:384 * u + 384], ps[0:r, (5 * u + t) % 8, 0:384]).then_inc(kv_ready, 1)
            act.wait_ge(step_done, STEP_ODD + 3)
            act.activation(gts[:, 0:4].rearrange("p t n -> p (t n)"), ps[:, 7, 0:4 * 3 * NH], ACT.Sigmoid)
            act.activation(gts[0:TS, 4], ps[0:TS, 7, 4 * 3 * NH:5 * 3 * NH], ACT.Sigmoid).then_inc(gt_ready, 1)
            for c in range(2):
                act.copy(halves(bgT[:, c]), banks(2 * c)).then_inc(bg_ready, 1)
            act.wait_ge(cg_done, 1)
            for c in range(2):
                act.copy(halves(cgT[:, c]), banks(4 + 2 * c)).then_inc(cg_ready, 1)
            act.wait_ge(ktf_done, 1)
            for kt, b in ((ktS, 4), (ktW, 6)):
                act.copy(kt[:, 0:SEQ], ps[:, b, :]).then_inc(kt_ready, 1)
                act.copy(kt[:, SEQ:T], ps[:, b + 1, 0:TS]).then_inc(kt_ready, 1)
            act.wait_ge(prefix_flip, 3)
            act.copy(cvs[:, :, :, 0:2], ps[:, 0, 0:4 * NB].rearrange("p (c b j) -> p c b j", c=2, b=NB)).then_inc(prefix_ready, 1)
            act.wait_ge(pre_done, 1)
            act.copy(pre_p, ps[:, 1, 0:64]).then_inc(pre_ready, 1)
            act.wait_ge(rows_done, 2)
            act.copy(c_rows[0:2, 0], ps[0:2, 4, 0:256]).then_inc(rows_ready, 1)
            act.copy(c_rows[0:2 * NB, 1], ps[0:2 * NB, 5, 0:256]).then_inc(rows_ready, 1)
            act.wait_ge(kc_done, 1)
            act.wait_ge(cm_in, 16 * 27)
            act.activation(kcT_p, ps[:, 2, 0:32], ACT.Identity, bias=k_bias).then_inc(kc_ready, 1)
            act.wait_ge(zeroed, 7)
            with act.Fori(0, 3) as i:
                for u in range(2):
                    act_queries(act, i, u)
            for j in range(4):
                act.wait_ge(of_done, j + 1)
                act.copy(oT[:, 0:4, 128 * j:128 * j + 128],
                         ps[:, 2 * (j % 2), :].rearrange("p (c t) -> p c t", c=4))
                act.copy(oT[:, 4:6, 128 * j:128 * j + 128],
                         ps[:, 2 * (j % 2) + 1, 0:256].rearrange("p (c t) -> p c t", c=2)).then_inc(of_ready, 1)
            with act.Fori(0, NB // 2) as i:
                act_pair(act, i)

        def act_queries(act, i, u):
            s = HD ** -0.5
            act.wait_ge(step_done, STEP_Q + u + 1 + i * 2)
            act.mul(qTp[:, u, 0:HALF], ps[:, 4, 0:HALF], s).then_inc(qp_ready, 1)
            act.mul(qTp[:, u, HALF:SEQ], ps[:, 5, 0:SPLIT], s).then_inc(qp_ready, 1)
            for g in range(2):
                act.mul(qB[64 * g:64 * g + 64, :, ds(i * 8 + 32 * g + 4 * u, NT)],
                        ps[64 * g:64 * g + 64, 5, SPLIT:HALF].rearrange("p (b t) -> p b t", b=NB), s).then_inc(qp_ready, 1)
            for g in range(2):
                act.wait_ge(scmp_neg, i * 4 + 2 * u + g + 1)
                e = sc_p[:, g].rearrange("p j n -> p (j n)")
                act.activation(e, e, ACT.Exp).then_inc(scmp_exp, 1)

            def exps(k):
                n = 128 * (k % 4) + 128
                act.wait_ge(neg_ready, i * 16 + 8 * u + k + 1)
                for br in range(2):
                    e = sP[:, k % 2, br, 0:n]
                    ex = act.activation(e, e, ACT.Exp, bias=mx_p[:, k % 2, br:br + 1], accum_out=rs_p[:, k % 2, br:br + 1])
                ex.then_inc(exp_ready, 1)

            exps(0)
            for g in range(2):
                act.wait_ge(tcmp_done, i * 4 + 2 * u + g + 1)
                act.copy((ptC, ptC2)[g].rearrange("p j q -> p (j q)"), ps[0:32, 4 + g, :]).then_inc(ptc_ready, 1)
            for k in range(8):
                n = 128 * (k % 4) + 128
                act.wait_ge(t_done, i * 16 + 8 * u + k + 3)
                act.copy(ptS[:, 0:n], ps[:, 4, 0:n]).then_inc(pts_ready, 1)
                if k < 7:
                    exps(k + 1)

        def act_pair(act, i):
            act.wait_ge(pre_done, i + 2)
            act.copy(preS, ps[:, 0:2, 0:256]).then_inc(pre_ready, 1)
            act.wait_ge(kc_done, i + 2)
            act.activation(kcS.rearrange("p b n -> p (b n)"), ps[:, 2, 0:256], ACT.Identity, bias=k_bias).then_inc(kc_ready, 1)
            for c in range(5):
                act.wait_ge(tk_done, i * 5 + c + 1)
                if c >= 2:
                    act.wait_ge(sk_done, i * 5 + c - 1)
                b = (0, 6)[c % 2]
                act.copy(ktc[c % 2], ps[:, b:b + 2, :]).then_inc(ktc_ready, 1)
                if c == 1:
                    act.wait_ge(negc_ready, i + 1)
                    act.activation(pcS[:, 0:NCS], pcS[:, 0:NCS], ACT.Exp, bias=mx[:, 0:1],
                                   accum_out=rs[:, 0:1]).then_inc(expc_ready, 1)
            for k, (s, m) in enumerate(((sW, 2), (sS, 1))):
                act.wait_ge(negs_ready, i * 2 + k + 1)
                act.activation(s, s, ACT.Exp, bias=mx[:, m:m + 1], accum_out=rs[:, m:m + 1]).then_inc(exps_ready, 1)
            act.wait_ge(tp_done, i + 1)
            for b in range(3):
                act.copy(pT[:, 4 * b:4 * b + 4].rearrange("p t q -> p (t q)"), ps[:, b, :]).then_inc(pTa_ready, 1)

        def dve_odd(dve, C):
            dve.wait_ge(step_done, STEP_ODD + 4)
            dve.wait_ge(cg_ready, 2)
            for c in range(2):
                for s, lo, hi, at in SEGS:
                    dve.tensor_tensor(cvp[:, c, 2 + at:2 + at + hi - lo], cgT[:, c, at:at + hi - lo],
                                      ps[:, 2 * c + s, lo:hi], ALU.mult)
                C.after(dve.tensor_tensor(cvs[:, c, :, 2:2 + NT], cgT[:, c, SEQ:T].rearrange("p (b t) -> p b t", b=NB),
                                          ps[:, 2 * c + 1, SPLIT:HALF].rearrange("p (b t) -> p b t", b=NB), ALU.mult))
                dve.tensor_copy(cv_last[:, c].rearrange("p (b j) -> p b j", b=NB), cvs[:, c, :, NT:2 + NT]).then_inc(cu_ready, 1)
            dve.wait_ge(kc_done, 1)
            dve.wait_ge(cm_in, 16 * 27)
            dve.tensor_tensor(vc_p[0:32], ps[0:32, 3, 0:128], v_bias[0:32], ALU.add).then_inc(vc_ready, 1)
            for s, n in ((sc_free, 2), (t_done, 2), (pts_ready, 1), (ptw_ready, 1), (o_used, 1), (pages_used, 1)):
                dve.sem_inc(s, n)
            per = 120
            with dve.Fori(0, 3) as i:
                C.loop(i, per, lambda: [dve_queries(dve, C, i, u) for u in range(2)])
            C.skip(2 * per)
            dve.wait_ge(of_ready, 4)
            dve.sem_inc(win_free, 1)
            dve.sem_inc(pair_free, 1)
            per = 28
            with dve.Fori(0, NB // 2) as i:
                C.loop(i, per, lambda: dve_pair(dve, C, i))
            C.skip(per * (NB // 2 - 1))
            dve.sem_inc(down_free, 2)
            dve_add(dve, 4, STEP_OOUT, 1, 1.0)

        def dve_queries(dve, C, i, u):
            ns_ = const("neg_slope")
            slope = lambda g: ns_[:, ds(i * 2 + u + GQ * g, 1)]
            gate = lambda g, j, a, n: gts[:, j, ds(i * 6 + 3 * u + 3 * GQ * g + a, n)]
            at = lambda k: i * 16 + 8 * u + k
            flat = lambda g: sc_p[:, g].rearrange("p j n -> p (j n)")
            wide = lambda g: mc[:, g].unsqueeze(2).broadcast_to([128, 4, 32])
            for g in range(2):
                dve.wait_ge(scmp_done, i * 4 + 2 * u + g + 1)
                C.after(dve.scalar_tensor_tensor(out=flat(g), in0=const("dist_cmp"), scalar=slope(g),
                                                 in1=ps[:, 6 + g, 0:128], op0=ALU.mult, op1=ALU.add))
                C.after(dve.tensor_reduce(mc[:, g], sc_p[:, g], AX.X, ALU.max))
                C.after(dve.tensor_scalar(mc[:, g], mc[:, g], -1e20, None, ALU.max))
                dve.tensor_tensor(sc_p[:, g], sc_p[:, g], wide(g), ALU.subtract).then_inc(scmp_neg, 1)

            def scores(k):
                g, j = k // 4, k % 4
                n = 128 * j + 128
                dve.wait_ge(sc_done, at(k + 1))
                dve.wait_ge(t_done, at(k + 1))
                for br in range(2):
                    st = dve.scalar_tensor_tensor(out=sP[:, k % 2, br, 0:n], in0=const("dist")[:, 512 - n:512],
                                                  scalar=slope(g), in1=ps[:, 2 * (k % 2) + br, 0:n],
                                                  op0=ALU.mult, op1=ALU.add)
                st.then_inc(sc_free, 1)
                dve.wait_ge(sc_free, at(k + 3))
                C.after(dve.tensor_reduce(mx_p[:, k % 2], sP[:, k % 2, :, 0:n], AX.X, ALU.max))
                dve.tensor_scalar(mx_p[:, k % 2], mx_p[:, k % 2], -1.0, None, ALU.mult).then_inc(neg_ready, 1)

            def combine(k):
                g, j = k // 4, k % 4
                o = ps[:, 6 + k % 2, :]
                dve.wait_ge(pv_done, at(k + 1))
                dve.wait_ge(o_used, at(k + 1))
                C.after(dve.tensor_scalar(o1, o[:, 0:HD], gate(g, j, 0, 1), None, ALU.mult))
                C.after(dve.scalar_tensor_tensor(out=o1, in0=o[:, HD:2 * HD], scalar=coef[:, k % 2, 0:1], in1=o1,
                                                 op0=ALU.mult, op1=ALU.add))
                dve.scalar_tensor_tensor(out=otok[j // 2][:, j % 2, ds(i * 256 + 128 * u + 64 * g, HD)],
                                         in0=o[:, 2 * HD:3 * HD], scalar=coef[:, k % 2, 1:2], in1=o1,
                                         op0=ALU.mult, op1=ALU.add).then_inc(o_used, 1)

            scores(0)
            for g in range(2):
                dve.wait_ge(scmp_exp, i * 4 + 2 * u + g + 1)
                C.after(dve.tensor_reduce(mc[:, g], sc_p[:, g], AX.X, ALU.add))
                C.after(dve.tensor_scalar(mc[:, g], mc[:, g], 1e-30, None, ALU.max))
                C.after(dve.reciprocal(mc[:, g], mc[:, g]))
                dve.tensor_tensor(sc_p[:, g], sc_p[:, g], wide(g), ALU.mult).then_inc(scmp_ready, 1)
            for k in range(8):
                n = 128 * (k % 4) + 128
                if k < 7:
                    scores(k + 1)
                dve.wait_ge(t_done, at(k + 3))
                dve.tensor_copy(ptW[:, 0:n], ps[:, 5, 0:n]).then_inc(ptw_ready, 1)
                dve.wait_ge(exp_ready, at(k + 1))
                dve.wait_ge(o_used, at(max(k, 1)))
                cf = coef[:, k % 2]
                C.after(dve.tensor_scalar(cf, rs_p[:, k % 2], 1e-30, None, ALU.max))
                C.after(dve.reciprocal(cf, cf))
                C.after(dve.tensor_tensor(cf, cf, gate(k // 4, k % 4, 1, 2), ALU.mult))
                if k >= 1:
                    combine(k - 1)
            combine(7)

        def dve_pair(dve, C, i):
            nsr = const("neg_slope_row")
            dve.wait_ge(pages_in, i * PAGES + PAGES)
            dve.sem_inc(waited, 1)
            dve.tensor_scalar(qP, qB[:, ds(i * 2, 2)], 1.0, None, ALU.mult).then_inc(qP_ready, 1)
            dve.tensor_scalar(eP[0:TS], const("row_token", TS)[:, ds(i * 128, 128)], 1.0, None, ALU.mult).then_inc(qP_ready, 1)
            dve.wait_ge(kc_done, i + 2)
            dve.tensor_tensor(vcS[0:NCS], ps[0:NCS, 3, 0:256].rearrange("p (b n) -> p b n", b=2),
                              v_bias[0:NCS].unsqueeze(1).broadcast_to([NCS, 2, 128]), ALU.add).then_inc(vc_ready, 1)
            pc = pcS[:, 0:NCS]
            dve.wait_ge(scs_done, i + 1)
            C.after(dve.scalar_tensor_tensor(out=pc, in0=const("dist_cmp_s")[:, 0:NCS], scalar=nsr, in1=ps[:, 4, 0:NCS],
                                             op0=ALU.mult, op1=ALU.add))
            C.after(dve.tensor_reduce(mx[:, 0:1], pc, AX.X, ALU.max))
            dve.tensor_scalar(mx[:, 0:1], mx[:, 0:1], -1e20, -1.0, ALU.max, ALU.mult).then_inc(negc_ready, 1)

            def evacuate(c):
                dve.wait_ge(sk_done, i * 5 + c + 1)
                b = ps[:, 2 + c % 2, :]
                if c < 4:
                    e = dve.scalar_tensor_tensor(
                        out=sS[:, 512 * c:512 * c + 512].rearrange("p (b k) -> p b k", b=8),
                        in0=const("dist_blk").unsqueeze(1).broadcast_to([128, 8, 64]), scalar=nsr,
                        in1=b.rearrange("p (b k) -> p b k", b=8), op0=ALU.mult, op1=ALU.add)
                else:
                    e = dve.scalar_tensor_tensor(out=sW[:, 0:512], in0=const("dist_win"), scalar=nsr, in1=b,
                                                 op0=ALU.mult, op1=ALU.add)
                e.then_inc(sk_ready, 1)

            evacuate(0)
            evacuate(1)
            dve.wait_ge(expc_ready, i + 1)
            C.after(dve.tensor_scalar(rs[:, 0:1], rs[:, 0:1], 1e-30, None, ALU.max))
            C.after(dve.reciprocal(rs[:, 0:1], rs[:, 0:1]))
            dve.tensor_scalar(pc, pc, rs[:, 0:1], None, ALU.mult).then_inc(pc_ready, 1)
            for c in (2, 3, 4):
                evacuate(c)
            dve.wait_ge(new_done, i + 1)
            dn = const("dist_new")[:, ds(i * TS, TS)]
            dve.sem_inc(waited, 1)
            for s, at, b in ((sS, PAST, 0), (sW, 512, TS)):
                C.after(dve.scalar_tensor_tensor(out=s[:, at:at + TS], in0=dn, scalar=nsr, in1=ps[:, 5, b:b + TS],
                                                 op0=ALU.mult, op1=ALU.add))
            C.after(dve.tensor_tensor(g36, ps[:, 5, 64:64 + 3 * NH].rearrange("p (h c) -> p h c", c=3),
                                      const("row_head").unsqueeze(2).broadcast_to([128, NH, 3]), ALU.mult))
            C.after(dve.tensor_reduce(gs, g36.rearrange("p h c -> p c h"), AX.X, ALU.add))
            dve.wait_ge(sk_ready, i * 5 + 5)
            C.after(dve.tensor_reduce(mx[:, 2:3], sW, AX.X, ALU.max))
            dve.tensor_scalar(mx[:, 2:3], mx[:, 2:3], -1.0, None, ALU.mult).then_inc(negs_ready, 1)
            dve.wait_ge(imp_done, i + 1)
            C.after(dve.tensor_copy(imp[:, 1:1 + NCS], ps[:, 4, 128:128 + NCS]))
            four = imp.rearrange("p (b r) -> p b r", r=4)
            C.after(dve.tensor_reduce(score[:, 0:NBLK - 1], four[:, 0:NBLK - 1], AX.X, ALU.add))
            C.after(dve.tensor_tensor(score[:, 0:NBLK - 1], score[:, 0:NBLK - 1], four[:, 1:NBLK, 0], ALU.add))
            C.after(dve.memset(score[:, 0:1], 1e30))
            C.after(dve.memset(score[:, NBLK - 2:NBLK], 1e30))
            for src, dst in ((score, score2), (score2, score)):
                dve.sem_inc(waited, 1)
                C.after(dve.max(top8, src))
                dve.sem_inc(waited, 1)
                C.after(dve.match_replace(dst, top8, src, -3e38))
            C.after(dve.tensor_scalar(score2, score, -1e38, -1e30, ALU.is_gt, ALU.mult))
            C.after(dve.tensor_tensor(blk_add, score2, const("blk_base"), ALU.add))
            sb_ = sS[:, 0:PAST].rearrange("p (b k) -> p b k", k=64)
            C.after(dve.tensor_tensor(sb_, sb_, blk_add[:, 0:NBLK - 1].unsqueeze(2).broadcast_to([128, NBLK - 1, 64]), ALU.add))
            C.after(dve.tensor_reduce(mx[:, 1:2], sS, AX.X, ALU.max))
            dve.tensor_scalar(mx[:, 1:2], mx[:, 1:2], -1.0, None, ALU.mult).then_inc(negs_ready, 1)
            dve.wait_ge(exps_ready, i * 2 + 2)
            C.after(dve.tensor_scalar(rs[:, 1:3], rs[:, 1:3], 1e-30, None, ALU.max))
            C.after(dve.reciprocal(rs[:, 1:3], rs[:, 1:3]))
            C.after(dve.tensor_tensor(gs[:, 1:3], gs[:, 1:3], rs[:, 1:3], ALU.mult))
            dve.wait_ge(tp_done, i + 1)
            dve.tensor_copy(pT[:, 12:16].rearrange("p t q -> p (t q)"), ps[:, 3, :]).then_inc(pTv_ready, 1)
            dve.tensor_copy(pT[:, 16:20].rearrange("p t q -> p (t q)"), ps[:, 4, :]).then_inc(pTv_ready, 1)
            dve.tensor_copy(pT[0:NCS, 20], ps[0:NCS, 5, 0:128]).then_inc(pTv_ready, 1)
            dve.tensor_copy(pT[0:TS, 21:23].rearrange("p t q -> p (t q)"), ps[0:TS, 5, 128:384]).then_inc(pTv_ready, 1)
            dve.wait_ge(pvs_done, i + 1)
            C.after(dve.tensor_scalar(o_s, ps[:, 6, 0:128], gs[:, 0:1], None, ALU.mult))
            dve.sem_inc(pages_used, 1)
            dve.sem_inc(win_free, 1)
            C.after(dve.scalar_tensor_tensor(out=o_s, in0=ps[:, 6, 128:256], scalar=gs[:, 1:2], in1=o_s,
                                             op0=ALU.mult, op1=ALU.add))
            dve.scalar_tensor_tensor(out=o_s, in0=ps[:, 6, 256:384], scalar=gs[:, 2:3], in1=o_s,
                                     op0=ALU.mult, op1=ALU.add).then_inc(os_ready, 1)
            dve.wait_ge(ot_done, i + 1)
            for b in range(2):
                for g in range(2):
                    src = ps[64 * g:64 * g + 64, 7, 64 * b + 32 * g:64 * b + 32 * g + 4 * GQ]
                    o = dve.tensor_scalar(oT[64 * g:64 * g + 64, :, ds(i * (2 * NT) + SEQ + NT * b, NT)],
                                          src.rearrange("p (i t) -> p i t", t=NT), 1.0, None, ALU.mult)
            C.after(o)
            dve.sem_inc(pair_free, 1)

        block = ctx.enter_context(nc.Block())

        @block.sync
        def _(sp):
            sp_load(sp)
            load_ffn(sp, 0, 0)
            load_even(sp)
            load_ffn(sp, 1, STEP_FFN1)
            load_ffn(sp, 2, STEP_FFN2)
            load_odd(sp)
            load_ffn(sp, 3, STEP_FFN3)

        @block.gpsimd
        def _(po):
            C = Chain(po, gchain)
            pool_even(po, C)
            pool_odd(po, C)
            po.wait_ge(stored, 16 * n_stored[0])

        @block.tensor
        def _(pe):
            pe_load(pe)
            pe_norm(pe, 0)
            pe_ffn(pe, 0, 0)
            pe_norm(pe, 1)
            pe_even(pe)
            pe_norm(pe, 2)
            pe_ffn(pe, 1, STEP_FFN1)
            pe_norm(pe, 3)
            pe_ffn(pe, 2, STEP_FFN2)
            pe_norm(pe, 4)
            pe_odd(pe)
            pe_norm(pe, 5)
            pe_ffn(pe, 3, STEP_FFN3)
            pe_norm(pe, 6)
            pe_final(pe)

        @block.scalar
        def _(act):
            act_load(act)
            act_norm(act, 0)
            act_ffn(act, 0, 0)
            act_norm(act, 1)
            act_even(act)
            act_norm(act, 2)
            act_ffn(act, 1, STEP_FFN1)
            act_norm(act, 3)
            act_ffn(act, 2, STEP_FFN2)
            act_norm(act, 4)
            act_odd(act)
            act_norm(act, 5)
            act_ffn(act, 3, STEP_FFN3)
            act_norm(act, 6)
            act_final(act)

        @block.vector
        def _(dve):
            C = Chain(dve, vchain)
            dve_load(dve)
            dve_norm(dve, 0)
            dve_ffn(dve, 0, 0)
            dve_norm(dve, 1)
            dve_even(dve, C)
            dve_norm(dve, 2)
            dve_ffn(dve, 1, STEP_FFN1)
            dve_norm(dve, 3)
            dve_ffn(dve, 2, STEP_FFN2)
            dve_norm(dve, 4)
            dve_odd(dve, C)
            dve_norm(dve, 5)
            dve_ffn(dve, 3, STEP_FFN3)
            dve_norm(dve, 6)


_INS = ['x_prompt', 'x_sample', 'state_pool', 'state_mlstm_c', 'state_mlstm_n', 'state_mlstm_m',
        'cache_nsa_kv', 'state_win_kv', 'state_conv', 'page_table', 'norm_g', 'final_g', 'w_ffn_in',
        'w_ffn_out', 'w_in_even', 'b_gate_even', 'w_pool', 'pool_scale', 'w_out_even', 'w_in_odd',
        'cmp_pos_w', 'cmp_w', 'cmp_b', 'conv_w', 'w_out_odd']
_OUTS = [(1, SEQ, D), (NB, NT, D), (1, 1, 15, 256), (1, NB, 15, 256), (1, 1, H4, DH, DH), (1, NB, H4, DH, DH),
         (1, 1, H4, DH), (1, NB, H4, DH), (1, 1, H4), (1, NB, H4), (1, 1, SEQ, 4, 2, HD), (1, NB, NT, 4, 2, HD),
         (1, 1, SEQ, 2, 2, HD), (1, NB, 512, 2, 2, HD), (1, 1, 2, 256), (1, NB, 2, 256)]


def kernel(**inputs):
    import numpy as _np
    import concourse.bacc as _bacc
    from concourse import mybir as _mybir
    from concourse.bass_utils import run_bass_kernel_spmd as _run

    nc = _bacc.Bacc("TRN2", target_bir_lowering=False, num_devices=1)
    arrays, args = {}, []
    for name in _INS + ["consts"]:
        a = CONSTS if name == "consts" else _np.ascontiguousarray(inputs[name])
        arrays[f"in_{name}_dram"] = a
        args.append(nc.dram_tensor(f"in_{name}_dram", a.shape, _mybir.dt.from_np(a.dtype), kind="ExternalInput").ap())
    for i, shape in enumerate(_OUTS):
        args.append(nc.dram_tensor(f"out_{i}_dram", shape, _mybir.dt.float32, kind="ExternalOutput").ap())
    trunk(nc, *args)
    r = _run(nc, [arrays], core_ids=[0])
    return tuple(r.results[0][f"out_{i}_dram"] for i in range(len(_OUTS)))
```

```python
from contextlib import ExitStack

import numpy as np
import concourse.bass as bass
from concourse import mybir

F32 = mybir.dt.float32
F32R = mybir.dt.float32r
I32 = mybir.dt.int32
ALU = mybir.AluOpType
ACT = mybir.ActivationFunctionType
AX = mybir.AxisListType
ds = bass.ds

D = 1024
NK = D // 128
SEQ = 512
NB = 8
NT = 4
TS = NB * NT
T = SEQ + TS
HALF = T // 2
SPLIT = SEQ - HALF
PAST = 2048
PAGE = 128
NPG = PAST // PAGE
DFF = 2816
NF = DFF // 128
EPS = 1e-6
H4 = 4
DH = 192
EC = 96
KTILES = 5
NH = 12
HD = 64
GQ = 6
NCP = SEQ // 16 - 1
NCS = PAST // 16 - 1
NBLK = PAST // 64 + 1
BIG = 3e37
SLOT = 4096

STEPS_FFN = NF // 2 + 8
STEP_EVEN = STEPS_FFN
STEP_HEADS = STEP_EVEN + 1
STEP_EOUT = STEP_HEADS + 2 * H4
STEP_FFN1 = STEP_EOUT + 4
STEP_FFN2 = STEP_FFN1 + STEPS_FFN
STEP_ODD = STEP_FFN2 + STEPS_FFN
STEP_Q = STEP_ODD + 4
STEP_OOUT = STEP_Q + 6
STEP_FFN3 = STEP_OOUT + 4


def slopes():
    return 2.0 ** (-8.0 * np.arange(1, NH + 1) / NH)


def tok_tile(t):
    return 128 if t < 4 else TS


def make_consts():
    parts, at = [], {}

    def put(name, a):
        a = np.asarray(a, np.float32)
        full = np.zeros((128, int(np.prod(a.shape[1:]))), np.float32)
        full[:a.shape[0]] = a.reshape(a.shape[0], -1)
        at[name] = (sum(x.shape[1] for x in parts), full.shape[1])
        parts.append(full)

    p = np.arange(128)
    put("ident", np.eye(128))
    put("ones", np.ones((128, 128)))
    put("zeros", np.zeros((128, 128)))
    put("eps", np.full((128, 1), EPS))
    put("mean", np.full((128, 128), 1.0 / D))
    put("late", np.where(p[:, None] <= p[None, :], 0.0, 1e30))
    s = np.arange(TS)
    same = (s[:, None] // NT) == (s[None, :] // NT)
    put("late_s", np.where(same & (s[:, None] <= s[None, :]), 0.0, 1e30))
    put("of_batch", (s[:, None] // NT) == np.arange(NB)[None, :])
    put("onehot4", np.eye(4))
    w = np.array([[2, 8], [4, 16]])
    wp = w[p // 64]
    put("inv_w", 1.0 / wp)
    put("inv_first", 1.0 / np.minimum(np.arange(16)[None, None, :] + 1.0, wp[:, :, None]))
    c = np.arange(512)
    dist = p[:, None] - (c[None, :] - 384)
    put("dist", np.where(dist >= 0, dist, BIG))
    n = np.arange(32)
    dc = (128 * np.arange(4)[None, :, None] + p[:, None, None]) - (16 * n[None, None, :] + 31)
    put("dist_cmp", np.where((dc >= 0) & (n < NCP)[None, None, :], dc, BIG))
    r = p % 32
    t, hq, g, b2 = r % NT, r // NT, (p // 32) % 2, p // 64
    real = r < GQ * NT
    n = np.arange(128)
    put("dist_cmp_s", PAST + t[:, None] - (16 * n[None, :] + 31))
    put("dist_blk", t[:, None] - np.arange(64)[None, :])
    k = np.arange(512)
    put("dist_win", np.where(k[None, :] > t[:, None], 512 + t[:, None] - k[None, :], BIG))
    pair = np.arange(4)
    ok = ((s[None, None, :] // NT) == (2 * pair[None, :, None] + b2[:, None, None])) & \
        ((s % NT)[None, None, :] <= t[:, None, None])
    put("dist_new", np.where(ok, t[:, None, None] - (s % NT)[None, None, :], BIG))
    sl = slopes()
    put("neg_slope", np.broadcast_to(-sl[None, :], (128, NH)))
    rs = np.where(real, sl[np.minimum(g * GQ + hq, NH - 1)], 1.0)
    put("neg_slope_row", -rs[:, None])
    put("blk_base", -rs[:, None] * (PAST - 64.0 * np.arange(NBLK))[None, :])
    put("same_query", real[:, None] & real[None, :] & (b2[:, None] == b2[None, :]) &
        (g[:, None] == g[None, :]) & (t[:, None] == t[None, :]))
    put("row_token", (s[:, None, None] == ((2 * pair[None, :, None] + b2[None, None, :]) * NT + t[None, None, :])))
    put("row_head", real[:, None] & ((g * GQ + hq)[:, None] == np.arange(NH)[None, :]))
    return np.concatenate(parts, axis=1), at


CONSTS, CAT = make_consts()
NCONST = CONSTS.shape[1]


class Arena:

    def __init__(self, tensor, size):
        self.tensor, self.size, self.at = tensor, size, 0

    def take(self, *shape):
        n = int(np.prod(shape))
        assert self.at + n <= self.size, (self.at, n, self.size)
        v = self.tensor[:, self.at:self.at + n]
        self.at += n
        if len(shape) == 2:
            v = v.rearrange("p (a b) -> p a b", a=shape[0])
        if len(shape) == 3:
            v = v.rearrange("p (a b c) -> p a b c", a=shape[0], b=shape[1])
        return v


class Chain:

    def __init__(self, eng, sem):
        self.eng, self.sem, self.n, self.moving = eng, sem, 0, 0

    def after(self, ins):
        ins.then_inc(self.sem, 1)
        self.n += 1
        self.eng.wait_ge(self.sem, self.n + self.moving)

    def loop(self, i, per, body):
        start = self.n
        self.moving = i * per
        body()
        assert self.n - start == per, ("links of a body", self.n - start)
        self.moving = 0

    def skip(self, count):
        self.n += count


def trunk(nc, x_prompt, x_sample, state_pool, state_mlstm_c, state_mlstm_n, state_mlstm_m,
          cache_nsa_kv, state_win_kv, state_conv, page_table,
          norm_g, final_g, w_ffn_in, w_ffn_out, w_in_even, b_gate_even, w_pool, pool_scale,
          w_out_even, w_in_odd, cmp_pos_w, cmp_w, cmp_b, conv_w, w_out_odd, consts,
          y_prompt, y_sample, pool_p, pool_s, c_p, c_s, n_p, n_s, m_p, m_s,
          kv_rows_p, kv_rows_s, win_p, win_s, conv_p, conv_s):
    ctx = ExitStack()
    with ctx:
        ctx.enter_context(nc.allow_non_contiguous_dma("small transposed vectors"))
        def sb(name, shape, dt=F32):
            return ctx.enter_context(nc.sbuf_tensor(name, shape, dt))

        def sem(name):
            return ctx.enter_context(nc.semaphore(name))

        A_SIZE, G_SIZE = 14080, 2 * NPG * 512
        at = {}

        def placed(name, shape, dt=F32):
            t = sb(name, shape, dt)
            at[name] = nc.sbuf_base - 4 * int(np.prod(shape[1:]))
            return t

        def over(name, base, skip, shape):
            return nc.alloc_sbuf_tensor_at(name, shape, F32R, offset=at[base] + 4 * skip)

        x = placed("x", [128, NK, T])
        h = placed("h", [128, NK, T])
        ring = placed("ring", [128, 2, SLOT])
        arena_t = placed("arena_t", [128, A_SIZE])
        pages_t = placed("pages_t", [128, G_SIZE])
        h_hi, h_lo = over("h_hi", "h", 0, [128, NK, T]), over("h_lo", "pages_t", 0, [128, NK, T])
        GC = 12
        g_hi = over("g_hi", "arena_t", 0, [128, GC, T])
        g_lo = over("g_lo", "arena_t", GC * T, [128, GC, T])
        w_split = over("w_split", "pages_t", NK * T, [128, 2, 2, 2048])
        h_raw = pages_t[:, NK * T + 8192:NK * T + 8192 + 4 * T].rearrange("p (i t) -> p i t", i=4)
        cst = sb("cst", [128, NCONST])
        vecs = sb("vecs", [128, 64])
        ns = sb("ns", [128, 5 * T])
        pt = sb("pt", [1, NB * NPG], I32)
        ps = ctx.enter_context(nc.psum_tensor("ps", [128, 8, 512], F32))

        def const(name, rows=128):
            a, n = CAT[name]
            return cst[0:rows, a:a + n]

        ident, ones = const("ident"), const("ones")
        gain = lambda r, c: vecs[:, 8 * r + c:8 * r + c + 1]
        V_POOL, V_CONV = 56, 58
        sq = [ns[:, i * T:(i + 1) * T] for i in (0, 1)]
        sil = [ns[:, i * T:(i + 1) * T] for i in (2, 3)]
        rinv = ns[:, 4 * T:5 * T]

        def halves(ap):
            return ap.rearrange("p (s t) -> p s t", s=2)

        def banks(b, rows=128):
            return ps[0:rows, b:b + 2, 0:HALF]

        consts_in, inputs_in = sem("consts_in"), sem("inputs_in")
        x_in = [sem(f"x_in_{t}") for t in range(KTILES)]
        weights_in = [sem("weights_in_0"), sem("weights_in_1")]
        step_done = sem("step_done")
        vecs_flip, vecs_ready = sem("vecs_flip"), sem("vecs_ready")
        x_flipped, x_copied, x_taken = sem("x_flipped"), sem("x_copied"), sem("x_taken")
        sq_ready, sq_used = sem("sq_ready"), sem("sq_used")
        rms_ready, rinv_ready, h_ready = sem("rms_ready"), sem("rinv_ready"), sem("h_ready")
        split_hi, split_lo = sem("split_hi"), sem("split_lo")
        part_done = sem("part_done")
        sil_ready, up_free, gated_ready = sem("sil_ready"), sem("up_free"), sem("gated_ready")
        down_free = sem("down_free")
        hraw_ready, hhi_ready = sem("hraw_ready"), sem("hhi_ready")
        y_flipped, y_copied, y_stored = sem("y_flipped"), sem("y_copied"), sem("y_stored")
        stored = sem("stored")
        vchain = sem("vchain")
        scratch_stored = sem("scratch_stored")
        n_stored = [0]

        ghi_ready = sem("ghi_ready")
        DOWN_BASE = [0, 20, 26, 46, 66, 72, 92]
        FFN_NORM = (0, 2, 3, 5)

        def use_step(pe, n, moved=0):
            pe.wait_ge(weights_in[n % 2], 32 * (n // 2 + 1) + moved)

        def slot(n, *shape):
            v = ring[:, n % 2, 0:int(np.prod(shape))]
            if len(shape) == 2:
                return v.rearrange("p (k n) -> p k n", k=shape[0])
            return v.rearrange("p (a k n) -> p a k n", a=shape[0], k=shape[1])

        def load(sp, n, out_in, moved=0, split=None):
            if split is None:
                sp.wait_ge(step_done, n - 1 + moved)
            elif n >= 2:
                sp.wait_ge(split_lo, split + moved)
            for o, i in out_in:
                sp.dma_start(o, i).then_inc(weights_in[n % 2], 16)

        PASSES = ((0, 12), (12, 10))
        PART = 38
        UP_AT, DOWN_AT = (0, 20), (12, 30)

        def part_views(n, m):
            u = m % 2
            if m < 12 or 20 <= m < 30:
                raw = slot(n, 2, NK, 256)[:, :, :, 128 * u:128 * u + 128]
                hl = [w_split[:, u, i, :].rearrange("p (a k n) -> p a k n", a=2, k=NK) for i in range(2)]
            else:
                k = PASSES[m >= 30][1]
                raw = slot(n, k, 256)[:, :, 128 * u:128 * u + 128]
                hl = [w_split[:, u, i, 0:128 * k].rearrange("p (k n) -> p k n", k=k) for i in range(2)]
            return raw, hl[0], hl[1]

        def load_ffn(sp, f, base):
            w_in = w_ffn_in[f // 2, f % 2].rearrange("(k p) n -> p k n", p=128)
            w_out = w_ffn_out[f // 2, f % 2].rearrange("(k p) n -> p k n", p=128)
            after_mixer = f in (1, 3)

            def up(j, at, i4=0, j2=False):
                n = base + j
                v = slot(n, 2, NK, 256)
                load(sp, n, [(v[:, 0], w_in[:, :, ds(at, 256)]),
                             (v[:, 1], w_in[:, :, ds(at + DFF, 256)])],
                     i4, None if j2 else PART * f + 2 * j - 2)

            def down(j, p, at, i4):
                n = base + j
                k0, k = PASSES[p]
                v = slot(n, k, 256)
                load(sp, n, [(v[:, 0:6], w_out[:, k0:k0 + 6, ds(at, 256)]),
                             (v[:, 6:k], w_out[:, k0 + 6:k0 + k, ds(at, 256)])], i4, PART * f + 2 * j - 2)

            for j in range(2):
                up(j, 256 * j, 0, after_mixer)
            with sp.Fori(0, 2) as i:
                for u in range(2):
                    up(2 + u, i * 512 + 512 + 256 * u, i * 4)
            with sp.Fori(0, 2) as i:
                for u in range(2):
                    down(6 + u, 0, i * 512 + 256 * u, i * 4)
            with sp.Fori(0, 2) as i:
                for u in range(2):
                    up(10 + u, i * 512 + 1536 + 256 * u, i * 4)
            up(14, 2560)
            with sp.Fori(0, 2) as i:
                for u in range(2):
                    down(15 + u, 1, i * 512 + 256 * u, i * 4)

        def pe_ffn(pe, f, base):
            r = FFN_NORM[f]

            def product(b, w_hi, w_lo, x_hi, x_lo, first, last):
                for q, (w, v) in enumerate(((w_hi, x_hi), (w_hi, x_lo), (w_lo, x_hi))):
                    for s in range(2):
                        mm = pe.matmul(ps[:, b + s, 0:HALF], w, v[:, HALF * s:HALF * s + HALF],
                                       start=first and q == 0, stop=last and q == 2)
                return mm

            def up(m, i):
                u, c = m % 2, m if m < 12 else m - 8
                _, hi, lo = part_views(base, m)
                pe.wait_ge(split_lo, PART * f + m + 1 + i * 4)
                pe.wait_ge(up_free, 24 * f + c + 1 + i * 4)
                for k in range(NK):
                    if m == 0:
                        pe.wait_ge(h_ready, NK * r + k + 1)
                    for ab in range(2):
                        mm = product(4 * u + 2 * ab, hi[:, ab, k], lo[:, ab, k], h_hi[:, k], h_lo[:, k],
                                     k == 0, k == NK - 1)
                mm.then_inc(part_done, 1)

            def down(m, p, moved):
                k0, n = PASSES[p]
                _, hi, lo = part_views(base, m)
                pe.wait_ge(split_lo, PART * f + m + 1 + moved)
                c = m - DOWN_AT[p]
                pe.wait_ge(down_free, DOWN_BASE[r] + 10 * p + c + 1 + moved)
                for k in range(n):
                    if c == 0 and k == n - 1:
                        pe.wait_ge(gated_ready, 24 * f + 2 + k0 + n)
                    mm = product(2 * (c % 2), hi[:, k], lo[:, k], g_hi[:, k], g_lo[:, k], k == 0, k == n - 1)
                mm.then_inc(part_done, 1)

            def mean(c, moved):
                pe.wait_ge(sq_ready, NK * (r + 1) + c + 1 + moved)
                for s in range(2):
                    mm = pe.matmul(ps[:, 6 + s, 0:HALF], const("mean"), sq[c % 2][:, HALF * s:HALF * s + HALF],
                                   start=(c == 0), stop=(c == NK - 1), skip_group_check=True)
                mm.then_inc(sq_used, 1)

            for p, (k0, n) in enumerate(PASSES):
                if p == 1:
                    pe.wait_ge(down_free, DOWN_BASE[r] + 10)
                with pe.Fori(0, n // 4) as i:
                    for j in range(4):
                        up(UP_AT[p] + j, i)
                for m in range(n // 4 * 4, n):
                    up(UP_AT[p] + m, 0)
                pe.wait_ge(gated_ready, 24 * f + 1 + k0 + n)
                if p == 0:
                    with pe.Fori(0, 2) as i:
                        for j in range(4):
                            down(DOWN_AT[0] + j, 0, i * 4)
                    continue
                down(DOWN_AT[1], 1, 0)
                down(DOWN_AT[1] + 1, 1, 0)
                pe.wait_ge(up_free, 24 * f + 24)
                mean(0, 0)
                with pe.Fori(0, 3) as i:
                    for j in range(2):
                        down(DOWN_AT[1] + 2 + j, 1, i * 2)
                        mean(1 + j, i * 2)
                mean(7, 0)
            pe.sem_inc(step_done, STEPS_FFN)

        def act_split(act, f, base, m, i=None):
            moved = 0 if i is None else i
            n = base + m // 2
            raw, hi, _ = part_views(n, m)
            act.wait_ge(weights_in[n % 2], 32 * (n // 2 + 1) + moved * 32)
            if PART * f + m >= 2:
                act.wait_ge(part_done, PART * f + m - 1 + moved * 4)
            act.copy(hi, raw).then_inc(split_hi, 1)

        def dve_split(dve, f, base, m, i=None):
            moved = 0 if i is None else i
            raw, hi, lo = part_views(base + m // 2, m)
            dve.wait_ge(split_hi, PART * f + m + 1 + moved * 4)
            dve.tensor_tensor(lo, raw, hi.bitcast(F32), ALU.subtract).then_inc(split_lo, 1)

        def dve_first_part(dve, f, base):
            raw, hi, _ = part_views(base, 0)
            dve.wait_ge(weights_in[base % 2], 32 * (base // 2 + 1))
            dve.tensor_copy(hi, raw).then_inc(split_hi, 1)
            dve_split(dve, f, base, 0)

        def act_ffn(act, f, base):
            def up(m, i):
                u, c = m % 2, m if m < 12 else m - 8
                act.wait_ge(part_done, PART * f + m + 1 + i * 4)
                act.wait_ge(gated_ready, 24 * f + c + 1 + i * 4)
                act.activation(halves(sil[u]), banks(4 * u), ACT.Silu).then_inc(sil_ready, 1)
                act_split(act, f, base, m + 2, i)

            for p, (k0, n) in enumerate(PASSES):
                with act.Fori(0, 2) as i:
                    for j in range(4):
                        up(UP_AT[p] + j, i)
                for j in range(8, n):
                    up(UP_AT[p] + j, 0)
                for j in range(NK):
                    if p == 0 or j < 6:
                        act_split(act, f, base, DOWN_AT[p] + j + 2)
                    if p == 1:
                        act.wait_ge(down_free, DOWN_BASE[FFN_NORM[f]] + 13 + j)
                        square(act, FFN_NORM[f] + 1, j)

        def dve_ffn(dve, f, base):
            r = FFN_NORM[f]
            def up(m, p, i):
                u, c = m % 2, m if m < 12 else m - 8
                at = i * 4 + (c - PASSES[p][0])
                dve.wait_ge(sil_ready, NF * f + c + 1 + i * 4)
                dve.tensor_tensor(halves(sil[u]), halves(sil[u]), banks(4 * u + 2), ALU.mult).then_inc(up_free, 1)
                hi = g_hi[:, ds(at, 1)].rearrange("p a t -> p (a t)")
                dve.wait_ge(up_free, 24 * f + c + 3 + i * 4)
                dve.tensor_scalar(hi, sil[u], 1.0, None, ALU.mult).then_inc(ghi_ready, 1)
                dve.wait_ge(ghi_ready, NF * f + c + 1 + i * 4)
                dve.tensor_tensor(g_lo[:, ds(at, 1)].rearrange("p a t -> p (a t)"), sil[u], hi.bitcast(F32),
                                  ALU.subtract).then_inc(gated_ready, 1)
                dve_split(dve, f, base, m + 2, i)

            for p, (k0, n) in enumerate(PASSES):
                with dve.Fori(0, 2) as i:
                    for j in range(4):
                        up(UP_AT[p] + j, p, i)
                for j in range(8, n):
                    up(UP_AT[p] + j, p, 0)
                    if j == n - 2:
                        dve.wait_ge(up_free, 24 * f + 2 + k0 + n - 1)
                        dve.sem_inc(down_free, 2)
                for c in range(NK):
                    m = DOWN_AT[p] + c
                    dve.wait_ge(part_done, PART * f + m + 1)
                    dve.scalar_tensor_tensor(out=halves(x[:, c]), in0=banks(2 * (c % 2)), scalar=0.5,
                                             in1=halves(x[:, c]), op0=ALU.mult, op1=ALU.add).then_inc(down_free, 1)
                    if p == 0 or c < 6:
                        dve_split(dve, f, base, m + 2)

        def dve_add(dve, q, base, per, scale):
            with dve.Fori(0, 2) as i:
                for u in range(2):
                    dve.wait_ge(step_done, base + per * (u + 1) + i * (2 * per))
                    for c in range(2):
                        xs = x[:, ds(i * 4 + 2 * u + c, 1)].rearrange("p a (s t) -> p (a s) t", s=2)
                        add = dve.scalar_tensor_tensor(out=xs, in0=banks(4 * u + 2 * c), scalar=scale,
                                                       in1=xs, op0=ALU.mult, op1=ALU.add)
                    add.then_inc(down_free, 1)

        FFN_STEP = (0, STEP_FFN1, STEP_FFN2, STEP_FFN3)

        AFTER_FFN = (1, 3, 4, 6)

        def square(act, r, c):
            if c >= 2:
                act.wait_ge(sq_used, NK * r + c - 1)
            act.activation(sq[c % 2], x[:, c, :], ACT.Square).then_inc(sq_ready, 1)

        def act_norm(act, r):
            if r == 0:
                act.wait_ge(x_copied, KTILES)
                act.wait_ge(x_taken, KTILES)
            if r not in AFTER_FFN:
                if r > 0:
                    act.wait_ge(down_free, DOWN_BASE[r])
                for c in range(NK):
                    square(act, r, c)
            act.wait_ge(sq_used, NK * (r + 1))
            act.activation(halves(rinv), banks(6 if r in AFTER_FFN else 0), ACT.Sqrt, bias=const("eps")).then_inc(rms_ready, 1)
            if r in FFN_NORM:
                f = FFN_NORM.index(r)
                for c in range(NK):
                    act.wait_ge(hraw_ready, NK * f + c + 1)
                    act.copy(h_hi[:, c], h_raw[:, c % 4]).then_inc(hhi_ready, 1)
                act.wait_ge(split_hi, PART * f + 1)
                act_split(act, f, FFN_STEP[f], 1)

        def pe_norm(pe, r):
            if r in AFTER_FFN:
                return
            if r > 0:
                pe.wait_ge(down_free, DOWN_BASE[r])
            else:
                pe.wait_ge(x_copied, KTILES)
                pe.wait_ge(x_taken, KTILES)
            for c in range(NK):
                pe.wait_ge(sq_ready, NK * r + c + 1)
                for s in range(2):
                    mm = pe.matmul(ps[:, s, 0:HALF], const("mean"), sq[c % 2][:, HALF * s:HALF * s + HALF],
                                   start=(c == 0), stop=(c == NK - 1))
                mm.then_inc(sq_used, 1)

        def dve_norm(dve, r):
            if r in FFN_NORM:
                f = FFN_NORM.index(r)
                if r > 0:
                    dve.wait_ge(down_free, DOWN_BASE[r])
                    dve.wait_ge(scratch_stored, (f + 1) // 2)
                dve_first_part(dve, f, FFN_STEP[f])
            dve.wait_ge(rms_ready, r + 1)
            if r in FFN_NORM:
                dve.sem_inc(up_free, 2)
                dve.sem_inc(gated_ready, 2)
            if r == 0:
                dve.wait_ge(vecs_ready, 1)
            dve.reciprocal(rinv, rinv).then_inc(rinv_ready, 1)
            dve.wait_ge(rinv_ready, r + 1)
            if r not in FFN_NORM:
                for c in range(NK):
                    dve.scalar_tensor_tensor(out=h[:, c, :], in0=x[:, c, :], scalar=gain(r, c), in1=rinv,
                                             op0=ALU.mult, op1=ALU.mult).then_inc(h_ready, 1)
                return
            f = FFN_NORM.index(r)
            for c in range(NK + 2):
                if c < NK:
                    if c >= 4:
                        dve.wait_ge(h_ready, NK * r + c - 3)
                    dve.scalar_tensor_tensor(out=h_raw[:, c % 4], in0=x[:, c, :], scalar=gain(r, c), in1=rinv,
                                             op0=ALU.mult, op1=ALU.mult).then_inc(hraw_ready, 1)
                if c >= 2:
                    dve.wait_ge(hhi_ready, NK * f + c - 1)
                    dve.tensor_tensor(h_lo[:, c - 2], h_raw[:, (c - 2) % 4], h_hi[:, c - 2].bitcast(F32),
                                      ALU.subtract).then_inc(h_ready, 1)
            dve_split(dve, f, FFN_STEP[f], 1)

        xt = arena_t[:, 0:KTILES * D].rearrange("p (t n) -> p t n", t=KTILES)
        gain_rows = pages_t[0:64, G_SIZE - 128:G_SIZE]

        def flip(pe, out, in_):
            k, m = in_.shape[0], int(np.prod(in_.shape[1:]))
            if k == 128 and m == 128:
                return pe.transpose(out, in_, ident)
            return pe.matmul(out, in_, ident[0:k, 0:k], start=True, stop=True)

        def pe_load(pe):
            pe.wait_ge(consts_in, 16)
            pe.wait_ge(inputs_in, 64)
            flip(pe, ps[:, 7, 0:64], gain_rows[0:64, :]).then_inc(vecs_flip, 1)
            for t in range(KTILES):
                pe.wait_ge(x_in[t], 16)
                if t >= 2:
                    pe.wait_ge(x_copied, t - 1)
                    pe.wait_ge(x_taken, t - 1)
                for c in range(NK):
                    mm = flip(pe, ps[:, 2 * (t % 2) + c // 4, 128 * (c % 4):128 * (c % 4) + tok_tile(t)],
                              xt[0:tok_tile(t), t, 128 * c:128 * c + 128])
                mm.then_inc(x_flipped, 1)

        def sp_load(sp):
            sp.dma_start(cst[:, :], consts).then_inc(consts_in, 16)
            sp.dma_start(gain_rows[0:48, :], norm_g.rearrange("l s (c p) -> (l s c) p", p=128)).then_inc(inputs_in, 16)
            sp.dma_start(gain_rows[48:56, :], final_g.rearrange("(c p) -> c p", p=128)).then_inc(inputs_in, 16)
            sp.dma_start(gain_rows[56:58, :], pool_scale[0].rearrange("(c p) -> c p", p=128)).then_inc(inputs_in, 16)
            sp.dma_start(gain_rows[58:64, :], conv_w[0].rearrange("j (c p) -> (j c) p", p=128)).then_inc(inputs_in, 16)
            for t in range(4):
                sp.dma_start(xt[:, t, :], x_prompt[0, 128 * t:128 * t + 128, :]).then_inc(x_in[t], 16)
            sp.dma_start(xt[0:TS, 4, :], x_sample.rearrange("b t n -> (b t) n")).then_inc(x_in[4], 16)

        def copy_x(eng, copy, lo, done):
            for t in range(KTILES):
                w = tok_tile(t)
                eng.wait_ge(x_flipped, t + 1)
                copy(x[:, lo:lo + 4, 128 * t:128 * t + w],
                     ps[:, 2 * (t % 2) + lo // 4, :].rearrange("p (c t) -> p c t", c=4)[:, :, 0:w]).then_inc(done, 1)

        def act_load(act):
            copy_x(act, act.copy, 0, x_copied)

        def dve_load(dve):
            dve.wait_ge(vecs_flip, 1)
            dve.tensor_copy(vecs[:, :], ps[:, 7, 0:64]).then_inc(vecs_ready, 1)
            copy_x(dve, dve.tensor_copy, 4, x_taken)

        yt = xt

        def pe_final(pe):
            pe.wait_ge(h_ready, NK * 7)
            for t in range(KTILES):
                w = tok_tile(t)
                if t >= 2:
                    pe.wait_ge(y_copied, t - 1)
                for c in range(NK):
                    mm = flip(pe, ps[0:w, 4 + 2 * (t % 2) + c // 4, 128 * (c % 4):128 * (c % 4) + 128],
                              h[:, c, 128 * t:128 * t + w])
                mm.then_inc(y_flipped, 1)

        def act_final(act):
            for t in range(KTILES):
                w = tok_tile(t)
                act.wait_ge(y_flipped, t + 1)
                b = 4 + 2 * (t % 2)
                act.copy(yt[0:w, t, :].rearrange("p (b n) -> p b n", b=2), ps[0:w, b:b + 2, :]).then_inc(y_copied, 1)
                act.wait_ge(y_copied, t + 1)
                out = y_prompt[0, 128 * t:128 * t + w, :] if t < 4 else y_sample.rearrange("b t n -> (b t) n")
                act.dma_start(out, yt[0:w, t, :]).then_inc(y_stored, 16)
            act.wait_ge(y_stored, 16 * KTILES)

        A, G = Arena(arena_t, A_SIZE), Arena(pages_t, G_SIZE - 128)
        yml = A.take(2 * H4, T)
        ypool = A.take(2, T)
        uep, ues = A.take(2, 15 + SEQ), A.take(2, NB, 15 + NT)
        w2p, w2s = A.take(2, 15 + SEQ), A.take(2, NB, 15 + NT)
        w4p, w4s = A.take(2, 15 + SEQ), A.take(2, NB, 15 + NT)
        mixed = A.take(2, T)
        ROW = 2 * T + TS + NB
        rows, rows_h = A.take(ROW), A.take(ROW)
        acol, wkcol = A.take(KTILES, H4), A.take(KTILES, H4)
        dec_b = A.take(H4)
        kw = A.take(KTILES, DH)
        qT, kT, ogT = G.take(2, T), G.take(2, T), G.take(2, T)
        vtok = G.take(KTILES, DH)
        kwb = G.take(NB, DH)
        wt = G.take(4, SEQ)
        cS = G.take(NB, 2, DH)
        cT = G.take(2, 2, DH)
        c_new_p, n_new_p = G.take(2, DH), G.take(DH)
        nS, nN = G.take(H4, DH), G.take(H4, DH)
        nT = G.take(2, H4, NB)
        pool_rows = G.take(256)
        wp_bd = G.take(2, 128)
        u_rows = G.take(2, 256)
        em_s, den_s, wts = G.take(TS), G.take(TS), G.take(TS)
        qn, acc_s = G.take(2, TS), G.take(2, TS)
        small = G.take(160)
        a_s, dec_s = small[:, 32:64], small[:, 96:104]
        m0, b_i, b_f, m_out = G.take(NB), G.take(1), G.take(1), G.take(NB)
        em, rden = ns[0:EC, 0:SEQ], ns[0:EC, T:T + SEQ]
        gate = Arena(arena_t, 8 * T)
        g_i, g_f, g_l, g_e, g_a, g_x = (gate.take(T) for _ in range(6))
        g_wk = gate.take(T)
        ones4, head4 = ones[0:4, :], const("onehot4", 4)

        ein, wp_in, c_in = sem("ein"), sem("wp_in"), sem("c_in")
        zeroed, gchain = sem("zeroed"), sem("gchain")
        e0_done, u_ready, mixed_ready = sem("e0_done"), sem("u_ready"), sem("mixed_ready")
        prefix_flip, prefix_ready = sem("prefix_flip"), sem("prefix_ready")
        gf_ready, gl_ready = sem("gf_ready"), sem("gl_ready")
        wk_arg, wk_ready, mout_ready = sem("wk_arg"), sem("wk_ready"), sem("mout_ready")
        cols_flip, cols_ready = sem("cols_flip"), sem("cols_ready")
        k_done, qT_ready, kT_ready, v_done, v_ready, og_ready = (sem(n) for n in (
            "k_done", "qT_ready", "kT_ready", "v_done", "v_ready", "og_ready"))
        rowh_ready, mb_done, kflip_done, kw_ready = sem("rowh_ready"), sem("mb_done"), sem("kflip_done"), sem("kw_ready")
        warg_ready, w_ready, s_done, sT_ready = sem("warg_ready"), sem("w_ready"), sem("s_done"), sem("sT_ready")
        small_done, small_ready, wsarg_ready, ws_ready = (sem(n) for n in (
            "small_done", "small_ready", "wsarg_ready", "ws_ready"))
        mrow_done, em_ready, num_done, den_done = sem("mrow_done"), sem("em_ready"), sem("num_done"), sem("den_done")
        cp_done, cp_ready, yp_ready = sem("cp_done"), sem("cp_ready"), sem("yp_ready")
        ct_done, cT_ready, cn_done, cn_ready = sem("ct_done"), sem("cT_ready"), sem("cn_done"), sem("cn_ready")
        qn_ready, sfin_done, head_free = sem("qn_ready"), sem("sfin_done"), sem("head_free")
        ypool_done, ypool_ready, rows_done, rows_ready = (sem(n) for n in (
            "ypool_done", "ypool_ready", "rows_done", "rows_ready"))
        c_stored, waited = sem("c_stored"), sem("waited")
        cells_free, den_used = sem("cells_free"), sem("den_used")
        SEGS = [(0, 0, HALF, 0), (1, 0, SPLIT, HALF)]

        def load_even(sp):
            w = w_in_even[0].rearrange("(k p) n -> p k n", p=128)
            n = STEP_EVEN
            v = slot(n, NK, 264)
            load(sp, n, [(v[:, :, 0:256], w[:, :, 0:256]), (v[:, :, 256:264], w[:, :, 3328:3336])], 0, PART - 2)
            with sp.Fori(0, H4) as i:
                for u in range(2):
                    n = STEP_HEADS + u
                    v = slot(n, NK, 2 * DH)
                    a, b = ((256, 1024), (1792, 2560))[u]
                    load(sp, n, [(v[:, :, 0:DH], w[:, :, ds(i * DH + a, DH)]),
                                 (v[:, :, DH:2 * DH], w[:, :, ds(i * DH + b, DH)])], i * 2)
            wo = w_out_even[0]
            with sp.Fori(0, 2) as i:
                for u in range(2):
                    n = STEP_EOUT + u
                    v = slot(n, 10, 256)
                    at = i * 512 + 256 * u
                    load(sp, n, [(v[:, 0:2], wo[0:256].rearrange("(k p) n -> p k n", p=128)[:, :, ds(at, 256)]),
                                 (v[0:EC, 2:10], wo[256:D].rearrange("(k p) n -> p k n", p=EC)[:, :, ds(at, 256)])],
                         i * 2)

        def pool_even(po, C):
            po.wait_ge(h_ready, NK * 2)
            po.memset(wp_bd[:, :, :], 0.0).then_inc(zeroed, 1)
            po.dma_start(pool_rows[0:120, :], state_pool[0].rearrange("b r n -> (b r) n")).then_inc(ein, 16)
            po.dma_start(nS[0:NB, :, :], state_mlstm_n[0]).then_inc(ein, 16)
            po.dma_start(m0[0:H4, :], state_mlstm_m[0].rearrange("b h -> h b")).then_inc(ein, 16)
            po.dma_start(b_i[0:H4, :], b_gate_even[0, 0:H4].rearrange("(h o) -> h o", o=1)).then_inc(ein, 16)
            po.dma_start(b_f[0:H4, :], b_gate_even[0, H4:2 * H4].rearrange("(h o) -> h o", o=1)).then_inc(ein, 16)
            po.wait_ge(zeroed, 1)
            for g in range(4):
                r = 64 * (g % 2)
                po.dma_start(wp_bd[r:r + 64, g // 2, r:r + 64], w_pool[0, g]).then_inc(wp_in, 16)
            po.dma_start(pool_s[0, :, 0:11, :], state_pool[0, :, 4:15, :]).then_inc(stored, 16)
            n_stored[0] += 1
            po.memset(uep[:, :, 0:15], 0.0).then_inc(zeroed, 1)
            po.wait_ge(zeroed, 2)
            po.wait_ge(u_ready, 6)
            po.wait_ge(prefix_ready, 1)
            for e, a, b in ((uep, w2p, w4p), (ues, w2s, w4s)):
                v = lambda t, lo, hi: t[..., lo:hi]
                n = 15 + (SEQ if e is uep else NT)
                c1 = lambda t: t[:, 1]
                C.after(po.tensor_tensor(v(a, 1, n), v(e, 1, n), v(e, 0, n - 1), ALU.add))
                C.after(po.tensor_tensor(v(b, 3, n), v(a, 3, n), v(a, 1, n - 2), ALU.add))
                C.after(po.tensor_tensor(v(c1(a), 7, n), v(c1(b), 7, n), v(c1(b), 3, n - 4), ALU.add))
                C.after(po.tensor_tensor(v(c1(b), 15, n), v(c1(a), 15, n), v(c1(a), 7, n - 8), ALU.add))
            inv_w, inv_f = const("inv_w"), const("inv_first").rearrange("p (c t) -> p c t", c=2)
            mp, ms = mixed[:, :, 0:SEQ], mixed[:, :, SEQ:T].rearrange("p c (b t) -> p c b t", b=NB)
            for r, sp_, ss_ in ((0, w2p, w2s), (64, w4p, w4s)):
                q = slice(r, r + 64)
                for c in range(2):
                    C.after(po.tensor_scalar(mp[q, c], sp_[q, c, 15:15 + SEQ], inv_w[q, c:c + 1], None, ALU.mult))
                    C.after(po.tensor_scalar(ms[q, c], ss_[q, c, :, 15:15 + NT], inv_w[q, c:c + 1], None, ALU.mult))
                C.after(po.tensor_tensor(mp[q, :, 0:16], sp_[q, :, 15:31], inv_f[q], ALU.mult))
            C.after(po.tensor_tensor(mp, mp, uep[:, :, 15:15 + SEQ], ALU.subtract))
            for c in range(2):
                po.tensor_tensor(ms[:, c], ms[:, c], ues[:, c, :, 15:15 + NT], ALU.subtract).then_inc(mixed_ready, 1)

            po.wait_ge(mout_ready, 1)
            po.dma_start(m_s[0].rearrange("b h -> h b"), m_out[0:H4, :]).then_inc(stored, 16)
            po.dma_start(m_p[0, 0].rearrange("(h o) -> h o", o=1), rows[0:H4, T + SEQ - 1:T + SEQ]).then_inc(stored, 16)
            n_stored[0] += 2
            with po.Fori(0, H4) as i:
                po.wait_ge(head_free, i + 1)
                po.sem_inc(waited, 1)
                for b in range(NB):
                    po.dma_start(cS[0:EC, b], state_mlstm_c[0, b, ds(i, 1)].rearrange("h (e p) d -> p (h e) d", p=EC)
                                 ).then_inc(c_in, 16)
                po.wait_ge(cp_ready, i * 2 + 2)
                po.sem_inc(waited, 1)
                po.dma_start(c_p[0, 0, ds(i, 1)].rearrange("h (e p) d -> p (h e) d", p=EC), c_new_p[0:EC]
                             ).then_inc(c_stored, 16)
                po.dma_start(n_p[0, 0, ds(i, 1)], n_new_p[0:1, :]).then_inc(c_stored, 16)
                for b in range(NB):
                    po.wait_ge(cn_ready, i * NB + b + 1)
                    po.sem_inc(waited, 1)
                    po.dma_start(c_s[0, b, ds(i, 1)].rearrange("h (e p) d -> p (h e) d", p=EC), cS[0:EC, b]
                                 ).then_inc(c_stored, 16)
                po.wait_ge(c_stored, i * (16 * (NB + 2)) + 16 * (NB + 2))
            po.wait_ge(head_free, H4 + 1)
            po.dma_start(n_s[0], nN[0:NB]).then_inc(stored, 16)
            po.wait_ge(rows_ready, 2)
            po.dma_start(pool_p[0, 0], u_rows[0:15, 0]).then_inc(stored, 16)
            for b in range(NB):
                po.dma_start(pool_s[0, b, 11:15, :], u_rows[NT * b:NT * b + NT, 1]).then_inc(stored, 16)
            n_stored[0] += NB + 2

        def project(pe, w, cols, m, b):
            for k in range(NK):
                for s in range(2):
                    mm = pe.matmul(ps[0:m, b + s, 0:HALF], w[:, k, cols:cols + m], h[:, k, HALF * s:HALF * s + HALF],
                                   start=(k == 0), stop=(k == NK - 1))
            return mm

        def project_tok(pe, out, w, lo, hi, t):
            for k in range(NK):
                mm = pe.matmul(out, h[:, k, 128 * t:128 * t + tok_tile(t)], w[:, k, lo:hi],
                               start=(k == 0), stop=(k == NK - 1))
            return mm

        def pe_even(pe):
            n = STEP_EVEN
            use_step(pe, n)
            pe.wait_ge(h_ready, NK * 2)
            w = slot(n, NK, 264)
            project(pe, w, 256, 4, 4)
            project(pe, w, 260, 4, 6).then_inc(e0_done, 1)
            project(pe, w, 0, 128, 0)
            project(pe, w, 128, 128, 2).then_inc(step_done, 1)
            pe.wait_ge(ein, 80)
            pe.wait_ge(gf_ready, 2)
            for c in range(2):
                mm = flip(pe, ps[:, 4, 128 * c:128 * c + 120], pool_rows[0:120, 128 * c:128 * c + 128])
            mm.then_inc(prefix_flip, 1)
            for hd in range(H4):
                for c in range(2):
                    mm = flip(pe, ps[0:EC, 5, (c * H4 + hd) * NB:(c * H4 + hd + 1) * NB], nS[0:NB, hd, EC * c:EC * c + EC])
            mm.then_inc(prefix_flip, 1)
            pe.wait_ge(wk_ready, 1)
            for t in range(KTILES):
                r = slice(128 * t, 128 * t + tok_tile(t))
                flip(pe, ps[0:tok_tile(t), 6, 4 * t:4 * t + 4], g_a[0:4, r])
                flip(pe, ps[0:tok_tile(t), 6, 32 + 4 * t:36 + 4 * t], g_wk[0:4, r])
            flip(pe, ps[0:NB, 6, 64:68], rows[0:4, 2 * T + TS:ROW]).then_inc(cols_flip, 1)
            pe.wait_ge(u_ready, 6)
            pe.wait_ge(prefix_ready, 2)
            pe.wait_ge(cols_ready, 2)
            with pe.Fori(0, H4) as i:
                pe_head(pe, i)
            pe.wait_ge(head_free, H4 + 1)
            pe.wait_ge(mixed_ready, 2)
            for c in range(2):
                for s in range(2):
                    mm = pe.matmul(ps[:, 2 * c + s, 0:HALF], wp_bd[:, c, :], mixed[:, c, HALF * s:HALF * s + HALF],
                                   start=True, stop=True)
            mm.then_inc(ypool_done, 1)
            for c in range(2):
                flip(pe, ps[0:15, 4, 128 * c:128 * c + 128], uep[:, c, SEQ:SEQ + 15])
                mm = flip(pe, ps[0:TS, 5, 128 * c:128 * c + 128], mixed_u(c))
            mm.then_inc(rows_done, 1)
            pe.wait_ge(ypool_ready, 2)
            pe.wait_ge(rows_ready, 2)
            rhs = [(128, ypool[:, c]) for c in range(2)] + [(EC, yml[0:EC, c]) for c in range(2 * H4)]
            with pe.Fori(0, 2) as i:
                for u in range(2):
                    pe_out(pe, 1, STEP_EOUT, u, i, rhs)

        def mixed_u(c):
            return u_last[:, c, :]

        u_last = G.take(2, TS)

        def pe_out(pe, q, base, u, i, rhs):
            n = base + u
            use_step(pe, n, i * 32)
            pe.wait_ge(down_free, DOWN_BASE[q] + u + 1 + i * 2)
            w = slot(n, len(rhs), 256)
            for c in range(2):
                for k, (rows_k, r) in enumerate(rhs):
                    for s in range(2):
                        mm = pe.matmul(ps[:, 4 * u + 2 * c + s, 0:HALF], w[0:rows_k, k, 128 * c:128 * c + 128],
                                       r[:, HALF * s:HALF * s + HALF], start=(k == 0), stop=(k == len(rhs) - 1))
            mm.then_inc(step_done, 1)

        def pe_head(pe, i):
            pe.wait_ge(cells_free, i + 1)
            use_step(pe, STEP_HEADS, i * 32)
            w = slot(STEP_HEADS, NK, 2 * DH)
            for c in range(2):
                mm = project(pe, w, DH + EC * c, EC, 4 + 2 * c)
            mm.then_inc(k_done, 1)
            pe.wait_ge(head_free, i + 1)
            for c in range(2):
                mm = project(pe, w, EC * c, EC, 2 * c)
            mm.then_inc(step_done, 1)
            use_step(pe, STEP_HEADS + 1, i * 32)
            w = slot(STEP_HEADS + 1, NK, 2 * DH)
            pe.wait_ge(qT_ready, i * 2 + 2)
            for t in range(KTILES):
                mm = project_tok(pe, ps[0:tok_tile(t), t // 2, DH * (t % 2):DH * (t % 2) + DH], w, 0, DH, t)
            mm.then_inc(v_done, 1)
            pe.wait_ge(rowh_ready, i + 1)
            pe.matmul(ps[:, 3, :], ones4, rows_h[0:4, 0:SEQ], start=True, stop=True).then_inc(mb_done, 1)
            pe.wait_ge(kT_ready, i * 2 + 2)
            for c in range(2):
                mm = project(pe, w, DH + EC * c, EC, 4 + 2 * c)
            mm.then_inc(step_done, 1)
            pe.wait_ge(v_ready, i * 2 + 2)
            for t in range(KTILES):
                for c in range(2):
                    mm = flip(pe, ps[0:tok_tile(t), t // 2, DH * (t % 2) + EC * c:DH * (t % 2) + EC * c + EC],
                              kT[0:EC, c, 128 * t:128 * t + tok_tile(t)])
            mm.then_inc(kflip_done, 1)
            pe.wait_ge(og_ready, i * 2 + 2)
            for j in range(4):
                for c in range(2):
                    mm = pe.matmul(ps[:, 4 + j, 128 * j:SEQ], kT[0:EC, c, 128 * j:128 * j + 128],
                                   qT[0:EC, c, 128 * j:SEQ], start=(c == 0), stop=(c == 1))
                mm.then_inc(s_done, 1)
            pe.wait_ge(kw_ready, i * 6 + 5)
            pe.matmul(ps[0:EC, 0, 32:64], ones4[:, 0:EC], rows_h[0:4, 2 * T:2 * T + TS], start=True, stop=True)
            pe.matmul(ps[0:EC, 0, 0:32], ones4[:, 0:EC], rows_h[0:4, SEQ:T], start=True, stop=True)
            pe.matmul(ps[0:EC, 0, 64:96], ones4[:, 0:EC], rows_h[0:4, T + SEQ:2 * T], start=True, stop=True)
            pe.matmul(ps[0:EC, 0, 96:104], ones4[:, 0:EC], rows_h[0:4, 2 * T + TS:ROW], start=True, stop=True)
            for c in range(2):
                mm = pe.matmul(ps[0:TS, 0, 128:160], kT[0:EC, c, SEQ:T], qT[0:EC, c, SEQ:T], start=(c == 0), stop=(c == 1))
            mm.then_inc(small_done, 1)
            pe.wait_ge(warg_ready, i * 4 + 4)
            pe.matmul(ps[0:EC, 3, :], ones4[:, 0:EC], rows_h[0:4, T:T + SEQ], start=True, stop=True).then_inc(mrow_done, 1)
            for c in range(2):
                for j in range(4):
                    if c == 0:
                        pe.wait_ge(sT_ready, i * 4 + j + 1)
                    mm = pe.matmul(ps[0:EC, 1 + c, 128 * j:SEQ], vtok[:, j, EC * c:EC * c + EC], wt[:, j, 128 * j:SEQ],
                                   start=(j == 0), stop=(j == 3))
            mm.then_inc(num_done, 1)
            for j in range(4):
                mm = pe.matmul(ps[0:EC, 4, 128 * j:SEQ], ones[:, 0:EC], wt[:, j, 128 * j:SEQ], start=(j == 0), stop=(j == 3))
            mm.then_inc(den_done, 1)
            for c in range(2):
                for j in range(4):
                    pe.matmul(ps[0:EC, 5, DH * c:DH * c + DH], vtok[:, j, EC * c:EC * c + EC], kw[:, j, :],
                              start=(j == 0), stop=(j == 3))
            for j in range(4):
                mm = pe.matmul(ps[0:1, 6, 0:DH], ones[:, 0:1], kw[:, j, :], start=(j == 0), stop=(j == 3))
            mm.then_inc(cp_done, 1)
            pe.wait_ge(c_in, i * (16 * NB) + 16 * NB)
            pe.wait_ge(den_used, i + 1)
            pe.wait_ge(cp_ready, i * 2 + 2)

            def c_flip(b):
                if b >= 2:
                    pe.wait_ge(cT_ready, i * NB + b - 1)
                for e in range(2):
                    for d in range(2):
                        mm = pe.matmul(ps[0:EC, 4 + b % 2, DH * d + EC * e:DH * d + EC * e + EC],
                                       cS[0:EC, b, e, EC * d:EC * d + EC], ident[0:EC, 0:EC], start=True, stop=True)
                mm.then_inc(ct_done, 1)

            pe.wait_ge(small_ready, i + 1)
            c_flip(0)
            for b in range(NB):
                if b + 1 < NB:
                    c_flip(b + 1)
                pe.wait_ge(cT_ready, i * NB + b + 1)
                for e in range(2):
                    for d in range(2):
                        pe.matmul(ps[0:EC, 0, 288 + 32 * e + NT * b:288 + 32 * e + NT * b + NT],
                                  cT[0:EC, b % 2, d, EC * e:EC * e + EC], qT[0:EC, d, SEQ + NT * b:SEQ + NT * b + NT],
                                  start=(d == 0), stop=(d == 1))
                if b == 0:
                    pe.wait_ge(kw_ready, i * 6 + 6)
                if b >= 2:
                    pe.wait_ge(cn_ready, i * NB + b - 1)
                if b == NB - 1:
                    pe.wait_ge(yp_ready, i * 2 + 2)
                for e in range(2):
                    mm = pe.matmul(ps[0:EC, 6 + b % 2, DH * e:DH * e + DH], vtok[0:TS, 4, EC * e:EC * e + EC],
                                   kwb[0:TS, b, :], start=True, stop=True)
                mm.then_inc(cn_done, 1)
            pe.matmul(ps[0:NB, 1, 0:DH], const("of_batch", TS), kw[0:TS, 4, :], start=True, stop=True)
            pe.wait_ge(ws_ready, i * 2 + 2)
            pe.wait_ge(qn_ready, i + 1)
            for c in range(2):
                pe.matmul(ps[0:EC, 0, 160 + 32 * c:192 + 32 * c], vtok[0:TS, 4, EC * c:EC * c + EC], wts[0:TS, :],
                          start=True, stop=True)
            pe.matmul(ps[0:EC, 0, 224:256], ones[0:TS, 0:EC], wts[0:TS, :], start=True, stop=True)
            for c in range(2):
                mm = pe.matmul(ps[0:EC, 0, 256:288], ones[0:EC, 0:EC], qn[0:EC, c, :], start=(c == 0), stop=(c == 1))
            mm.then_inc(sfin_done, 1)

        def act_even(act):
            act.wait_ge(gf_ready, 3)
            act.activation(g_e[0:4], g_x[0:4], ACT.Exp).then_inc(gl_ready, 1)
            act.wait_ge(gl_ready, 1)
            act.activation(g_l[0:4], g_e[0:4], ACT.Ln, bias=1.0).then_inc(gl_ready, 1)
            act.wait_ge(step_done, STEP_EVEN + 1)
            for c in range(2):
                for s, lo, hi, at in SEGS:
                    act.copy(uep[:, c, 15 + at:15 + at + hi - lo], ps[:, 2 * c + s, lo:hi]).then_inc(u_ready, 1)
                act.copy(ues[:, c, :, 15:15 + NT],
                         ps[:, 2 * c + 1, SPLIT:HALF].rearrange("p (b t) -> p b t", b=NB)).then_inc(u_ready, 1)
                act.copy(u_last[:, c, :], ps[:, 2 * c + 1, SPLIT:HALF])
            act.wait_ge(prefix_flip, 2)
            act.copy(ues[:, :, :, 0:15], ps[:, 4, 0:256].rearrange("p (c n) -> p c n", c=2)[:, :, 0:120]
                     .rearrange("p c (b r) -> p c b r", b=NB)).then_inc(prefix_ready, 1)
            act.copy(nT[0:EC].rearrange("p c h b -> p (c h b)"), ps[0:EC, 5, 0:2 * H4 * NB]).then_inc(prefix_ready, 1)
            act.wait_ge(wk_arg, 2)
            act.activation(rows[0:4, 2 * T:ROW], rows[0:4, 2 * T:ROW], ACT.Exp)
            act.activation(g_wk[0:4], g_wk[0:4], ACT.Exp).then_inc(wk_ready, 1)
            with act.Fori(0, H4) as i:
                act_head(act, i)
            act.wait_ge(ypool_done, 1)
            for c in range(2):
                act.activation(halves(ypool[:, c]), banks(2 * c), ACT.Copy,
                               scale=vecs[:, V_POOL + c:V_POOL + c + 1]).then_inc(ypool_ready, 1)
            act.wait_ge(rows_done, 1)
            act.copy(u_rows[0:15, 0], ps[0:15, 4, 0:256]).then_inc(rows_ready, 1)
            act.copy(u_rows[0:TS, 1], ps[0:TS, 5, 0:256]).then_inc(rows_ready, 1)

        def act_head(act, i):
            act.wait_ge(k_done, i + 1)
            for c in range(2):
                act.mul(halves(kT[0:EC, c]), banks(4 + 2 * c, EC), DH ** -0.5).then_inc(kT_ready, 1)
            act.wait_ge(step_done, STEP_HEADS + 1 + i * 2)
            for c in range(2):
                act.copy(halves(qT[0:EC, c]), banks(2 * c, EC)).then_inc(qT_ready, 1)
            act.wait_ge(v_done, i + 1)
            act.copy(vtok[:, 0:4].rearrange("p (b t) d -> p b (t d)", b=2), ps[:, 0:2, 0:2 * DH]).then_inc(v_ready, 1)
            act.copy(vtok[0:TS, 4], ps[0:TS, 2, 0:DH]).then_inc(v_ready, 1)
            act.wait_ge(step_done, STEP_HEADS + 2 + i * 2)
            for c in range(2):
                act.activation(halves(ogT[0:EC, c]), banks(4 + 2 * c, EC), ACT.Sigmoid).then_inc(og_ready, 1)
            for j in range(4):
                act.wait_ge(warg_ready, i * 4 + j + 1)
                act.activation(wt[:, j, 128 * j:SEQ], wt[:, j, 128 * j:SEQ], ACT.Exp, scale=-1.0).then_inc(w_ready, 1)
            act.wait_ge(mrow_done, i + 1)
            act.activation(em, ps[0:EC, 3, :], ACT.Exp, scale=-1.0).then_inc(em_ready, 1)
            act.wait_ge(small_ready, i + 1)
            act.activation(em_s[0:EC], small[0:EC, 64:96], ACT.Exp, scale=-1.0).then_inc(em_ready, 1)
            act.wait_ge(wsarg_ready, i + 1)
            act.activation(wts[0:TS], wts[0:TS], ACT.Exp, scale=-1.0).then_inc(ws_ready, 1)
            act.wait_ge(cp_done, i + 1)
            act.wait_ge(c_in, i * (16 * NB) + 16 * NB)
            act.copy(c_new_p[0:EC], ps[0:EC, 5, 0:2 * DH].rearrange("p (e d) -> p e d", e=2)).then_inc(cp_ready, 1)
            act.copy(n_new_p[0:1], ps[0:1, 6, 0:DH]).then_inc(cp_ready, 1)
            for b in range(NB):
                act.wait_ge(ct_done, i * NB + b + 1)
                if b >= 2:
                    act.wait_ge(cn_done, i * NB + b - 1)
                act.copy(cT[0:EC, b % 2], ps[0:EC, 4 + b % 2, 0:2 * DH].rearrange("p (e d) -> p e d", e=2)
                         ).then_inc(cT_ready, 1)

        def dve_even(dve, C):
            dve.wait_ge(e0_done, 1)
            dve.wait_ge(ein, 80)
            dve.tensor_scalar(halves(g_i[0:4]), banks(4, 4), b_i[0:4], None, ALU.add).then_inc(gf_ready, 1)
            dve.tensor_scalar(halves(g_f[0:4]), banks(6, 4), b_f[0:4], None, ALU.add).then_inc(gf_ready, 1)
            dve.wait_ge(gf_ready, 2)
            dve.scalar_tensor_tensor(out=g_x[0:4], in0=g_f[0:4], scalar=-1.0, in1=g_f[0:4],
                                     op0=ALU.mult, op1=ALU.min).then_inc(gf_ready, 1)
            dve.wait_ge(gl_ready, 2)
            C.after(dve.scalar_tensor_tensor(out=g_f[0:4], in0=g_f[0:4], scalar=0.0, in1=g_l[0:4],
                                             op0=ALU.min, op1=ALU.subtract))
            fs, bs = (v[0:4, SEQ:T].rearrange("p (b t) -> p b t", b=NB) for v in (g_f, g_e))
            C.after(dve.memset(ones_row, 1.0))
            C.after(dve.tensor_tensor_scan(g_e[0:4, 0:SEQ], ones_row, g_f[0:4, 0:SEQ], 0.0, ALU.mult, ALU.add))
            C.after(dve.tensor_copy(bs[:, :, 0], fs[:, :, 0]))
            for t in range(1, NT):
                C.after(dve.tensor_tensor(bs[:, :, t], bs[:, :, t - 1], fs[:, :, t], ALU.add))
            C.after(dve.tensor_tensor(g_a[0:4], g_i[0:4], g_e[0:4], ALU.subtract))
            M, m, ga = rows[0:4, 0:T], rows[0:4, T:2 * T], rows[0:4, 2 * T:2 * T + TS]
            Ms, as_ = (v.rearrange("p (b t) -> p b t", b=NB) for v in (M[:, SEQ:T], g_a[0:4, SEQ:T]))
            C.after(dve.tensor_tensor_scan(M[:, 0:SEQ], g_a[0:4, 0:SEQ], g_a[0:4, 0:SEQ], 0.0, ALU.max, ALU.max))
            C.after(dve.tensor_tensor(Ms[:, :, 0], m0[0:4], as_[:, :, 0], ALU.max))
            for t in range(1, NT):
                C.after(dve.tensor_tensor(Ms[:, :, t], Ms[:, :, t - 1], as_[:, :, t], ALU.max))
            C.after(dve.tensor_tensor(m, g_e[0:4], M, ALU.add))
            dve.tensor_copy(m_out[0:4], rows[0:4, T + SEQ + 3:2 * T:4]).then_inc(mout_ready, 1)
            for t in range(NT):
                dve.tensor_tensor(ga.rearrange("p (b t) -> p b t", b=NB)[:, :, t], m0[0:4], Ms[:, :, t], ALU.subtract)
            dve.tensor_tensor(rows[0:4, 2 * T + TS:ROW], m0[0:4], Ms[:, :, 3], ALU.subtract)
            dve.tensor_scalar(g_wk[0:4, 0:SEQ], g_a[0:4, 0:SEQ], M[:, SEQ - 1:SEQ], None, ALU.subtract).then_inc(wk_arg, 1)
            dve.tensor_tensor(g_wk[0:4, SEQ:T].rearrange("p (b t) -> p b t", b=NB), as_,
                              Ms[:, :, 3].unsqueeze(2).broadcast_to([4, NB, NT]), ALU.subtract).then_inc(wk_arg, 1)
            dve.wait_ge(cols_flip, 1)
            dve.tensor_copy(acol.rearrange("p t h -> p (t h)")[:, 0:16], ps[:, 6, 0:16])
            dve.tensor_copy(acol[0:TS, 4], ps[0:TS, 6, 16:20])
            dve.tensor_copy(wkcol.rearrange("p t h -> p (t h)")[:, 0:16], ps[:, 6, 32:48]).then_inc(cols_ready, 1)
            dve.tensor_copy(wkcol[0:TS, 4], ps[0:TS, 6, 48:52])
            dve.tensor_copy(dec_b[0:NB], ps[0:NB, 6, 64:68]).then_inc(cols_ready, 1)
            dve.wait_ge(cols_ready, 2)
            dve.sem_inc(head_free, 1)
            dve.sem_inc(cells_free, 1)
            per = 20
            with dve.Fori(0, H4) as i:
                C.loop(i, per, lambda: dve_head(dve, C, i))
            C.skip(per * (H4 - 1))
            dve.wait_ge(ypool_ready, 2)
            dve.wait_ge(rows_ready, 2)
            dve.sem_inc(down_free, 2)
            dve_add(dve, 1, STEP_EOUT, 1, 1.0)

        def dve_head(dve, C, i):
            late, late_s = const("late"), const("late_s", TS)
            dve.tensor_scalar(rows_h[0:4], rows[0:4], head4[:, ds(i, 1)], None, ALU.mult).then_inc(rowh_ready, 1)
            dve.wait_ge(mb_done, i + 1)
            for j in range(4):
                a = acol[:, j, ds(i, 1)]
                dve_w = dve.scalar_tensor_tensor(out=wt[:, j, 128 * j:128 * j + 128], in0=ps[:, 3, 128 * j:128 * j + 128],
                                                 scalar=a, in1=late, op0=ALU.subtract, op1=ALU.max)
                if j < 3:
                    dve_w = dve.tensor_scalar(wt[:, j, 128 * j + 128:SEQ], ps[:, 3, 128 * j + 128:SEQ], a, 0.0,
                                              ALU.subtract, ALU.max)
                dve_w.then_inc(warg_ready, 1)
            dve.wait_ge(kflip_done, i + 1)
            for t in range(KTILES):
                r = tok_tile(t)
                dve.tensor_scalar(kw[0:r, t], ps[0:r, t // 2, DH * (t % 2):DH * (t % 2) + DH],
                                  wkcol[0:r, t, ds(i, 1)], None, ALU.mult).then_inc(kw_ready, 1)
            for j in range(4):
                dve.wait_ge(w_ready, i * 4 + j + 1)
                dve.wait_ge(s_done, i * 4 + j + 1)
                dve.tensor_tensor(wt[:, j, 128 * j:SEQ], wt[:, j, 128 * j:SEQ], ps[:, 4 + j, 128 * j:SEQ],
                                  ALU.mult).then_inc(sT_ready, 1)
            dve.wait_ge(small_done, i + 1)
            C.after(dve.tensor_copy(small[0:EC, 0:104], ps[0:EC, 0, 0:104]))
            dve.tensor_copy(small[0:TS, 128:160], ps[0:TS, 0, 128:160]).then_inc(small_ready, 1)
            dve.wait_ge(small_ready, i + 1)
            dve.scalar_tensor_tensor(out=wts[0:TS], in0=small[0:TS, 0:32], scalar=acol[0:TS, 4, ds(i, 1)], in1=late_s,
                                     op0=ALU.subtract, op1=ALU.max).then_inc(wsarg_ready, 1)
            dve.wait_ge(kw_ready, i * 6 + 5)
            dve.tensor_tensor(kwb[0:TS], kw[0:TS, 4].unsqueeze(1).broadcast_to([TS, NB, DH]),
                              const("of_batch", TS).unsqueeze(2).broadcast_to([TS, NB, DH]), ALU.mult
                              ).then_inc(kw_ready, 1)
            for c in range(2):
                q = dve.tensor_tensor(qn[0:EC, c].rearrange("p (b t) -> p b t", b=NB),
                                      qT[0:EC, c, SEQ:T].rearrange("p (b t) -> p b t", b=NB),
                                      nT[0:EC, c, ds(i, 1)].rearrange("p h b -> p (h b)").unsqueeze(2)
                                      .broadcast_to([EC, NB, NT]), ALU.mult)
                if c == 1:
                    q.then_inc(qn_ready, 1)
                else:
                    C.after(q)
            dve.wait_ge(ws_ready, i * 2 + 1)
            dve.tensor_tensor(wts[0:TS], wts[0:TS], small[0:TS, 128:160], ALU.mult).then_inc(ws_ready, 1)
            dve.wait_ge(em_ready, i * 2 + 1)
            dve.wait_ge(den_done, i + 1)
            C.after(dve.tensor_tensor(rden, ps[0:EC, 4, :], em, ALU.max))
            dve.scalar_tensor_tensor(out=rden, in0=ps[0:EC, 4, :], scalar=-1.0, in1=rden, op0=ALU.mult,
                                     op1=ALU.max).then_inc(den_used, 1)
            dve.wait_ge(den_used, i + 1)
            C.after(dve.reciprocal(rden, rden))
            for c in range(2):
                y = yml[0:EC, ds(i * 2 + c, 1), 0:SEQ].rearrange("p a t -> p (a t)")
                C.after(dve.tensor_tensor(ogT[0:EC, c, 0:SEQ], ogT[0:EC, c, 0:SEQ], rden, ALU.mult))
                dve.tensor_tensor(y, ogT[0:EC, c, 0:SEQ], ps[0:EC, 1 + c, :], ALU.mult).then_inc(yp_ready, 1)
            for b in range(NB):
                dve.wait_ge(cn_done, i * NB + b + 1)
                dve.scalar_tensor_tensor(out=cS[0:EC, b], in0=cS[0:EC, b], scalar=dec_s[0:EC, b:b + 1],
                                         in1=ps[0:EC, 6 + b % 2, 0:2 * DH].rearrange("p (e d) -> p e d", e=2),
                                         op0=ALU.mult, op1=ALU.add).then_inc(cn_ready, 1)
            dve.wait_ge(cn_ready, i * NB + NB)
            dve.sem_inc(cells_free, 1)
            dve.wait_ge(sfin_done, i + 1)
            nh = nS[0:NB, ds(i, 1)].rearrange("p a d -> p (a d)")
            C.after(dve.scalar_tensor_tensor(out=nN[0:NB, ds(i, 1)].rearrange("p a d -> p (a d)"), in0=nh,
                                             scalar=dec_b[0:NB, ds(i, 1)], in1=ps[0:NB, 1, 0:DH],
                                             op0=ALU.mult, op1=ALU.add))
            C.after(dve.tensor_tensor(den_s[0:EC], a_s[0:EC], ps[0:EC, 0, 256:288], ALU.mult))
            C.after(dve.tensor_tensor(den_s[0:EC], den_s[0:EC], ps[0:EC, 0, 224:256], ALU.add))
            dve.wait_ge(em_ready, i * 2 + 2)
            C.after(dve.tensor_tensor(em_s[0:EC], em_s[0:EC], den_s[0:EC], ALU.max))
            C.after(dve.scalar_tensor_tensor(out=den_s[0:EC], in0=den_s[0:EC], scalar=-1.0, in1=em_s[0:EC],
                                             op0=ALU.mult, op1=ALU.max))
            C.after(dve.reciprocal(den_s[0:EC], den_s[0:EC]))
            for c in range(2):
                u = acc_s[0:EC, c]
                C.after(dve.tensor_tensor(u, a_s[0:EC], ps[0:EC, 0, 288 + 32 * c:320 + 32 * c], ALU.mult))
                C.after(dve.tensor_tensor(u, u, ps[0:EC, 0, 160 + 32 * c:192 + 32 * c], ALU.add))
                C.after(dve.tensor_tensor(u, u, den_s[0:EC], ALU.mult))
                y = yml[0:EC, ds(i * 2 + c, 1), SEQ:T].rearrange("p a t -> p (a t)")
                C.after(dve.tensor_tensor(y, u, ogT[0:EC, c, SEQ:T], ALU.mult))
            dve.sem_inc(head_free, 1)

        ones_row = ns[0:4, 2 * T:2 * T + SEQ]

        A, G = Arena(arena_t, A_SIZE), Arena(pages_t, G_SIZE)
        kvtok = A.take(KTILES, 6 * 128)
        ktS, ktW = A.take(T), A.take(T)
        gts = A.take(KTILES, 3 * NH)
        yconv = A.take(2, T)
        oT = A.take(GQ, T)
        qB = A.take(NB, 64)
        cmp_a = A.take(2, 9)
        cmp_bd = A.take(2, 128)
        k_bias, v_bias = A.take(1), A.take(128)
        kcT_p, vc_p = A.take(32), A.take(128)
        imp, score, score2, top8 = A.take(132), A.take(NBLK), A.take(NBLK), A.take(8)
        blk_add = A.take(NBLK)
        mx, rs, gs, mx_p, rs_p, coef = A.take(3), A.take(3), A.take(3), A.take(2, 2), A.take(2, 2), A.take(2, 2)
        A_TAIL = A.at
        qTp = A.take(2, SEQ)
        ptS, ptW = A.take(2, SEQ), A.take(2, SEQ)
        mc, o1 = A.take(2, 4), A.take(HD)
        sP = ns[:, 0:4 * SEQ].rearrange("p (u b k) -> p u b k", u=2, b=2)
        sc_p = ns[:, 4 * SEQ:4 * SEQ + 2 * 128].rearrange("p (g j n) -> p g j n", g=2, j=4)
        half_ring = lambda i: ring[:, i, SLOT // 2:SLOT]
        otok = [half_ring(i)[:, 0:2 * 6 * 128].rearrange("p (j n) -> p j n", j=2) for i in range(2)]
        ptC = half_ring(0)[0:32, 1536:2048].rearrange("p (j q) -> p j q", j=4)
        ptC2 = half_ring(1)[0:32, 1536:2048].rearrange("p (j q) -> p j q", j=4)
        A2 = Arena(arena_t, A_SIZE)
        A2.at = A_TAIL
        qP, eP, g36, pcS = A2.take(2, 64), A2.take(128), A2.take(NH, 3), A2.take(128)
        o_s = A2.take(128)
        BAND = 8 * (NPG - 1) - 1
        band = A2.take(2, BAND + 1 + 128)
        pre_k = A2.take(2, 2, 128)
        hflat = h[:, :, :].rearrange("p c t -> p (c t)")
        H = Arena(hflat, NK * T)
        pT = H.take(23, 128)
        preS, kcS, vcS = H.take(2, 256), H.take(2, 128), H.take(2, 128)
        sS, sW = ns[:, 0:PAST + TS], ns[:, PAST + TS:PAST + TS + 512 + TS]
        ktc = [half_ring(0)[:, 1024 * i:1024 * i + 1024].rearrange("p (b k) -> p b k", b=2) for i in range(2)]
        pages = pages_t[:, :].rearrange("p (b g n) -> p b g n", b=2, g=NPG)
        cvp, cvs = G.take(2, 2 + SEQ), G.take(2, NB, 2 + NT)
        bgT, cgT = G.take(2, T), G.take(2, T)
        cv_t = G.take(T)
        cs_rows, c_rows = G.take(256), G.take(2, 256)
        pre_p = G.take(64)

        cm_in = sem("cm_in")
        table_keys_in = sem("table_keys_in")
        kv_ready, gt_ready, bg_ready, cg_done, cg_ready = (sem(n) for n in (
            "kv_ready", "gt_ready", "bg_ready", "cg_done", "cg_ready"))
        cu_ready, conv_ready = sem("cu_ready"), sem("conv_ready")
        ktf_done, kt_ready = sem("ktf_done"), sem("kt_ready")
        pre_done, pre_ready, kc_done, kc_ready, vc_ready = (sem(n) for n in (
            "pre_done", "pre_ready", "kc_done", "kc_ready", "vc_ready"))
        qp_ready, scmp_done, scmp_neg, scmp_exp, scmp_ready, tcmp_done, ptc_ready = (sem(n) for n in (
            "qp_ready", "scmp_done", "scmp_neg", "scmp_exp", "scmp_ready", "tcmp_done", "ptc_ready"))
        sc_done, sc_free, neg_ready, exp_ready, t_done = (sem(n) for n in (
            "sc_done", "sc_free", "neg_ready", "exp_ready", "t_done"))
        pts_ready, ptw_ready, pv_done, o_used = sem("pts_ready"), sem("ptw_ready"), sem("pv_done"), sem("o_used")
        chunk_free, of_done, of_ready = sem("chunk_free"), sem("of_done"), sem("of_ready")
        pair_free = sem("pair_free")
        cmp_in, selk_in, selv_in, win_in = sem("cmp_in"), sem("selk_in"), sem("selv_in"), sem("win_in")
        qP_ready = sem("qP_ready")
        scs_done, negc_ready, expc_ready, pc_ready, imp_done = (sem(n) for n in (
            "scs_done", "negc_ready", "expc_ready", "pc_ready", "imp_done"))
        tk_done, ktc_ready, sk_done, sk_ready, new_done = (sem(n) for n in (
            "tk_done", "ktc_ready", "sk_done", "sk_ready", "new_done"))
        negs_ready, exps_ready, tp_done, pTa_ready, pTv_ready = (sem(n) for n in (
            "negs_ready", "exps_ready", "tp_done", "pTa_ready", "pTv_ready"))
        pvs_done, os_ready, ot_done = sem("pvs_done"), sem("os_ready"), sem("ot_done")

        def load_odd(sp):
            w = w_in_odd[0].rearrange("(k p) n -> p k n", p=128)
            for u in range(2):
                n = STEP_ODD + u
                v = slot(n, NK, 384)
                a = 768 + 384 * u
                load(sp, n, [(v[:, :, 0:192], w[:, :, a:a + 192]), (v[:, :, 192:384], w[:, :, a + 192:a + 384])],
                     0, 3 * PART - 2 + 2 * u)
            n = STEP_ODD + 2
            v = slot(n, NK, 292)
            load(sp, n, [(v[:, :, 0:36], w[:, :, 1536:1572]), (v[:, :, 36:292], w[:, :, 1572:1828])])
            n = STEP_ODD + 3
            v = slot(n, NK, 512)
            load(sp, n, [(v[:, :, 0:256], w[:, :, 1828:2084]), (v[:, :, 256:512], w[:, :, 2084:2340])])
            with sp.Fori(0, 3) as i:
                for u in range(2):
                    n = STEP_Q + u
                    v = slot(n, NK, 128)
                    load(sp, n, [(v[:, :, 64 * g:64 * g + 64], w[:, :, ds(i * 128 + 64 * u + 384 * g, 64)])
                                 for g in range(2)], i * 2)
            load_keys(sp)
            wo = w_out_odd[0]
            wh = wo[0:768].rearrange("(g i p) n -> g p i n", g=2, i=GQ)
            with sp.Fori(0, 2) as i:
                for u in range(2):
                    n = STEP_OOUT + u
                    v = slot(n, 8, 256)
                    at = i * 512 + 256 * u
                    load(sp, n, [(v[64 * g:64 * g + 64, 0:GQ], wh[g][:, :, ds(at, 256)]) for g in range(2)], i * 2)
                    sp.dma_start(v[:, GQ:8], wo[768:D].rearrange("(k p) n -> p k n", p=128)[:, :, ds(at, 256)]
                                 ).then_inc(oconv_in[n % 2], 16)

        oconv_in = [sem("oconv_in_0"), sem("oconv_in_1")]

        def pool_odd(po, C):
            po.wait_ge(h_ready, NK * 5)
            for z in (cmp_a[:, :, :], cmp_bd[:, :, :], qB[:, :, :], imp[:, :], cvp[:, :, 0:2]):
                mz = po.memset(z, 0.0)
                mz.then_inc(zeroed, 1)
            po.wait_ge(zeroed, 7)
            n = 0
            for kv in range(2):
                for c in range(9):
                    lo, hi = max(0, 16 * (c - 1)), min(128, 16 * (c - 1) + 32)
                    j = lo - 16 * (c - 1)
                    po.dma_start(cmp_a[lo:hi, kv, c:c + 1],
                                 cmp_pos_w[0, kv, j:j + hi - lo].rearrange("(j o) -> j o", o=1)).then_inc(cm_in, 16)
                for g in range(2):
                    r = slice(64 * g, 64 * g + 64)
                    po.dma_start(cmp_bd[r, kv, r], cmp_w[0, kv]).then_inc(cm_in, 16)
            for g in range(2):
                r = slice(64 * g, 64 * g + 64)
                po.dma_start(k_bias[r], cmp_b[0, 0].rearrange("(d o) -> d o", o=1)).then_inc(cm_in, 16)
                po.dma_start(v_bias[:, r], cmp_b[0, 1:2, :].broadcast_to([128, HD])).then_inc(cm_in, 16)
            po.dma_start(cs_rows[0:2 * NB], state_conv[0].rearrange("b j n -> (b j) n")).then_inc(cm_in, 16)
            po.dma_start(pt[:, :], page_table.rearrange("(o b) g -> o (b g)", o=1)).then_inc(table_keys_in, 16)
            po.dma_start(win_s[0, :, 0:508].rearrange("b k r g d -> b k (r g d)"),
                         state_win_kv[0, :, 4:512].rearrange("b k r g d -> b k (r g d)")).then_inc(stored, 16)
            po.wait_ge(kv_ready, 10)
            po.dma_start(kv_rows_p[0, 0].rearrange("(t p) r g d -> p t (r g d)", p=128), kvtok[:, 0:4, 0:512]).then_inc(stored, 16)
            po.dma_start(kv_rows_s[0].rearrange("b t r g d -> (b t) (r g d)"), kvtok[0:TS, 4, 0:512]).then_inc(stored, 16)
            po.dma_start(win_p[0, 0].rearrange("(t p) r g d -> p t (r g d)", p=128), kvtok[:, 0:4, 512:768]).then_inc(stored, 16)
            for b in range(NB):
                po.dma_start(win_s[0, b, 508:512].rearrange("k r g d -> k (r g d)"),
                             kvtok[NT * b:NT * b + NT, 4, 512:768]).then_inc(stored, 16)
            n_stored[0] += 4 + NB
            po.wait_ge(cu_ready, 2)
            po.wait_ge(prefix_ready, 3)
            po.wait_ge(bg_ready, 2)
            for c in range(2):
                tap = lambda j: vecs[:, V_CONV + 2 * j + c:V_CONV + 2 * j + c + 1]
                y, t = yconv[:, c], cv_t
                for o, tmp, e, w in ((y[:, 0:SEQ], t[:, 0:SEQ], cvp[:, c], SEQ),
                                     (y[:, SEQ:T].rearrange("p (b t) -> p b t", b=NB),
                                      t[:, SEQ:T].rearrange("p (b t) -> p b t", b=NB), cvs[:, c], NT)):
                    C.after(po.tensor_scalar(o, e[..., 0:w], tap(0), None, ALU.mult))
                    for j in (1, 2):
                        C.after(po.tensor_scalar(tmp, e[..., j:j + w], tap(j), None, ALU.mult))
                        C.after(po.tensor_tensor(o, o, tmp, ALU.add))
                po.tensor_tensor(y, y, bgT[:, c], ALU.mult).then_inc(conv_ready, 1)
            po.wait_ge(rows_ready, 4)
            po.dma_start(conv_p[0, 0], c_rows[0:2, 0]).then_inc(crow_stored, 16)
            po.dma_start(conv_s[0].rearrange("b j n -> (b j) n"), c_rows[0:2 * NB, 1]).then_inc(crow_stored, 16)
            po.wait_ge(crow_stored, 32)
            po.wait_ge(conv_ready, 2)
            po.wait_ge(pre_ready, 1)
            po.wait_ge(kc_ready, 1)
            po.wait_ge(vc_ready, 1)
            po.wait_ge(table_keys_in, 16)
            load_pages(po, 0, 256, 384, table_keys_in, (1,))
            load_pages(po, 0, 384, 512, selv_in)
            po.wait_ge(pair_free, 1)
            load_windows(po, 0)
            with po.Fori(0, NB // 2 - 1) as i:
                po.wait_ge(tk_done, i * 5 + 4)
                po.sem_inc(waited, 1)
                load_pages(po, i + 1, 256, 384, table_keys_in, (1,))
                po.wait_ge(pvs_done, i + 1)
                po.sem_inc(waited, 1)
                load_windows(po, i + 1)
                load_pages(po, i + 1, 384, 512, selv_in)

        def load_pages(eng, i, lo, hi, landed, of=(0, 1)):
            for b in of:
                for g in range(NPG):
                    page = eng.value_load(pt[0:1, ds(i * (2 * NPG) + (b * NPG + g), 1)], min_val=0,
                                          max_val=cache_nsa_kv.shape[1] - 1)
                    eng.dma_start(pages[:, b, g, lo:hi],
                                  cache_nsa_kv[0, ds(page, 1)].rearrange("a k r g d -> (a k) (r g d)")[:, lo:hi]
                                  ).then_inc(landed, 16)

        def load_windows(po, i):
            for b in range(2):
                po.dma_start(wst_[:, b], state_win_kv[0, ds(i * 2 + b, 1)].rearrange(
                    "a (t p) r g d -> p (a t) (r g d)", p=128)).then_inc(win_in, 16)

        def load_keys(sp):
            for s, n in ((crow_stored, 32), (conv_ready, 2), (pre_ready, 1), (kc_ready, 1), (vc_ready, 1), (table_keys_in, 16)):
                sp.wait_ge(s, n)
            load_pages(sp, 0, 0, 256, cmp_in)
            load_pages(sp, 0, 256, 384, selk_in, (0,))
            with sp.Fori(0, NB // 2 - 1) as i:
                sp.wait_ge(sums_done, i + 1)
                sp.sem_inc(waited, 1)
                load_pages(sp, i + 1, 0, 256, cmp_in)
                sp.wait_ge(tk_done, i * 5 + 4)
                sp.sem_inc(waited, 1)
                load_pages(sp, i + 1, 256, 384, selk_in, (0,))

        crow_stored = sem("crow_stored")
        wst_ = half_ring(1).rearrange("p (b t n) -> p b t n", b=2, t=4)
        PAGES = 16 * 2 * NPG

        def compress(pe, b, at, src, rows_pages, kv, cols):
            pe.matmul(ps[:, b, at:at + cols], ident, zeros[:, 0:cols], start=True, stop=False, skip_group_check=True)
            for p in range(rows_pages):
                lo = 1 if p == 0 else 0
                hi = 8 if p == rows_pages - 1 else 9
                mm = pe.matmul(ps[:, b, at + 8 * p - 1 + lo:at + 8 * p - 1 + hi], src(p), cmp_a[:, kv, lo:hi],
                               start=False, stop=(p == rows_pages - 1), skip_group_check=True)
            return mm

        zeros = const("zeros")

        def pe_odd(pe):
            pe.wait_ge(h_ready, NK * 5)
            for u in range(2):
                n = STEP_ODD + u
                use_step(pe, n)
                w = slot(n, NK, 384)
                for t in range(KTILES):
                    if u == 1 and t == 3:
                        pe.wait_ge(kv_ready, 2)
                    mm = project_tok(pe, ps[0:tok_tile(t), (5 * u + t) % 8, 0:384], w, 0, 384, t)
                mm.then_inc(step_done, 1)
            pe.wait_ge(kv_ready, 10)
            n = STEP_ODD + 2
            use_step(pe, n)
            w = slot(n, NK, 292)
            for t in range(KTILES):
                project_tok(pe, ps[0:tok_tile(t), 7, 36 * t:36 * t + 36], w, 0, 36, t)
            for c in range(2):
                mm = project(pe, w, 36 + 128 * c, 128, 2 * c)
            mm.then_inc(step_done, 1)
            n = STEP_ODD + 3
            use_step(pe, n)
            w = slot(n, NK, 512)
            project(pe, w, 0, 128, 4)
            pe.wait_ge(gt_ready, 1)
            project(pe, w, 128, 128, 6).then_inc(cg_done, 1)
            for c in range(2):
                pe.wait_ge(bg_ready, c + 1)
                mm = project(pe, w, 256 + 128 * c, 128, 2 * c)
            mm.then_inc(step_done, 1)
            pe.wait_ge(cg_ready, 2)
            for b, at in ((4, 256), (6, 512)):
                for t in range(4):
                    flip(pe, ps[:, b, 128 * t:128 * t + 128], kvtok[:, t, at:at + 128])
                mm = flip(pe, ps[:, b + 1, 0:TS], kvtok[0:TS, 4, at:at + 128])
            mm.then_inc(ktf_done, 1)
            pe.wait_ge(cu_ready, 2)
            pe.wait_ge(cm_in, 16 * 27)
            for c in range(2):
                mm = flip(pe, ps[:, 0, 16 * c:16 * c + 16], cs_rows[0:2 * NB, 128 * c:128 * c + 128])
            mm.then_inc(prefix_flip, 1)
            for kv in range(2):
                mm = compress(pe, 1, 32 * kv, lambda p: kvtok[:, p, 128 * kv:128 * kv + 128], 4, kv, 32)
            mm.then_inc(pre_done, 1)
            pe.wait_ge(kt_ready, 4)
            for c in range(2):
                flip(pe, ps[0:2, 4, 128 * c:128 * c + 128], cvp[:, c, SEQ:SEQ + 2])
            for c in range(2):
                mm = flip(pe, ps[0:2 * NB, 5, 128 * c:128 * c + 128], cv_last[:, c, :])
            mm.then_inc(rows_done, 1)
            pe.wait_ge(pre_ready, 1)
            pe.matmul(ps[:, 2, 0:32], cmp_bd[:, 0], pre_p[:, 0:32], start=True, stop=True)
            pe.matmul(ps[0:32, 3, 0:128], pre_p[:, 32:64], cmp_bd[:, 1], start=True, stop=True).then_inc(kc_done, 1)
            pe.wait_ge(rows_ready, 4)
            pe.wait_ge(kc_ready, 1)
            pe.wait_ge(vc_ready, 1)
            with pe.Fori(0, 3) as i:
                for u in range(2):
                    pe_queries(pe, i, u)
            pe.wait_ge(o_used, 49)
            for j in range(4):
                if j >= 2:
                    pe.wait_ge(of_ready, j - 1)
                for c in range(GQ):
                    mm = flip(pe, ps[:, 2 * (j % 2) + c // 4, 128 * (c % 4):128 * (c % 4) + 128],
                              otok[j // 2][:, j % 2, 128 * c:128 * c + 128])
                mm.then_inc(of_done, 1)
            pe.wait_ge(of_ready, 4)
            pe.wait_ge(pair_free, 1)
            pe_compress_pair(pe, 0)
            with pe.Fori(0, NB // 2 - 1) as i:
                pe_pair(pe, i)
            pe_pair(pe, NB // 2 - 1, last=True)
            pe.wait_ge(pair_free, NB // 2 + 1)
            pe.wait_ge(conv_ready, 2)
            rhs = [(128, oT[:, c]) for c in range(GQ)] + [(128, yconv[:, c]) for c in range(2)]
            with pe.Fori(0, 2) as i:
                for u in range(2):
                    pe.wait_ge(oconv_in[(STEP_OOUT + u) % 2], i * 16 + 16)
                    pe_out(pe, 4, STEP_OOUT, u, i, rhs)

        cv_last = G.take(2, 2 * NB)

        def pe_queries(pe, i, u):
            n = STEP_Q + u
            use_step(pe, n, i * 32)
            w = slot(n, NK, 128)
            pe.wait_ge(pts_ready, i * 16 + 8 * u + 1)
            pe.wait_ge(ptw_ready, i * 16 + 8 * u + 1)
            project(pe, w, 0, 128, 4).then_inc(step_done, 1)
            pe.wait_ge(qp_ready, i * 8 + 4 * u + 4)
            pe.wait_ge(o_used, i * 16 + 8 * u + 1)
            q = lambda g, j: qTp[64 * g:64 * g + 64, u, 128 * j:128 * j + 128]
            for g in range(2):
                for j in range(4):
                    mm = pe.matmul(ps[:, 6 + g, 32 * j:32 * j + 32], q(g, j), kcT_p[64 * g:64 * g + 64, :],
                                   start=True, stop=True)
                mm.then_inc(scmp_done, 1)

            def scores(k):
                g, j = k // 4, k % 4
                pe.wait_ge(sc_free, i * 16 + 8 * u + k + 1)
                pe.matmul(ps[:, 2 * (k % 2), 0:128 * j + 128], q(g, j), ktS[64 * g:64 * g + 64, 0:128 * j + 128],
                          start=True, stop=True)
                pe.matmul(ps[:, 2 * (k % 2) + 1, 0:128 * j + 128], q(g, j), ktW[64 * g:64 * g + 64, 0:128 * j + 128],
                          start=True, stop=True).then_inc(sc_done, 1)

            scores(0)
            scores(1)

            def flip_compressed():
                for g in range(2):
                    pe.wait_ge(scmp_ready, i * 4 + 2 * u + g + 1)
                    for j in range(4):
                        mm = pe.matmul(ps[0:32, 6 + g, 128 * j:128 * j + 128], sc_p[:, g, j, :], ident, start=True, stop=True)
                    mm.then_inc(tcmp_done, 1)
            def weigh(k):
                g, j = k // 4, k % 4
                o = 6 + k % 2
                if k == 0:
                    pe.wait_ge(ptc_ready, i * 4 + 2 * u + 2)
                else:
                    pe.wait_ge(o_used, i * 16 + 8 * u + k)
                pe.wait_ge(pts_ready, i * 16 + 8 * u + k + 2)
                pe.wait_ge(ptw_ready, i * 16 + 8 * u + k + 2)
                pe.matmul(ps[:, o, 0:HD], (ptC, ptC2)[g][:, j, :], vc_p[0:32, 64 * g:64 * g + 64], start=True, stop=True)
                for br, p, at in ((0, ptS, 384), (1, ptW, 640)):
                    for t in range(j + 1):
                        mm = pe.matmul(ps[:, o, HD * (br + 1):HD * (br + 2)], p[:, k % 2, 128 * t:128 * t + 128],
                                       kvtok[:, t, at + 64 * g:at + 64 * g + 64], start=(t == 0), stop=(t == j))
                mm.then_inc(pv_done, 1)

            for k in range(8):
                j = k % 4
                pe.wait_ge(exp_ready, i * 16 + 8 * u + k + 1)
                pe.wait_ge(pts_ready, i * 16 + 8 * u + k + 1)
                pe.wait_ge(ptw_ready, i * 16 + 8 * u + k + 1)
                for br in range(2):
                    for t in range(j + 1):
                        mm = pe.transpose(ps[:, 4 + br, 128 * t:128 * t + 128], sP[:, k % 2, br, 128 * t:128 * t + 128], ident)
                mm.then_inc(t_done, 1)
                if k < 6:
                    scores(k + 2)
                if k == 0:
                    flip_compressed()
                if k >= 1:
                    weigh(k - 1)
            weigh(7)

        sums_ready, sums_done = sem("sums_ready"), sem("sums_done")

        def pe_compress_pair(pe, i):
            pe.wait_ge(cmp_in, i * PAGES + PAGES)
            for kv in range(2):
                for p in range(NPG):
                    at = BAND + 1 - 8 * p
                    mm = pe.matmul(ps[:, 0, 256 * kv:256 * kv + 256], band[:, kv, at:at + 128],
                                   pages[:, :, p, 128 * kv:128 * kv + 128], start=(p == 0), stop=(p == NPG - 1))
            mm.then_inc(sums_done, 1)
            pe.wait_ge(sums_ready, i + 1)
            for kv in range(2):
                for b in range(2):
                    mm = pe.transpose(ps[:, 1, 256 * kv + 128 * b:256 * kv + 128 * b + 128], pre_k[:, kv, b], ident)
            mm.then_inc(pre_done, 1)

        def pe_pair(pe, i, last=False):
            row = lambda b: slice(64 * b, 64 * b + 64)
            pe.wait_ge(pair_free, i + 1)

            def flip_keys(c):
                if c == 0:
                    pe.wait_ge(selk_in, i * (PAGES // 2) + PAGES // 2)
                    pe.wait_ge(table_keys_in, i * (PAGES // 2) + PAGES // 2 + 16)
                if c == 4:
                    pe.wait_ge(win_in, i * 32 + 32)
                if c >= 2:
                    pe.wait_ge(ktc_ready, i * 5 + c - 1)
                for b in range(2):
                    for t in range(4):
                        src = pages[:, b, 4 * c + t, 256:384] if c < 4 else wst_[:, b, t, 0:128]
                        mm = pe.transpose(ps[:, (0, 6)[c % 2] + b, 128 * t:128 * t + 128], src, ident)
                mm.then_inc(tk_done, 1)

            pe.wait_ge(pre_ready, i + 2)
            pe.matmul(ps[:, 2, 0:256], cmp_bd[:, 0], preS[:, 0, :], start=True, stop=True)
            for b in range(2):
                mm = pe.matmul(ps[0:NCS, 3, 128 * b:128 * b + 128], preS[:, 1, 128 * b:128 * b + NCS], cmp_bd[:, 1],
                               start=True, stop=True)
            mm.then_inc(kc_done, 1)
            flip_keys(0)
            pe.wait_ge(qP_ready, i * 2 + 2)
            pe.wait_ge(kc_ready, i + 2)
            for b in range(2):
                mm = pe.matmul(ps[row(b), 4, 0:NCS], qP[:, b], kcS[:, b, 0:NCS], start=True, stop=True)
            mm.then_inc(scs_done, 1)
            pe.wait_ge(vc_ready, i + 2)
            for c in range(5):
                if c < 4:
                    flip_keys(c + 1)
                pe.wait_ge(ktc_ready, i * 5 + c + 1)
                if c >= 2:
                    pe.wait_ge(sk_ready, i * 5 + c - 1)
                for b in range(2):
                    mm = pe.matmul(ps[row(b), 2 + c % 2, :], qP[:, b], ktc[c % 2][:, b], start=True, stop=True)
                mm.then_inc(sk_done, 1)
            for b in range(2):
                pe.matmul(ps[row(b), 5, 0:TS], qP[:, b], ktS[:, SEQ:T], start=True, stop=True)
                pe.matmul(ps[row(b), 5, TS:2 * TS], qP[:, b], ktW[:, SEQ:T], start=True, stop=True)
            pe.matmul(ps[:, 5, 64:64 + 3 * NH], eP[0:TS, :], gts[0:TS, 4, :], start=True, stop=True).then_inc(new_done, 1)
            pe.wait_ge(pc_ready, i + 1)
            pe.matmul(ps[:, 4, 128:128 + NCS], const("same_query"), pcS[:, 0:NCS], start=True, stop=True).then_inc(imp_done, 1)
            if not last:
                pe_compress_pair(pe, i + 1)
                pe.wait_ge(pre_ready, i + 3)
            pe.wait_ge(exps_ready, i * 2 + 2)
            for t in range(16):
                pe.transpose(ps[:, t // 4, 128 * (t % 4):128 * (t % 4) + 128], sS[:, 128 * t:128 * t + 128], ident)
            for t in range(4):
                pe.transpose(ps[:, 4, 128 * t:128 * t + 128], sW[:, 128 * t:128 * t + 128], ident)
            flip(pe, ps[0:TS, 5, 128:256], sS[:, PAST:PAST + TS])
            flip(pe, ps[0:TS, 5, 256:384], sW[:, 512:512 + TS])
            flip(pe, ps[0:NCS, 5, 0:128], pcS[:, 0:NCS]).then_inc(tp_done, 1)
            pe.wait_ge(pTa_ready, i * 3 + 3)
            pe.wait_ge(pTv_ready, i * 4 + 4)
            pe.wait_ge(selv_in, i * PAGES + PAGES)
            for b in range(2):
                pe.matmul(ps[row(b), 6, 0:128], pT[0:NCS, 20, row(b)], vcS[0:NCS, b], start=True, stop=True)
                for t in range(17):
                    lhs, rhs = (pT[:, t, row(b)], pages[:, b, t, 384:512]) if t < 16 else \
                        (pT[0:TS, 21, row(b)], kvtok[0:TS, 4, 384:512])
                    pe.matmul(ps[row(b), 6, 128:256], lhs, rhs, start=(t == 0), stop=(t == 16))
                for t in range(5):
                    lhs, rhs = (pT[:, 16 + t, row(b)], wst_[:, b, t, 128:256]) if t < 4 else \
                        (pT[0:TS, 22, row(b)], kvtok[0:TS, 4, 640:768])
                    mm = pe.matmul(ps[row(b), 6, 256:384], lhs, rhs, start=(t == 0), stop=(t == 4))
            mm.then_inc(pvs_done, 1)
            pe.wait_ge(os_ready, i + 1)
            pe.transpose(ps[:, 7, 0:128], o_s[:, :], ident).then_inc(ot_done, 1)

        def act_odd(act):
            for u in range(2):
                act.wait_ge(step_done, STEP_ODD + u + 1)
                for t in range(KTILES):
                    r = tok_tile(t)
                    act.copy(kvtok[0:r, t, 384 * u:384 * u + 384], ps[0:r, (5 * u + t) % 8, 0:384]).then_inc(kv_ready, 1)
            act.wait_ge(step_done, STEP_ODD + 3)
            act.activation(gts[:, 0:4].rearrange("p t n -> p (t n)"), ps[:, 7, 0:4 * 3 * NH], ACT.Sigmoid)
            act.activation(gts[0:TS, 4], ps[0:TS, 7, 4 * 3 * NH:5 * 3 * NH], ACT.Sigmoid).then_inc(gt_ready, 1)
            for c in range(2):
                act.copy(halves(bgT[:, c]), banks(2 * c)).then_inc(bg_ready, 1)
            act.wait_ge(cg_done, 1)
            for c in range(2):
                act.copy(halves(cgT[:, c]), banks(4 + 2 * c)).then_inc(cg_ready, 1)
            act.wait_ge(ktf_done, 1)
            for kt, b in ((ktS, 4), (ktW, 6)):
                act.copy(kt[:, 0:SEQ], ps[:, b, :]).then_inc(kt_ready, 1)
                act.copy(kt[:, SEQ:T], ps[:, b + 1, 0:TS]).then_inc(kt_ready, 1)
            act.wait_ge(prefix_flip, 3)
            act.copy(cvs[:, :, :, 0:2], ps[:, 0, 0:4 * NB].rearrange("p (c b j) -> p c b j", c=2, b=NB)).then_inc(prefix_ready, 1)
            act.wait_ge(pre_done, 1)
            act.copy(pre_p, ps[:, 1, 0:64]).then_inc(pre_ready, 1)
            act.wait_ge(rows_done, 2)
            act.copy(c_rows[0:2, 0], ps[0:2, 4, 0:256]).then_inc(rows_ready, 1)
            act.copy(c_rows[0:2 * NB, 1], ps[0:2 * NB, 5, 0:256]).then_inc(rows_ready, 1)
            act.wait_ge(kc_done, 1)
            act.wait_ge(cm_in, 16 * 27)
            act.activation(kcT_p, ps[:, 2, 0:32], ACT.Identity, bias=k_bias).then_inc(kc_ready, 1)
            act.wait_ge(zeroed, 7)
            with act.Fori(0, 3) as i:
                for u in range(2):
                    act_queries(act, i, u)
            for j in range(4):
                act.wait_ge(of_done, j + 1)
                act.copy(oT[:, 0:4, 128 * j:128 * j + 128],
                         ps[:, 2 * (j % 2), :].rearrange("p (c t) -> p c t", c=4))
                act.copy(oT[:, 4:6, 128 * j:128 * j + 128],
                         ps[:, 2 * (j % 2) + 1, 0:256].rearrange("p (c t) -> p c t", c=2)).then_inc(of_ready, 1)
            act_pre(act, 0)
            with act.Fori(0, NB // 2 - 1) as i:
                act_pair(act, i)
            act_pair(act, NB // 2 - 1, last=True)

        def act_queries(act, i, u):
            s = HD ** -0.5
            act.wait_ge(step_done, STEP_Q + u + 1 + i * 2)
            act.mul(qTp[:, u, 0:HALF], ps[:, 4, 0:HALF], s).then_inc(qp_ready, 1)
            act.mul(qTp[:, u, HALF:SEQ], ps[:, 5, 0:SPLIT], s).then_inc(qp_ready, 1)
            for g in range(2):
                act.mul(qB[64 * g:64 * g + 64, :, ds(i * 8 + 32 * g + 4 * u, NT)],
                        ps[64 * g:64 * g + 64, 5, SPLIT:HALF].rearrange("p (b t) -> p b t", b=NB), s).then_inc(qp_ready, 1)
            def exps(k):
                n = 128 * (k % 4) + 128
                act.wait_ge(neg_ready, i * 16 + 8 * u + k + 1)
                for br in range(2):
                    e = sP[:, k % 2, br, 0:n]
                    ex = act.activation(e, e, ACT.Exp, bias=mx_p[:, k % 2, br:br + 1], accum_out=rs_p[:, k % 2, br:br + 1])
                ex.then_inc(exp_ready, 1)

            exps(0)
            for g in range(2):
                act.wait_ge(scmp_neg, i * 4 + 2 * u + g + 1)
                e = sc_p[:, g].rearrange("p j n -> p (j n)")
                act.activation(e, e, ACT.Exp).then_inc(scmp_exp, 1)
            for k in range(8):
                n = 128 * (k % 4) + 128
                act.wait_ge(t_done, i * 16 + 8 * u + k + 3)
                act.copy(ptS[:, k % 2, 0:n], ps[:, 4, 0:n]).then_inc(pts_ready, 1)
                if k < 7:
                    exps(k + 1)
                if k == 0:
                    for g in range(2):
                        act.wait_ge(tcmp_done, i * 4 + 2 * u + g + 1)
                        act.copy((ptC, ptC2)[g].rearrange("p j q -> p (j q)"), ps[0:32, 6 + g, :]).then_inc(ptc_ready, 1)

        def act_pre(act, i):
            act.wait_ge(sums_done, i + 1)
            act.copy(pre_k.rearrange("p a b n -> p (a b n)"), ps[:, 0, :]).then_inc(sums_ready, 1)
            act.wait_ge(pre_done, i + 2)
            act.copy(preS.rearrange("p a n -> p (a n)"), ps[:, 1, :]).then_inc(pre_ready, 1)

        def act_pair(act, i, last=False):
            act.wait_ge(kc_done, i + 2)
            act.activation(kcS.rearrange("p b n -> p (b n)"), ps[:, 2, 0:256], ACT.Identity, bias=k_bias).then_inc(kc_ready, 1)
            for c in range(5):
                act.wait_ge(tk_done, i * 5 + c + 1)
                if c >= 2:
                    act.wait_ge(sk_done, i * 5 + c - 1)
                b = (0, 6)[c % 2]
                act.copy(ktc[c % 2], ps[:, b:b + 2, :]).then_inc(ktc_ready, 1)
                if c == 1:
                    act.wait_ge(negc_ready, i + 1)
                    act.activation(pcS[:, 0:NCS], pcS[:, 0:NCS], ACT.Exp, bias=mx[:, 0:1],
                                   accum_out=rs[:, 0:1]).then_inc(expc_ready, 1)
            for k, (s, m) in enumerate(((sW, 2), (sS, 1))):
                act.wait_ge(negs_ready, i * 2 + k + 1)
                act.activation(s, s, ACT.Exp, bias=mx[:, m:m + 1], accum_out=rs[:, m:m + 1]).then_inc(exps_ready, 1)
                if k == 0 and not last:
                    act_pre(act, i + 1)
            act.wait_ge(tp_done, i + 1)
            for b in range(3):
                act.copy(pT[:, 4 * b:4 * b + 4].rearrange("p t q -> p (t q)"), ps[:, b, :]).then_inc(pTa_ready, 1)

        def dve_odd(dve, C):
            dve.wait_ge(step_done, STEP_ODD + 4)
            dve.wait_ge(cg_ready, 2)
            for c in range(2):
                for s, lo, hi, at in SEGS:
                    dve.tensor_tensor(cvp[:, c, 2 + at:2 + at + hi - lo], cgT[:, c, at:at + hi - lo],
                                      ps[:, 2 * c + s, lo:hi], ALU.mult)
                C.after(dve.tensor_tensor(cvs[:, c, :, 2:2 + NT], cgT[:, c, SEQ:T].rearrange("p (b t) -> p b t", b=NB),
                                          ps[:, 2 * c + 1, SPLIT:HALF].rearrange("p (b t) -> p b t", b=NB), ALU.mult))
                dve.tensor_copy(cv_last[:, c].rearrange("p (b j) -> p b j", b=NB), cvs[:, c, :, NT:2 + NT]).then_inc(cu_ready, 1)
            dve.wait_ge(kc_done, 1)
            dve.wait_ge(cm_in, 16 * 27)
            dve.tensor_tensor(vc_p[0:32], ps[0:32, 3, 0:128], v_bias[0:32], ALU.add).then_inc(vc_ready, 1)
            for s, n in ((sc_free, 2), (t_done, 2), (pts_ready, 1), (ptw_ready, 1), (o_used, 1)):
                dve.sem_inc(s, n)
            per = 120
            with dve.Fori(0, 3) as i:
                C.loop(i, per, lambda: [dve_queries(dve, C, i, u) for u in range(2)])
            C.skip(2 * per)
            dve.wait_ge(of_ready, 4)
            C.after(dve.memset(band, 0.0))
            C.after(dve.tensor_copy(band[:, :, BAND:BAND + 9], cmp_a))
            dve.sem_inc(pair_free, 1)
            per = 28
            with dve.Fori(0, NB // 2) as i:
                C.loop(i, per, lambda: dve_pair(dve, C, i))
            C.skip(per * (NB // 2 - 1))
            dve.sem_inc(down_free, 2)
            dve_add(dve, 4, STEP_OOUT, 1, 1.0)

        def dve_queries(dve, C, i, u):
            ns_ = const("neg_slope")
            slope = lambda g: ns_[:, ds(i * 2 + u + GQ * g, 1)]
            gate = lambda g, j, a, n: gts[:, j, ds(i * 6 + 3 * u + 3 * GQ * g + a, n)]
            at = lambda k: i * 16 + 8 * u + k
            flat = lambda g: sc_p[:, g].rearrange("p j n -> p (j n)")
            wide = lambda g: mc[:, g].unsqueeze(2).broadcast_to([128, 4, 32])
            def scores(k):
                g, j = k // 4, k % 4
                n = 128 * j + 128
                dve.wait_ge(sc_done, at(k + 1))
                dve.wait_ge(t_done, at(k + 1))
                for br in range(2):
                    st = dve.scalar_tensor_tensor(out=sP[:, k % 2, br, 0:n], in0=const("dist")[:, 512 - n:512],
                                                  scalar=slope(g), in1=ps[:, 2 * (k % 2) + br, 0:n],
                                                  op0=ALU.mult, op1=ALU.add)
                st.then_inc(sc_free, 1)
                dve.wait_ge(sc_free, at(k + 3))
                C.after(dve.tensor_reduce(mx_p[:, k % 2], sP[:, k % 2, :, 0:n], AX.X, ALU.max))
                dve.tensor_scalar(mx_p[:, k % 2], mx_p[:, k % 2], -1.0, None, ALU.mult).then_inc(neg_ready, 1)

            def combine(k):
                g, j = k // 4, k % 4
                o = ps[:, 6 + k % 2, :]
                dve.wait_ge(pv_done, at(k + 1))
                dve.wait_ge(o_used, at(k + 1))
                C.after(dve.tensor_scalar(o1, o[:, 0:HD], gate(g, j, 0, 1), None, ALU.mult))
                C.after(dve.scalar_tensor_tensor(out=o1, in0=o[:, HD:2 * HD], scalar=coef[:, k % 2, 0:1], in1=o1,
                                                 op0=ALU.mult, op1=ALU.add))
                dve.scalar_tensor_tensor(out=otok[j // 2][:, j % 2, ds(i * 256 + 128 * u + 64 * g, HD)],
                                         in0=o[:, 2 * HD:3 * HD], scalar=coef[:, k % 2, 1:2], in1=o1,
                                         op0=ALU.mult, op1=ALU.add).then_inc(o_used, 1)

            scores(0)
            for g in range(2):
                dve.wait_ge(scmp_done, i * 4 + 2 * u + g + 1)
                C.after(dve.scalar_tensor_tensor(out=flat(g), in0=const("dist_cmp"), scalar=slope(g),
                                                 in1=ps[:, 6 + g, 0:128], op0=ALU.mult, op1=ALU.add))
                C.after(dve.tensor_reduce(mc[:, g], sc_p[:, g], AX.X, ALU.max))
                C.after(dve.tensor_scalar(mc[:, g], mc[:, g], -1e20, None, ALU.max))
                dve.tensor_tensor(sc_p[:, g], sc_p[:, g], wide(g), ALU.subtract).then_inc(scmp_neg, 1)
            scores(1)
            for g in range(2):
                dve.wait_ge(scmp_exp, i * 4 + 2 * u + g + 1)
                C.after(dve.tensor_reduce(mc[:, g], sc_p[:, g], AX.X, ALU.add))
                C.after(dve.tensor_scalar(mc[:, g], mc[:, g], 1e-30, None, ALU.max))
                C.after(dve.reciprocal(mc[:, g], mc[:, g]))
                dve.tensor_tensor(sc_p[:, g], sc_p[:, g], wide(g), ALU.mult).then_inc(scmp_ready, 1)
            for k in range(8):
                n = 128 * (k % 4) + 128
                if 1 <= k < 7:
                    scores(k + 1)
                dve.wait_ge(t_done, at(k + 3))
                dve.tensor_copy(ptW[:, k % 2, 0:n], ps[:, 5, 0:n]).then_inc(ptw_ready, 1)
                dve.wait_ge(exp_ready, at(k + 1))
                dve.wait_ge(o_used, at(max(k, 1)))
                cf = coef[:, k % 2]
                C.after(dve.tensor_scalar(cf, rs_p[:, k % 2], 1e-30, None, ALU.max))
                C.after(dve.reciprocal(cf, cf))
                C.after(dve.tensor_tensor(cf, cf, gate(k // 4, k % 4, 1, 2), ALU.mult))
                if k >= 1:
                    combine(k - 1)
            combine(7)

        def dve_pair(dve, C, i):
            nsr = const("neg_slope_row")
            dve.tensor_scalar(qP, qB[:, ds(i * 2, 2)], 1.0, None, ALU.mult).then_inc(qP_ready, 1)
            dve.tensor_scalar(eP[0:TS], const("row_token", TS)[:, ds(i * 128, 128)], 1.0, None, ALU.mult).then_inc(qP_ready, 1)
            dve.wait_ge(kc_done, i + 2)
            dve.tensor_tensor(vcS[0:NCS], ps[0:NCS, 3, 0:256].rearrange("p (b n) -> p b n", b=2),
                              v_bias[0:NCS].unsqueeze(1).broadcast_to([NCS, 2, 128]), ALU.add).then_inc(vc_ready, 1)
            pc = pcS[:, 0:NCS]
            dve.wait_ge(scs_done, i + 1)
            C.after(dve.scalar_tensor_tensor(out=pc, in0=const("dist_cmp_s")[:, 0:NCS], scalar=nsr, in1=ps[:, 4, 0:NCS],
                                             op0=ALU.mult, op1=ALU.add))
            C.after(dve.tensor_reduce(mx[:, 0:1], pc, AX.X, ALU.max))
            dve.tensor_scalar(mx[:, 0:1], mx[:, 0:1], -1e20, -1.0, ALU.max, ALU.mult).then_inc(negc_ready, 1)

            def evacuate(c):
                dve.wait_ge(sk_done, i * 5 + c + 1)
                b = ps[:, 2 + c % 2, :]
                if c < 4:
                    e = dve.scalar_tensor_tensor(
                        out=sS[:, 512 * c:512 * c + 512].rearrange("p (b k) -> p b k", b=8),
                        in0=const("dist_blk").unsqueeze(1).broadcast_to([128, 8, 64]), scalar=nsr,
                        in1=b.rearrange("p (b k) -> p b k", b=8), op0=ALU.mult, op1=ALU.add)
                else:
                    e = dve.scalar_tensor_tensor(out=sW[:, 0:512], in0=const("dist_win"), scalar=nsr, in1=b,
                                                 op0=ALU.mult, op1=ALU.add)
                e.then_inc(sk_ready, 1)

            evacuate(0)
            evacuate(1)
            dve.wait_ge(expc_ready, i + 1)
            C.after(dve.tensor_scalar(rs[:, 0:1], rs[:, 0:1], 1e-30, None, ALU.max))
            C.after(dve.reciprocal(rs[:, 0:1], rs[:, 0:1]))
            dve.tensor_scalar(pc, pc, rs[:, 0:1], None, ALU.mult).then_inc(pc_ready, 1)
            for c in (2, 3, 4):
                evacuate(c)
            dve.wait_ge(new_done, i + 1)
            dn = const("dist_new")[:, ds(i * TS, TS)]
            dve.sem_inc(waited, 1)
            for s, at, b in ((sS, PAST, 0), (sW, 512, TS)):
                C.after(dve.scalar_tensor_tensor(out=s[:, at:at + TS], in0=dn, scalar=nsr, in1=ps[:, 5, b:b + TS],
                                                 op0=ALU.mult, op1=ALU.add))
            C.after(dve.tensor_tensor(g36, ps[:, 5, 64:64 + 3 * NH].rearrange("p (h c) -> p h c", c=3),
                                      const("row_head").unsqueeze(2).broadcast_to([128, NH, 3]), ALU.mult))
            C.after(dve.tensor_reduce(gs, g36.rearrange("p h c -> p c h"), AX.X, ALU.add))
            dve.wait_ge(sk_ready, i * 5 + 5)
            C.after(dve.tensor_reduce(mx[:, 2:3], sW, AX.X, ALU.max))
            dve.tensor_scalar(mx[:, 2:3], mx[:, 2:3], -1.0, None, ALU.mult).then_inc(negs_ready, 1)
            dve.wait_ge(imp_done, i + 1)
            C.after(dve.tensor_copy(imp[:, 1:1 + NCS], ps[:, 4, 128:128 + NCS]))
            four = imp.rearrange("p (b r) -> p b r", r=4)
            C.after(dve.tensor_reduce(score[:, 0:NBLK - 1], four[:, 0:NBLK - 1], AX.X, ALU.add))
            C.after(dve.tensor_tensor(score[:, 0:NBLK - 1], score[:, 0:NBLK - 1], four[:, 1:NBLK, 0], ALU.add))
            C.after(dve.memset(score[:, 0:1], 1e30))
            C.after(dve.memset(score[:, NBLK - 2:NBLK], 1e30))
            for src, dst in ((score, score2), (score2, score)):
                dve.sem_inc(waited, 1)
                C.after(dve.max(top8, src))
                dve.sem_inc(waited, 1)
                C.after(dve.match_replace(dst, top8, src, -3e38))
            C.after(dve.tensor_scalar(score2, score, -1e38, -1e30, ALU.is_gt, ALU.mult))
            C.after(dve.tensor_tensor(blk_add, score2, const("blk_base"), ALU.add))
            sb_ = sS[:, 0:PAST].rearrange("p (b k) -> p b k", k=64)
            C.after(dve.tensor_tensor(sb_, sb_, blk_add[:, 0:NBLK - 1].unsqueeze(2).broadcast_to([128, NBLK - 1, 64]), ALU.add))
            C.after(dve.tensor_reduce(mx[:, 1:2], sS, AX.X, ALU.max))
            dve.tensor_scalar(mx[:, 1:2], mx[:, 1:2], -1.0, None, ALU.mult).then_inc(negs_ready, 1)
            dve.wait_ge(exps_ready, i * 2 + 2)
            C.after(dve.tensor_scalar(rs[:, 1:3], rs[:, 1:3], 1e-30, None, ALU.max))
            C.after(dve.reciprocal(rs[:, 1:3], rs[:, 1:3]))
            C.after(dve.tensor_tensor(gs[:, 1:3], gs[:, 1:3], rs[:, 1:3], ALU.mult))
            dve.wait_ge(tp_done, i + 1)
            dve.tensor_copy(pT[:, 12:16].rearrange("p t q -> p (t q)"), ps[:, 3, :]).then_inc(pTv_ready, 1)
            dve.tensor_copy(pT[:, 16:20].rearrange("p t q -> p (t q)"), ps[:, 4, :]).then_inc(pTv_ready, 1)
            dve.tensor_copy(pT[0:NCS, 20], ps[0:NCS, 5, 0:128]).then_inc(pTv_ready, 1)
            dve.tensor_copy(pT[0:TS, 21:23].rearrange("p t q -> p (t q)"), ps[0:TS, 5, 128:384]).then_inc(pTv_ready, 1)
            dve.wait_ge(pvs_done, i + 1)
            C.after(dve.tensor_scalar(o_s, ps[:, 6, 0:128], gs[:, 0:1], None, ALU.mult))
            C.after(dve.scalar_tensor_tensor(out=o_s, in0=ps[:, 6, 128:256], scalar=gs[:, 1:2], in1=o_s,
                                             op0=ALU.mult, op1=ALU.add))
            dve.scalar_tensor_tensor(out=o_s, in0=ps[:, 6, 256:384], scalar=gs[:, 2:3], in1=o_s,
                                     op0=ALU.mult, op1=ALU.add).then_inc(os_ready, 1)
            dve.wait_ge(ot_done, i + 1)
            for b in range(2):
                for g in range(2):
                    src = ps[64 * g:64 * g + 64, 7, 64 * b + 32 * g:64 * b + 32 * g + 4 * GQ]
                    o = dve.tensor_scalar(oT[64 * g:64 * g + 64, :, ds(i * (2 * NT) + SEQ + NT * b, NT)],
                                          src.rearrange("p (i t) -> p i t", t=NT), 1.0, None, ALU.mult)
            C.after(o)
            dve.sem_inc(pair_free, 1)

        block = ctx.enter_context(nc.Block())

        @block.sync
        def _(sp):
            sp_load(sp)
            load_ffn(sp, 0, 0)
            load_even(sp)
            load_ffn(sp, 1, STEP_FFN1)
            load_ffn(sp, 2, STEP_FFN2)
            load_odd(sp)
            load_ffn(sp, 3, STEP_FFN3)

        @block.gpsimd
        def _(po):
            C = Chain(po, gchain)
            pool_even(po, C)
            po.wait_ge(stored, 16 * n_stored[0])
            po.sem_inc(scratch_stored, 1)
            pool_odd(po, C)
            po.wait_ge(stored, 16 * n_stored[0])
            po.sem_inc(scratch_stored, 1)

        @block.tensor
        def _(pe):
            pe_load(pe)
            pe_norm(pe, 0)
            pe_ffn(pe, 0, 0)
            pe_norm(pe, 1)
            pe_even(pe)
            pe_norm(pe, 2)
            pe_ffn(pe, 1, STEP_FFN1)
            pe_norm(pe, 3)
            pe_ffn(pe, 2, STEP_FFN2)
            pe_norm(pe, 4)
            pe_odd(pe)
            pe_norm(pe, 5)
            pe_ffn(pe, 3, STEP_FFN3)
            pe_norm(pe, 6)
            pe_final(pe)

        @block.scalar
        def _(act):
            act_load(act)
            act_norm(act, 0)
            act_ffn(act, 0, 0)
            act_norm(act, 1)
            act_even(act)
            act_norm(act, 2)
            act_ffn(act, 1, STEP_FFN1)
            act_norm(act, 3)
            act_ffn(act, 2, STEP_FFN2)
            act_norm(act, 4)
            act_odd(act)
            act_norm(act, 5)
            act_ffn(act, 3, STEP_FFN3)
            act_norm(act, 6)
            act_final(act)

        @block.vector
        def _(dve):
            C = Chain(dve, vchain)
            dve_load(dve)
            dve_norm(dve, 0)
            dve_ffn(dve, 0, 0)
            dve_norm(dve, 1)
            dve_even(dve, C)
            dve_norm(dve, 2)
            dve_ffn(dve, 1, STEP_FFN1)
            dve_norm(dve, 3)
            dve_ffn(dve, 2, STEP_FFN2)
            dve_norm(dve, 4)
            dve_odd(dve, C)
            dve_norm(dve, 5)
            dve_ffn(dve, 3, STEP_FFN3)
            dve_norm(dve, 6)


_INS = ['x_prompt', 'x_sample', 'state_pool', 'state_mlstm_c', 'state_mlstm_n', 'state_mlstm_m',
        'cache_nsa_kv', 'state_win_kv', 'state_conv', 'page_table', 'norm_g', 'final_g', 'w_ffn_in',
        'w_ffn_out', 'w_in_even', 'b_gate_even', 'w_pool', 'pool_scale', 'w_out_even', 'w_in_odd',
        'cmp_pos_w', 'cmp_w', 'cmp_b', 'conv_w', 'w_out_odd']
_OUTS = [(1, SEQ, D), (NB, NT, D), (1, 1, 15, 256), (1, NB, 15, 256), (1, 1, H4, DH, DH), (1, NB, H4, DH, DH),
         (1, 1, H4, DH), (1, NB, H4, DH), (1, 1, H4), (1, NB, H4), (1, 1, SEQ, 4, 2, HD), (1, NB, NT, 4, 2, HD),
         (1, 1, SEQ, 2, 2, HD), (1, NB, 512, 2, 2, HD), (1, 1, 2, 256), (1, NB, 2, 256)]


def kernel(**inputs):
    import numpy as _np
    import concourse.bacc as _bacc
    from concourse import mybir as _mybir
    from concourse.bass_utils import run_bass_kernel_spmd as _run

    nc = _bacc.Bacc("TRN2", target_bir_lowering=False, num_devices=1)
    arrays, args = {}, []
    for name in _INS + ["consts"]:
        a = CONSTS if name == "consts" else _np.ascontiguousarray(inputs[name])
        arrays[f"in_{name}_dram"] = a
        args.append(nc.dram_tensor(f"in_{name}_dram", a.shape, _mybir.dt.from_np(a.dtype), kind="ExternalInput").ap())
    for i, shape in enumerate(_OUTS):
        args.append(nc.dram_tensor(f"out_{i}_dram", shape, _mybir.dt.float32, kind="ExternalOutput").ap())
    trunk(nc, *args)
    r = _run(nc, [arrays], core_ids=[0])
    return tuple(r.results[0][f"out_{i}_dram"] for i in range(len(_OUTS)))
```
